# Optimizing a Trainium2 kernel written in Bass

```python
import jax
import jax.numpy as jnp
from jax import lax
import numpy as np
import math
import jax, jax.numpy as jnp

D_MODEL = 1024
BATCH = 1
SEQ = 512
DEPTH = 1

MLA_HEADS = 8
MLA_Q_RANK = 256
MLA_KV_RANK = 128
MLA_NOPE = 64
MLA_ROPE = 32
MLA_V = 64
ROPE_THETA = 10000.0
DSA_HEADS = 8
DSA_KV_HEADS = 2
DSA_HEAD_DIM = 64
IDX_HEADS = 8
IDX_DIM = 32
IDX_TOPK_MAX = 256
N_EXPERTS = 32
TOP_K = 4
D_EXPERT = D_MODEL
SWIGLU_ALPHA = 1.702
SWIGLU_LIMIT = 7.0

NORM_EPS = 1e-6
NEG_INF = -1e30
Q_BLOCK = 128
MOE_BLOCK = 128

MIX_WIDTH = MLA_HEADS * MLA_V + DSA_HEADS * DSA_HEAD_DIM
IN_SPLITS = (MLA_Q_RANK, MLA_KV_RANK, MLA_ROPE,
             DSA_HEADS * DSA_HEAD_DIM, DSA_KV_HEADS * DSA_HEAD_DIM, DSA_KV_HEADS * DSA_HEAD_DIM,
             IDX_HEADS * IDX_DIM, IDX_DIM, IDX_HEADS)
IN_WIDTH = sum(IN_SPLITS)


def rms_norm(x, g):
    xf = x.astype(jnp.float32)
    y = xf * lax.rsqrt(jnp.mean(xf * xf, axis=-1, keepdims=True) + NORM_EPS)
    return (y * g.astype(jnp.float32)).astype(x.dtype)

def rope(x, pos):
    half = x.shape[-1] // 2
    freqs = ROPE_THETA ** (-jnp.arange(half, dtype=jnp.float32) / half)
    ang = pos.astype(jnp.float32)[..., None] * freqs
    ang = ang.reshape(ang.shape[:2] + (1,) * (x.ndim - 3) + (half,))
    cos, sin = jnp.cos(ang), jnp.sin(ang)
    x1 = x[..., :half].astype(jnp.float32)
    x2 = x[..., half:].astype(jnp.float32)
    return jnp.concatenate([x1 * cos - x2 * sin, x2 * cos + x1 * sin], axis=-1).astype(x.dtype)

def to_blocks(a):
    b, s = a.shape[:2]
    return jnp.moveaxis(a.reshape((b, s // Q_BLOCK, Q_BLOCK) + a.shape[2:]), 1, 0)

def from_blocks(a):
    a = jnp.moveaxis(a, 0, 1)
    return a.reshape((a.shape[0], a.shape[1] * a.shape[2]) + a.shape[3:])

def mla_attention(c_q, c_kv, k_rope_in, pos, g_q_a, g_kv_a, w_q_b, w_kv_b):
    b, s, _ = c_q.shape
    q = (rms_norm(c_q, g_q_a) @ w_q_b).reshape(b, s, MLA_HEADS, MLA_NOPE + MLA_ROPE)
    q_nope = q[..., :MLA_NOPE]
    q_rope = rope(q[..., MLA_NOPE:], pos)
    kv = (rms_norm(c_kv, g_kv_a) @ w_kv_b).reshape(b, s, MLA_HEADS, MLA_NOPE + MLA_V)
    k_nope, v = kv[..., :MLA_NOPE], kv[..., MLA_NOPE:]
    k_rope = rope(k_rope_in, pos)
    scale = (MLA_NOPE + MLA_ROPE) ** -0.5
    key_idx = jnp.arange(s)

    def block(args):
        qn, qr, qi = args
        sc = (jnp.einsum('bqhd,bkhd->bhqk', qn, k_nope)
              + jnp.einsum('bqhd,bkd->bhqk', qr, k_rope)).astype(jnp.float32) * scale
        sc = jnp.where(key_idx[None, None, None, :] <= qi[None, None, :, None], sc, NEG_INF)
        p = jax.nn.softmax(sc, axis=-1).astype(v.dtype)
        return jnp.einsum('bhqk,bkhd->bqhd', p, v)

    q_ids = jnp.arange(s).reshape(-1, Q_BLOCK)
    out = lax.map(block, (to_blocks(q_nope), to_blocks(q_rope), q_ids))
    return from_blocks(out).reshape(b, s, MLA_HEADS * MLA_V)

def dsa_attention(q, k, v, q_i, k_i, w_i, pos):
    b, s, _ = q.shape
    grp = DSA_HEADS // DSA_KV_HEADS
    q = q.reshape(b, s, DSA_KV_HEADS, grp, DSA_HEAD_DIM)
    k = k.reshape(b, s, DSA_KV_HEADS, DSA_HEAD_DIM)
    v = v.reshape(b, s, DSA_KV_HEADS, DSA_HEAD_DIM)
    q_i = q_i.reshape(b, s, IDX_HEADS, IDX_DIM) * (IDX_DIM ** -0.5)
    w_i = w_i * (IDX_HEADS ** -0.5)
    n_sel = min(IDX_TOPK_MAX, s // 4)
    key_idx = jnp.arange(s)
    slopes = jnp.exp2(-8.0 * jnp.arange(1, DSA_HEADS + 1, dtype=jnp.float32) / DSA_HEADS)
    slopes = slopes.reshape(DSA_KV_HEADS, grp)
    gather = jax.vmap(lambda a, i: a[i])

    def block(args):
        qb, qib, wib, posb, ti = args
        rel = jax.nn.relu(jnp.einsum('bqhd,bsd->bqsh', qib, k_i).astype(jnp.float32))
        idx_score = jnp.einsum('bqsh,bqh->bqs', rel, wib.astype(jnp.float32))
        idx_score = jnp.where(key_idx[None, None, :] <= ti[None, :, None], idx_score, NEG_INF)
        _, sel = lax.top_k(idx_score, n_sel)
        k_sel = gather(k, sel)
        v_sel = gather(v, sel)
        pos_sel = gather(pos, sel)
        sc = jnp.einsum('bqhgd,bqnhd->bqhgn', qb, k_sel).astype(jnp.float32) * (DSA_HEAD_DIM ** -0.5)
        dist = jnp.abs(posb[:, :, None] - pos_sel).astype(jnp.float32)
        sc = sc - slopes[None, None, :, :, None] * dist[:, :, None, None, :]
        valid = sel <= ti[None, :, None]
        sc = jnp.where(valid[:, :, None, None, :], sc, NEG_INF)
        p = jax.nn.softmax(sc, axis=-1).astype(v.dtype)
        return jnp.einsum('bqhgn,bqnhd->bqhgd', p, v_sel)

    q_ids = jnp.arange(s).reshape(-1, Q_BLOCK)
    out = lax.map(block, (to_blocks(q), to_blocks(q_i), to_blocks(w_i), to_blocks(pos), q_ids))
    return from_blocks(out).reshape(b, s, DSA_HEADS * DSA_HEAD_DIM)

def moe_ffn(h, w_router, b_router, w_mlp1, b_mlp1, w_mlp2, b_mlp2):
    b, s, d = h.shape
    xf = h.reshape(-1, d)
    n = xf.shape[0]
    logits = (xf @ w_router + b_router).astype(jnp.float32)
    top_val, top_idx = lax.top_k(logits, TOP_K)
    gates = jax.nn.softmax(top_val, axis=-1)
    n_assign = n * TOP_K
    flat_e = top_idx.reshape(-1)
    flat_tok = jnp.arange(n_assign, dtype=jnp.int32) // TOP_K
    flat_gate = gates.reshape(-1)
    order = jnp.argsort(flat_e)
    e_sorted = flat_e[order]
    counts = jnp.bincount(flat_e, length=N_EXPERTS)
    start = jnp.cumsum(counts) - counts
    padded = (counts + MOE_BLOCK - 1) // MOE_BLOCK * MOE_BLOCK
    pad_end = jnp.cumsum(padded)
    pad_start = pad_end - padded
    dest = pad_start[e_sorted] + jnp.arange(n_assign) - start[e_sorted]
    n_slots = (n_assign + MOE_BLOCK - 1) // MOE_BLOCK * MOE_BLOCK + N_EXPERTS * MOE_BLOCK
    n_blocks = n_slots // MOE_BLOCK
    slot_tok = jnp.full((n_slots,), n, jnp.int32).at[dest].set(flat_tok[order])
    slot_gate = jnp.zeros((n_slots,), jnp.float32).at[dest].set(flat_gate[order])
    block_e = jnp.minimum(
        jnp.searchsorted(pad_end, jnp.arange(n_blocks) * MOE_BLOCK, side='right'), N_EXPERTS - 1)
    x_pad = jnp.concatenate([xf, jnp.zeros((1, d), xf.dtype)], axis=0)
    x_slots = x_pad[slot_tok].reshape(n_blocks, MOE_BLOCK, d)

    def expert_block(args):
        xb, e = args
        hid = xb @ w_mlp1[e] + b_mlp1[e]
        glu = jnp.minimum(hid[..., ::2], SWIGLU_LIMIT)
        lin = jnp.clip(hid[..., 1::2], -SWIGLU_LIMIT, SWIGLU_LIMIT)
        act = glu * jax.nn.sigmoid(SWIGLU_ALPHA * glu) * (lin + 1.0)
        return act @ w_mlp2[e] + b_mlp2[e]

    y = lax.map(expert_block, (x_slots, block_e)).reshape(n_slots, d)
    y = y * slot_gate[:, None].astype(y.dtype)
    out = jax.ops.segment_sum(y, slot_tok, num_segments=n + 1)[:n]
    return out.reshape(b, s, d)

def first_inputs(seed: int = 0) -> dict:
    key = jax.random.key(seed)
    ks = jax.random.split(key, 24)
    f32 = jnp.float32
    L, D, F, E = DEPTH, D_MODEL, D_EXPERT, N_EXPERTS

    def nrm(k, shape, scale):
        return jax.random.normal(k, shape, f32) * scale

    def gain(k, width):
        return 1.0 + nrm(k, (L, width), 0.02)

    x = nrm(ks[0], (BATCH, SEQ, D), 1.0)
    c = nrm(ks[1], (BATCH, D), 1.0)
    offsets = jax.random.randint(ks[2], (BATCH, 1), 0, 4096, dtype=jnp.int32)
    positions = offsets + jnp.arange(SEQ, dtype=jnp.int32)[None, :]
    return {
        "x": x,
        "c": c,
        "positions": positions,
        "w_ada": nrm(ks[3], (L, D, 6 * D), 0.2 * D ** -0.5),
        "b_ada": nrm(ks[4], (L, 6 * D), 0.01),
        "g_pre_mix": gain(ks[5], D),
        "g_post_mix": gain(ks[6], D),
        "g_pre_ffn": gain(ks[7], D),
        "g_post_ffn": gain(ks[8], D),
        "w_in": nrm(ks[9], (L, D, IN_WIDTH), D ** -0.5),
        "g_q_a": gain(ks[10], MLA_Q_RANK),
        "g_kv_a": gain(ks[11], MLA_KV_RANK),
        "w_q_b": nrm(ks[12], (L, MLA_Q_RANK, MLA_HEADS * (MLA_NOPE + MLA_ROPE)), MLA_Q_RANK ** -0.5),
        "w_kv_b": nrm(ks[13], (L, MLA_KV_RANK, MLA_HEADS * (MLA_NOPE + MLA_V)), MLA_KV_RANK ** -0.5),
        "w_o": nrm(ks[14], (L, MIX_WIDTH, D), MIX_WIDTH ** -0.5),
        "w_router": nrm(ks[15], (L, D, E), D ** -0.5),
        "b_router": nrm(ks[16], (L, E), 0.01),
        "w_mlp1": nrm(ks[17], (L, E, D, 2 * F), D ** -0.5),
        "b_mlp1": nrm(ks[18], (L, E, 2 * F), 0.01),
        "w_mlp2": nrm(ks[19], (L, E, F, D), F ** -0.5),
        "b_mlp2": nrm(ks[20], (L, E, D), 0.01),
    }

def first_block(x, c, positions, w_ada, b_ada, g_pre_mix, g_post_mix, g_pre_ffn, g_post_ffn,
              w_in, g_q_a, g_kv_a, w_q_b, w_kv_b, w_o, w_router, b_router,
              w_mlp1, b_mlp1, w_mlp2, b_mlp2):
    split_at = np.cumsum(IN_SPLITS)[:-1].tolist()
    cond = jax.nn.silu(c)
    for l in range(DEPTH):
        mod = cond @ w_ada[l] + b_ada[l]
        sh1, sc1, gt1, sh2, sc2, gt2 = [m[:, None, :] for m in jnp.split(mod, 6, axis=-1)]

        h = rms_norm(x, g_pre_mix[l]) * (1.0 + sc1) + sh1
        proj = h @ w_in[l]
        (c_q, c_kv, k_rope, q_d, k_d, v_d, q_idx, k_idx, w_idx) = jnp.split(proj, split_at, axis=-1)
        y_mla = mla_attention(c_q, c_kv, k_rope, positions, g_q_a[l], g_kv_a[l], w_q_b[l], w_kv_b[l])
        y_dsa = dsa_attention(q_d, k_d, v_d, q_idx, k_idx, w_idx, positions)
        mix = jnp.concatenate([y_mla, y_dsa], axis=-1) @ w_o[l]
        x = x + gt1 * rms_norm(mix, g_post_mix[l])

        h2 = rms_norm(x, g_pre_ffn[l]) * (1.0 + sc2) + sh2
        ffn = moe_ffn(h2, w_router[l], b_router[l], w_mlp1[l], b_mlp1[l], w_mlp2[l], b_mlp2[l])
        x = x + gt2 * rms_norm(ffn, g_post_ffn[l])
    return x


DEPTH_2 = 2

HEAD_DIM = 64
HGRN_WIDTH = D_MODEL // 4
HGRN_HEADS = HGRN_WIDTH // HEAD_DIM
HGRN_CHUNK = 64
FOURIER_WIDTH = D_MODEL // 4
FOURIER_GROUPS = FOURIER_WIDTH // HEAD_DIM
ATTN_WIDTH = D_MODEL // 2
ATTN_HEADS = ATTN_WIDTH // HEAD_DIM
MIX_WIDTH_2 = HGRN_WIDTH + FOURIER_WIDTH + ATTN_WIDTH
DILATED_PATTERNS = ((128, 1), (512, 4), (2048, 16))
D_FF = 4 * D_MODEL
RMS_EPS = 1e-6
NEG_BIG = -1e30
IN_SPLITS_2 = (HGRN_WIDTH, HGRN_WIDTH, HGRN_WIDTH, HGRN_WIDTH, HGRN_WIDTH, FOURIER_WIDTH, ATTN_WIDTH, ATTN_WIDTH, ATTN_WIDTH)
IN_WIDTH_2 = sum(IN_SPLITS_2)
SPLIT_POINTS = [sum(IN_SPLITS_2[:i + 1]) for i in range(len(IN_SPLITS_2) - 1)]


def rms_norm_2(x, w):
    xf = x.astype(jnp.float32)
    y = xf * lax.rsqrt(jnp.mean(xf * xf, axis=-1, keepdims=True) + RMS_EPS)
    return (y * w.astype(jnp.float32)).astype(x.dtype)

def hgrn2_chunk_scan(q, k, v, log_f):
    B, H, S, dk = q.shape
    dv = v.shape[-1]
    C = HGRN_CHUNK
    n = S // C

    def chunked(t):
        return jnp.moveaxis(t.reshape(B, H, n, C, t.shape[-1]), 2, 0)

    tri = jnp.tril(jnp.ones((C, C), dtype=bool))[:, :, None]

    def step(state, inp):
        qc, kc, vc, gc = inp
        b = jnp.cumsum(gc, axis=-2)
        inter = jnp.einsum('bhtk,bhkv->bhtv', qc * jnp.exp(b), state)
        diff = b[..., :, None, :] - b[..., None, :, :]
        pair = jnp.where(tri, jnp.exp(jnp.where(tri, diff, 0.0)), 0.0)
        scores = jnp.einsum('bhtk,bhsk,bhtsk->bhts', qc, kc, pair)
        intra = jnp.einsum('bhts,bhsv->bhtv', scores, vc)
        b_last = b[..., -1:, :]
        new_state = (jnp.exp(b_last[..., 0, :])[..., None] * state
                     + jnp.einsum('bhsk,bhsv->bhkv', kc * jnp.exp(b_last - b), vc))
        return new_state, inter + intra

    init = jnp.zeros((B, H, dk, dv), dtype=jnp.float32)
    _, out = lax.scan(step, init, (chunked(q), chunked(k), chunked(v), chunked(log_f)))
    return jnp.moveaxis(out, 0, 2).reshape(B, H, S, dv)

def hgrn2_mixer(q_in, i_in, zf, zb, g_in, lb):
    B, S, W = q_in.shape
    H, dh = HGRN_HEADS, HEAD_DIM
    f32 = jnp.float32
    z = jnp.stack([zf, zb[:, ::-1]], axis=1).astype(f32)
    lbb = lb.astype(f32)[None, :, None, :]
    f = lbb + (1.0 - lbb) * jax.nn.sigmoid(z)
    log_f = jnp.log(f)
    k = 1.0 - f
    q = jax.nn.silu(q_in.astype(f32))
    v = i_in.astype(f32)
    q2 = jnp.stack([q, q[:, ::-1]], axis=1)
    v2 = jnp.stack([v, v[:, ::-1]], axis=1)

    def heads(t):
        return t.reshape(B, 2, S, H, dh).transpose(0, 1, 3, 2, 4).reshape(B, 2 * H, S, dh)

    o = hgrn2_chunk_scan(heads(q2), heads(k), heads(v2), heads(log_f)).reshape(B, 2, H, S, dh)
    o = o[:, 0] + o[:, 1][:, :, ::-1]
    o = o * lax.rsqrt(jnp.mean(o * o, axis=-1, keepdims=True) + RMS_EPS)
    o = o.transpose(0, 2, 1, 3).reshape(B, S, W)
    return o * jax.nn.silu(g_in.astype(f32))

def fourier_mixer(u):
    B, S, W = u.shape
    ug = u.astype(jnp.float32).reshape(B, S, FOURIER_GROUPS, W // FOURIER_GROUPS)
    y = jnp.fft.fft2(ug, axes=(1, 3), norm='ortho').real
    return y.reshape(B, S, W)

def rotary(t, positions):
    hd = t.shape[-1]
    inv_freq = ROPE_THETA ** (-jnp.arange(0, hd, 2, dtype=jnp.float32) / hd)
    ang = positions.astype(jnp.float32)[:, None, :, None] * inv_freq
    cos, sin = jnp.cos(ang), jnp.sin(ang)
    t1, t2 = t[..., :hd // 2], t[..., hd // 2:]
    return jnp.concatenate([t1 * cos - t2 * sin, t2 * cos + t1 * sin], axis=-1)

def dilated_window_attention(q, k, v, window, dilation):
    B, H, S, hd = q.shape
    d = dilation
    R = window // (2 * dilation)
    BLK = R
    L = S // d
    nb = -(-L // BLK)
    Lp = nb * BLK

    def sub(t):
        return t.reshape(B, H, L, d, hd).transpose(0, 1, 3, 2, 4)

    qs = jnp.pad(sub(q), ((0, 0), (0, 0), (0, 0), (0, Lp - L), (0, 0))).reshape(B, H, d, nb, BLK, hd)

    def key_blocks(t):
        tp = jnp.pad(sub(t), ((0, 0), (0, 0), (0, 0), (BLK, Lp - L + BLK), (0, 0))).reshape(B, H, d, nb + 2, BLK, hd)
        return jnp.concatenate([tp[:, :, :, :-2], tp[:, :, :, 1:-1], tp[:, :, :, 2:]], axis=-2)

    k3 = key_blocks(k)
    v3 = key_blocks(v)
    qj = jnp.arange(nb)[:, None, None] * BLK + jnp.arange(BLK)[None, :, None]
    kj = (jnp.arange(nb)[:, None, None] - 1) * BLK + jnp.arange(3 * BLK)[None, None, :]
    valid = (kj >= 0) & (kj < L) & (jnp.abs(qj - kj) <= R)
    s = jnp.einsum('bhrnqc,bhrnkc->bhrnqk', qs, k3)
    s = jnp.where(valid, s, NEG_BIG)
    lse = jax.nn.logsumexp(s, axis=-1)
    p = jnp.exp(s - lse[..., None])
    o = jnp.einsum('bhrnqk,bhrnkc->bhrnqc', p, v3)
    o = o.reshape(B, H, d, Lp, hd)[:, :, :, :L].transpose(0, 1, 3, 2, 4).reshape(B, H, S, hd)
    lse = lse.reshape(B, H, d, Lp)[..., :L].transpose(0, 1, 3, 2).reshape(B, H, S)
    return o, lse

def dilated_attention_mixer(cq, ck, cv, positions):
    B, S, W = cq.shape
    f32 = jnp.float32

    def heads(t):
        return t.astype(f32).reshape(B, S, ATTN_HEADS, HEAD_DIM).transpose(0, 2, 1, 3)

    q = rotary(heads(cq), positions) * (HEAD_DIM ** -0.5)
    k = rotary(heads(ck), positions)
    v = heads(cv)
    outs = []
    lses = []
    for window, dilation in DILATED_PATTERNS:
        o_p, lse_p = dilated_window_attention(q, k, v, window, dilation)
        outs.append(o_p)
        lses.append(lse_p)
    weights = jax.nn.softmax(jnp.stack(lses, axis=0), axis=0)
    o = jnp.sum(weights[..., None] * jnp.stack(outs, axis=0), axis=0)
    return o.transpose(0, 2, 1, 3).reshape(B, S, W)

def second_inputs(seed: int = 0) -> dict:
    key = jax.random.key(seed)
    ks = jax.random.split(key, 10)
    f32 = jnp.float32
    x = jax.random.normal(ks[0], (BATCH, SEQ, D_MODEL), f32)
    positions = jnp.broadcast_to(jnp.arange(SEQ, dtype=jnp.int32)[None, :], (BATCH, SEQ))
    attn_norm_w = 1.0 + 0.02 * jax.random.normal(ks[1], (DEPTH_2, D_MODEL), f32)
    w_in = jax.random.normal(ks[2], (DEPTH_2, D_MODEL, IN_WIDTH_2), f32) * D_MODEL ** -0.5
    hgrn_lower_bounds = 0.5 * jax.random.normal(ks[3], (DEPTH_2, 2, HGRN_WIDTH), f32)
    w_out = jax.random.normal(ks[4], (DEPTH_2, MIX_WIDTH_2, D_MODEL), f32) * MIX_WIDTH_2 ** -0.5
    mlp_norm_w = 1.0 + 0.02 * jax.random.normal(ks[5], (DEPTH_2, D_MODEL), f32)
    w_up = jax.random.normal(ks[6], (DEPTH_2, D_MODEL, D_FF), f32) * D_MODEL ** -0.5
    w_down = jax.random.normal(ks[7], (DEPTH_2, D_FF, D_MODEL), f32) * D_FF ** -0.5
    final_norm_w = 1.0 + 0.02 * jax.random.normal(ks[8], (D_MODEL,), f32)
    return {"x": x, "positions": positions, "attn_norm_w": attn_norm_w, "w_in": w_in,
            "hgrn_lower_bounds": hgrn_lower_bounds, "w_out": w_out, "mlp_norm_w": mlp_norm_w,
            "w_up": w_up, "w_down": w_down, "final_norm_w": final_norm_w}

def second_block(x, positions, attn_norm_w, w_in, hgrn_lower_bounds, w_out, mlp_norm_w, w_up, w_down, final_norm_w):
    p_lb = jax.nn.softmax(hgrn_lower_bounds.astype(jnp.float32), axis=0)
    lb_all = jnp.cumsum(p_lb, axis=0) - p_lb[0:1]
    for layer in range(DEPTH_2):
        h = rms_norm_2(x, attn_norm_w[layer])
        proj = h @ w_in[layer]
        a_q, a_i, a_zf, a_zb, a_g, b_u, c_q, c_k, c_v = jnp.split(proj, SPLIT_POINTS, axis=-1)
        o_a = hgrn2_mixer(a_q, a_i, a_zf, a_zb, a_g, lb_all[layer]).astype(x.dtype)
        o_b = fourier_mixer(b_u).astype(x.dtype)
        o_c = dilated_attention_mixer(c_q, c_k, c_v, positions).astype(x.dtype)
        mixed = jnp.concatenate([o_a, o_b, o_c], axis=-1)
        x = x + mixed @ w_out[layer]
        h = rms_norm_2(x, mlp_norm_w[layer])
        x = x + jnp.square(jax.nn.relu(h @ w_up[layer])) @ w_down[layer]
    return rms_norm_2(x, final_norm_w)


def setup_inputs(seed=0):
    out = dict(first_inputs(seed))
    for name, value in second_inputs(seed + 1).items():
        if name != "x":
            out[name + "_2"] = value
    return out


def reference(
    x, c, positions, w_ada, b_ada, g_pre_mix, g_post_mix, g_pre_ffn, g_post_ffn, w_in, g_q_a,
    g_kv_a, w_q_b, w_kv_b, w_o, w_router, b_router, w_mlp1, b_mlp1, w_mlp2, b_mlp2, positions_2,
    attn_norm_w_2, w_in_2, hgrn_lower_bounds_2, w_out_2, mlp_norm_w_2, w_up_2, w_down_2,
    final_norm_w_2,
):
    x = first_block(
        x, c, positions, w_ada, b_ada, g_pre_mix, g_post_mix, g_pre_ffn, g_post_ffn, w_in,
        g_q_a, g_kv_a, w_q_b, w_kv_b, w_o, w_router, b_router, w_mlp1, b_mlp1, w_mlp2, b_mlp2,
    )
    return second_block(
        x, positions_2, attn_norm_w_2, w_in_2, hgrn_lower_bounds_2, w_out_2, mlp_norm_w_2,
        w_up_2, w_down_2, final_norm_w_2,
    )


_drawn_inputs = setup_inputs


def setup_inputs(seed=0):
    import zlib

    import numpy as np

    out = dict(_drawn_inputs(seed))
    spreads = {}
    factors = {'g_post_mix': 8.0,
     'g_pre_ffn': 3.311,
     'g_post_ffn': 8.0,
     'g_q_a': 8.0,
     'g_kv_a': 8.0,
     'b_router': 5.115,
     'b_mlp1': 8.0,
     'b_mlp2': 8.0,
     'attn_norm_w_2': 3.951,
     'hgrn_lower_bounds_2': 4.31,
     'final_norm_w_2': 2.705}
    for name, (base, spread) in spreads.items():
        noise = np.random.default_rng([zlib.crc32(name.encode()), seed]).standard_normal(out[name].shape)
        drawn = base * np.exp(spread * noise) if base else spread * noise
        out[name] = jnp.asarray(drawn.astype(out[name].dtype))
    for name, factor in factors.items():
        out[name] = (out[name] * factor).astype(out[name].dtype)
    return out
```

```python
from contextlib import ExitStack

import numpy as np

import concourse.bass as bass
from concourse import mybir

ALU = mybir.AluOpType
ACT = mybir.ActivationFunctionType
AX = mybir.AxisListType
F32 = mybir.dt.float32
I32 = mybir.dt.int32
U32 = mybir.dt.uint32

P = 128
D = 1024
KD = D // P
S = 512
T = S // P
BANK = 512
NEG = -1e30
EPS = 1e-6

H1 = 8
Q_RANK, KV_RANK, ROPE = 256, 128, 32
NOPE, VDIM = 64, 64
QK1 = NOPE + ROPE
HD = 64
KV2 = 2
IDX_H, IDX_D = 8, 32
TOPK = 128
E = 32
TOP_E = 4
F = 1024
SPLITS1 = (Q_RANK, KV_RANK, ROPE, H1 * HD, KV2 * HD, KV2 * HD, IDX_H * IDX_D, IDX_D, IDX_H)
OFF1 = [sum(SPLITS1[:i]) for i in range(len(SPLITS1) + 1)]
IN1 = OFF1[-1]

L2 = 2
GW = 256
AW = 512
IN2 = 5 * GW + GW + 3 * AW
H2 = AW // HD
DFF = 4 * D
PATTERNS = ((128, 1), (512, 4), (2048, 16))

PANELS = 3
PW = KD * BANK


def shape_constants():
    f32 = np.float32
    i = np.arange(P)
    c = {}
    c["ident"] = np.eye(P, dtype=f32)
    c["flip"] = np.eye(P, dtype=f32)[::-1].copy()
    c["causal"] = np.where(i[None, :] <= i[:, None], 0.0, NEG).astype(f32)
    c["before"] = (i[:, None] < i[None, :]).astype(f32)
    c["iota"] = np.tile(np.arange(S, dtype=f32)[None, :], (P, 1))
    c["tok"] = (i[:, None] + P * np.arange(T)[None, :]).astype(f32)
    half = ROPE // 2
    c["freq1"] = np.tile((f32(10000.0) ** (-np.arange(half, dtype=f32) / f32(half))).astype(f32)[None, :], (P, 1))
    half = HD // 2
    c["freq2"] = np.tile((f32(10000.0) ** (-np.arange(0, HD, 2, dtype=f32) / f32(HD))).astype(f32)[None, :], (P, 1))
    q = np.arange(S)
    count = np.zeros((S, S))
    for window, dil in PATTERNS:
        r = window // (2 * dil)
        same = (q[:, None] % dil) == (q[None, :] % dil)
        count += same & (np.abs(q[:, None] // dil - q[None, :] // dil) <= r)
    scale = HD ** -0.5
    table = np.where(count > 0, np.log(np.maximum(count, 1)), NEG) / scale
    c["pairs"] = table.astype(f32).reshape(T, P, S).transpose(1, 0, 2).reshape(P, T * S).copy()
    a = 2 * np.pi * ((q[:, None] * q[None, :]) % S) / S
    c["dft_cos"] = (np.cos(a) / np.sqrt(S)).astype(f32).reshape(T, P, S).transpose(1, 0, 2).reshape(P, T * S).copy()
    c["dft_sin"] = (np.sin(a) / np.sqrt(S)).astype(f32).reshape(T, P, S).transpose(1, 0, 2).reshape(P, T * S).copy()
    h = np.arange(HD)
    a = 2 * np.pi * ((h[:, None] * h[None, :]) % HD) / HD
    ch = np.zeros((P, 2, P))
    for g in range(2):
        s = slice(g * HD, (g + 1) * HD)
        ch[s, 0, s] = np.cos(a) / np.sqrt(HD)
        ch[s, 1, s] = -np.sin(a) / np.sqrt(HD)
    c["dft_ch"] = ch.astype(f32).reshape(P, 2 * P)
    lv = np.zeros((P, 8, P), np.int32)
    for n in range(7):
        lv[:, n, :] = ((i[:, None] >> (n + 1)) == (i[None, :] >> (n + 1))) & (((i[:, None] >> n) & 1) == 0) & (((i[None, :] >> n) & 1) == 1)
    lv[:, 7, :] = np.eye(P)
    c["split"] = lv.reshape(P, 8 * P)
    c["heads2"] = np.kron(np.eye(2), np.ones((HD, HD))).astype(f32)
    return c


class Signal:

    def __init__(self, sem):
        self.sem, self.base = sem, 0

    def __call__(self, n):
        return self.sem, self.base + n

    def passed(self, n):
        self.base += n


class Chain:

    def __init__(self, eng, signal):
        self.eng, self.count, self.n = eng, signal, 0

    def __call__(self, ins):
        self.n += 1
        ins.then_inc(self.count.sem, 1)
        self.eng.wait_ge(*self.count(self.n))


class Core:
    def __init__(self, nc, ctx, ins, out):
        self.nc, self.ctx, self.ins, self.out = nc, ctx, ins, out
        self.events = {}
        self.tensors = 0

    def event(self, name):
        if name not in self.events:
            self.events[name] = Signal(self.ctx.enter_context(self.nc.semaphore(name)))
        return self.events[name]

    def sb(self, name, shape, dtype=F32, ctx=None):
        self.tensors += 1
        return (ctx or self.ctx).enter_context(self.nc.sbuf_tensor(f"{name}_{self.tensors}", shape, dtype))

    def step(self, name, eng, signal_total):
        c = Chain(eng, self.event(name))
        signal_total.append(c)
        return c


def close(chains):
    for c in chains:
        c.count.passed(c.n)


class Panels:

    def __init__(self, core, ring, sources):
        self.ring, self.sources, self.issued, self.used = ring, sources, 0, 0
        self.full = [core.event(f"panel_full{i}") for i in range(PANELS)]
        self.used_at = []

    def place(self, p, width=BANK):
        return self.ring[:, p % PANELS, :].rearrange("p (k n) -> p k n", k=KD)[:, :, 0:width]

    def load_ahead(self, sp, count):
        last = min(self.used + count + PANELS, len(self.sources))
        while self.issued < last:
            p = self.issued
            if p >= PANELS:
                sp.wait_ge(*self.used_at[p - PANELS])
            src = self.sources[p]
            sp.dma_start(self.place(p, src.shape[2]), src).then_inc(self.full[p % PANELS].sem, 16)
            self.issued += 1

    def close(self):
        for p in range(len(self.sources)):
            self.full[p % PANELS].passed(16)

    def arrived(self, pe, p):
        pe.wait_ge(*self.full[p % PANELS](16 * (p // PANELS + 1)))


def panel_of(w, r, n, width=BANK):
    return w[r * D:(r + 1) * D, n:n + width].rearrange("(k p) n -> p k n", p=P)


def load_stage(core, loads, name):
    nc, arrived_a, arrived_b = core.nc, core.event(name + "_a"), core.event(name + "_b")
    halves = loads[0::2], loads[1::2]
    with nc.Block() as block:
        @block.sync
        def _(sp):
            for dst, src in halves[0]:
                sp.dma_start(dst, src).then_inc(arrived_a.sem, 16)
            if halves[0]:
                sp.wait_ge(*arrived_a(16 * len(halves[0])))

        @block.scalar
        def _(act):
            for dst, src in halves[1]:
                act.dma_start(dst, src).then_inc(arrived_b.sem, 16)
            if halves[1]:
                act.wait_ge(*arrived_b(16 * len(halves[1])))
    arrived_a.passed(16 * len(halves[0]))
    arrived_b.passed(16 * len(halves[1]))


def transposes_pe(core, pe, src_tile, done, bank0):
    for j in range(2):
        for c in range(4):
            k = 4 * j + c
            last = core.nc.tensor.transpose(core.psum[:, bank0 + j, c * P:(c + 1) * P], src_tile[:, k * P:(k + 1) * P], core.ident[:])
        last.then_inc(done.sem, 1)


def norm_stage(core, x, gain, shift, h, hT=None, out=None):
    nc, stats = core.nc, core.stats
    squares, spread, root = core.event("squares"), core.event("mean_square"), core.event("root")
    h_ready, turned = core.event("h_ready"), core.event("turned")
    stored = core.event("stored")
    ms, rt, rstd = stats[:, 0:T], stats[:, T:2 * T], stats[:, 2 * T:3 * T]
    chains = []
    with nc.Block() as block:
        @block.scalar
        def _(act):
            for t in range(T):
                if t:
                    act.wait_ge(*squares(t))
                nc.scalar.activation(core.junk[:, 0, :], x[:, t, :], ACT.Square, accum_out=stats[:, 3 * T + t:3 * T + t + 1]).then_inc(squares.sem, 1)
            act.wait_ge(*spread(1))
            nc.scalar.activation(rt, ms, ACT.Sqrt).then_inc(root.sem, 1)
            if hT is not None:
                for j in range(2 * T):
                    t = j // 2
                    act.wait_ge(*turned(j + 1))
                    nc.scalar.activation(hT[:, 4 * (j % 2):4 * (j % 2) + 4, t * P:(t + 1) * P],
                                         core.psum[:, j, :].rearrange("p (k n) -> p k n", k=4), ACT.Copy)

        @block.vector
        def _(dve):
            step = core.step("dve_step", dve, chains)
            dve.wait_ge(*squares(T))
            nc.vector.tensor_scalar(ms, stats[:, 3 * T:4 * T], 1.0 / D, EPS, ALU.mult, ALU.add).then_inc(spread.sem, 1)
            dve.wait_ge(*root(1))
            step(nc.vector.reciprocal(rstd, rt))
            for t in range(T):
                ins = nc.vector.scalar_tensor_tensor(out=h[:, t, :], in0=x[:, t, :], scalar=rstd[:, t:t + 1], in1=gain, op0=ALU.mult, op1=ALU.mult)
                if shift is not None:
                    step(ins)
                    ins = nc.vector.tensor_tensor(h[:, t, :], h[:, t, :], shift, ALU.add)
                ins.then_inc(h_ready.sem, 1)

        if hT is not None:
            @block.tensor
            def _(pe):
                for t in range(T):
                    pe.wait_ge(*h_ready(t + 1))
                    transposes_pe(core, pe, h[:, t, :], turned, 2 * t)

        if out is not None:
            @block.sync
            def _(sp):
                for t in range(T):
                    sp.wait_ge(*h_ready(t + 1))
                    sp.dma_start(out[t * P:(t + 1) * P, :], h[:, t, :]).then_inc(stored.sem, 16)
                sp.wait_ge(*stored(16 * T))
    squares.passed(T); spread.passed(1); root.passed(1); h_ready.passed(T)
    if hT is not None:
        turned.passed(2 * T)
    if out is not None:
        stored.passed(16 * T)
    close(chains)


def transpose_stage(core, src, dstT):
    nc, turned = core.nc, core.event("turned")
    with nc.Block() as block:
        @block.tensor
        def _(pe):
            for t in range(T):
                transposes_pe(core, pe, src[:, t, :], turned, 2 * t)

        def copy(eng, do, j):
            eng.wait_ge(*turned(j + 1))
            do(dstT[:, 4 * (j % 2):4 * (j % 2) + 4, (j // 2) * P:(j // 2 + 1) * P], core.psum[:, j, :].rearrange("p (k n) -> p k n", k=4))

        @block.scalar
        def _(act):
            for j in range(0, 2 * T, 2):
                copy(act, lambda o, i: nc.scalar.activation(o, i, ACT.Copy), j)

        @block.vector
        def _(dve):
            for j in range(1, 2 * T, 2):
                copy(dve, lambda o, i: nc.vector.tensor_copy(o, i), j)
    turned.passed(2 * T)


def product_stage(core, panels, hT, widths, take):
    nc = core.nc
    product, taken = core.event("product"), core.event("product_taken")
    first = panels.used
    panels.used_at += [product(T * (n + 1)) for n in range(len(widths))]
    with nc.Block() as block:
        @block.sync
        def _(sp):
            panels.load_ahead(sp, len(widths))

        @block.tensor
        def _(pe):
            i = 0
            for n, width in enumerate(widths):
                panels.arrived(pe, first + n)
                w = panels.place(first + n, width)
                for t in range(T):
                    if i >= 8:
                        pe.wait_ge(*taken(i - 7))
                    for k in range(KD):
                        last = nc.tensor.matmul(core.psum[:, i % 8, 0:width], hT[:, k, t * P:(t + 1) * P], w[:, k, :], start=(k == 0), stop=(k == KD - 1))
                    last.then_inc(product.sem, 1)
                    i += 1

        @block.vector
        def _(dve):
            for n, width in enumerate(widths):
                for t in range(T):
                    i = n * T + t
                    dve.wait_ge(*product(i + 1))
                    take(n, t, core.psum[:, i % 8, 0:width]).then_inc(taken.sem, 1)
    panels.used += len(widths)
    product.passed(T * len(widths))
    taken.passed(T * len(widths))


def residual_stage(core, x, y, gain):
    nc, stats = core.nc, core.stats
    squares, spread, root = core.event("squares"), core.event("mean_square"), core.event("root")
    ms, rt, rstd = stats[:, 0:T], stats[:, T:2 * T], stats[:, 2 * T:3 * T]
    chains = []
    with nc.Block() as block:
        @block.scalar
        def _(act):
            for t in range(T):
                if t:
                    act.wait_ge(*squares(t))
                nc.scalar.activation(core.junk[:, 0, :], y[:, t, :], ACT.Square, accum_out=stats[:, 3 * T + t:3 * T + t + 1]).then_inc(squares.sem, 1)
            act.wait_ge(*spread(1))
            nc.scalar.activation(rt, ms, ACT.Sqrt).then_inc(root.sem, 1)

        @block.vector
        def _(dve):
            step = core.step("dve_step", dve, chains)
            dve.wait_ge(*squares(T))
            nc.vector.tensor_scalar(ms, stats[:, 3 * T:4 * T], 1.0 / D, EPS, ALU.mult, ALU.add).then_inc(spread.sem, 1)
            dve.wait_ge(*root(1))
            step(nc.vector.reciprocal(rstd, rt))
            for t in range(T):
                step(nc.vector.scalar_tensor_tensor(out=y[:, t, :], in0=y[:, t, :], scalar=rstd[:, t:t + 1], in1=gain, op0=ALU.mult, op1=ALU.mult))
                step(nc.vector.tensor_tensor(x[:, t, :], x[:, t, :], y[:, t, :], ALU.add))
    squares.passed(T); spread.passed(1); root.passed(1)
    close(chains)


def angles(core, step, posf, freq, cos, sin, tmp):
    nc = core.nc
    magic = 1.5 * 2.0 ** 23
    c1 = 6.28125
    c2 = float(np.float32(np.round((2 * np.pi - c1) * 2 ** 21) / 2 ** 21))
    c3 = float(np.float32(2 * np.pi - c1 - c2))
    ang, turns, red = tmp
    for t in range(T):
        step(nc.vector.tensor_scalar(ang[:, t, :], freq, posf[:, t:t + 1], None, ALU.mult))
    for out, quarter in ((cos, 0.25), (sin, 0.0)):
        step(nc.vector.tensor_scalar(turns, ang, 1.0 / (2 * np.pi), quarter, ALU.mult, ALU.add))
        step(nc.vector.tensor_scalar(turns, turns, magic, None, ALU.add))
        step(nc.vector.tensor_scalar(turns, turns, magic, None, ALU.subtract))
        step(nc.vector.scalar_tensor_tensor(out=red, in0=turns, scalar=-c1, in1=ang, op0=ALU.mult, op1=ALU.add))
        step(nc.vector.scalar_tensor_tensor(out=red, in0=turns, scalar=-c2, in1=red, op0=ALU.mult, op1=ALU.add))
        step(nc.vector.scalar_tensor_tensor(out=red, in0=turns, scalar=-c3, in1=red, op0=ALU.mult, op1=ALU.add))
        step(nc.vector.tensor_scalar(red, red, quarter * 2 * np.pi, 3.1415925, ALU.add, ALU.min))
        step(nc.vector.tensor_scalar(out, red, -3.1415925, None, ALU.max))


def angle_stage(core, posi, posf, freq, half, cos, sin, tmp):
    nc, reduced = core.nc, core.event("angles_reduced")
    chains = []
    with nc.Block() as block:
        @block.vector
        def _(dve):
            step = core.step("dve_step", dve, chains)
            step(nc.vector.tensor_copy(posf[:], posi[:]))
            angles(core, step, posf, freq, cos[:], sin[:], tmp)
            dve.sem_inc(reduced.sem, 1)

        @block.scalar
        def _(act):
            act.wait_ge(*reduced(1))
            nc.scalar.activation(cos[:], cos[:], ACT.Sin)
            nc.scalar.activation(sin[:], sin[:], ACT.Sin)
    reduced.passed(1)
    close(chains)


def rotate(nc, step, dst, src, cos, sin, tmp, heads, half):
    c = cos.unsqueeze(1).broadcast_to([P, heads, half])
    s = sin.unsqueeze(1).broadcast_to([P, heads, half])
    a, b = src[:, :, 0:half], src[:, :, half:2 * half]
    t1, t2 = tmp[:, 0, 0:heads, 0:half], tmp[:, 1, 0:heads, 0:half]
    nc.vector.tensor_tensor(t1, a, c, ALU.mult)
    step(nc.vector.tensor_tensor(t2, b, s, ALU.mult))
    t3, t4 = tmp[:, 2, 0:heads, 0:half], tmp[:, 3, 0:heads, 0:half]
    nc.vector.tensor_tensor(t3, b, c, ALU.mult)
    step(nc.vector.tensor_tensor(t4, a, s, ALU.mult))
    nc.vector.tensor_tensor(dst[:, :, 0:half], t1, t2, ALU.subtract)
    step(nc.vector.tensor_tensor(dst[:, :, half:2 * half], t3, t4, ALU.add))


def attention_stage(core, units, scale, prepare=None):
    nc = core.nc
    n = len(units)
    scores, biased = core.event("scores"), core.event("scores_biased")
    probs, turned, turned_sb = core.event("probs"), core.event("probs_turned"), core.event("probs_turned_sb")
    summed, done = core.event("values_summed"), core.event("head_out")
    chains = []
    with ExitStack() as ctx:
        s_sb = core.sb("att_scores", [P, 3, S], ctx=ctx)
        p_sb = core.sb("att_probs", [P, 3, S], ctx=ctx)
        pt_sb = core.sb("att_turned", [P, 3, S], ctx=ctx)
        top = core.sb("att_max", [P, 4], ctx=ctx)
        low = core.sb("att_negmax", [P, 4], ctx=ctx)
        den = core.sb("att_den", [P, 4], ctx=ctx)
        inv = core.sb("att_inv", [P, 4], ctx=ctx)
        with nc.Block() as block:
            @block.tensor
            def _(pe):
                def score(u):
                    q, k, _, _, _, keys = units[u]
                    if u >= 3:
                        pe.wait_ge(*biased(u - 2))
                    nc.tensor.matmul(core.psum[:, u % 3, 0:keys], q, k, start=True, stop=True).then_inc(scores.sem, 1)

                def turn(u):
                    keys = units[u][5]
                    pe.wait_ge(*probs(u + 1))
                    if u >= 3:
                        pe.wait_ge(*turned_sb(u - 2))
                    for j in range(keys // P):
                        last = nc.tensor.transpose(core.psum[:, 3 + u % 3, j * P:(j + 1) * P], p_sb[:, u % 3, j * P:(j + 1) * P], core.ident[:])
                    last.then_inc(turned.sem, 1)

                def values(u):
                    _, _, _, v, _, keys = units[u]
                    pe.wait_ge(*turned_sb(u + 1))
                    if u >= 2:
                        pe.wait_ge(*done(u - 1))
                    for j in range(keys // P):
                        last = nc.tensor.matmul(core.psum[:, 6 + u % 2, 0:HD], pt_sb[:, u % 3, j * P:(j + 1) * P], v(j), start=(j == 0), stop=(j == keys // P - 1))
                    last.then_inc(summed.sem, 1)

                for u in range(n + 3):
                    if u < n:
                        score(u)
                    if 2 <= u < n + 2:
                        turn(u - 2)
                    if u >= 3:
                        values(u - 3)

            @block.vector
            def _(dve):
                step = core.step("dve_step", dve, chains)

                def bias(u):
                    _, _, b, _, _, keys = units[u]
                    if prepare is not None:
                        prepare(step, u)
                    dve.wait_ge(*scores(u + 1))
                    if u >= 3:
                        dve.wait_ge(*probs(u - 2))
                    step(nc.vector.tensor_tensor_reduce(out=s_sb[:, u % 3, 0:keys], in0=core.psum[:, u % 3, 0:keys], in1=b, scale=scale, scalar=-3e38,
                                                        op0=ALU.add, op1=ALU.max, accum_out=top[:, u % 4:u % 4 + 1]))
                    nc.vector.tensor_scalar(low[:, u % 4:u % 4 + 1], top[:, u % 4:u % 4 + 1], -1.0, None, ALU.mult).then_inc(biased.sem, 1)

                def finish(u):
                    dve.wait_ge(*summed(u + 1))
                    step(nc.vector.reciprocal(inv[:, u % 4:u % 4 + 1], den[:, u % 4:u % 4 + 1]))
                    nc.vector.tensor_scalar(units[u][4], core.psum[:, 6 + u % 2, 0:HD], inv[:, u % 4:u % 4 + 1], None, ALU.mult).then_inc(done.sem, 1)

                for u in range(n + 3):
                    if u < n:
                        bias(u)
                    if u >= 3:
                        finish(u - 3)

            @block.scalar
            def _(act):
                def exps(u):
                    keys = units[u][5]
                    act.wait_ge(*biased(u + 1))
                    if u >= 3:
                        act.wait_ge(*turned(u - 2))
                    if u >= 4:
                        act.wait_ge(*done(u - 3))
                    nc.scalar.activation(p_sb[:, u % 3, 0:keys], s_sb[:, u % 3, 0:keys], ACT.Exp, bias=low[:, u % 4:u % 4 + 1], accum_out=den[:, u % 4:u % 4 + 1]).then_inc(probs.sem, 1)

                def copy(u):
                    keys = units[u][5]
                    act.wait_ge(*turned(u + 1))
                    if u >= 3:
                        act.wait_ge(*summed(u - 2))
                    nc.scalar.activation(pt_sb[:, u % 3, 0:keys], core.psum[:, 3 + u % 3, 0:keys], ACT.Copy).then_inc(turned_sb.sem, 1)

                for u in range(n + 2):
                    if u < n:
                        exps(u)
                    if u >= 2:
                        copy(u - 2)
    for s in (scores, biased, probs, turned, turned_sb, summed, done):
        s.passed(n)
    close(chains)


def turn_stage(core, turns):
    nc, turned, taken_a, taken_d = core.nc, core.event("turned"), core.event("taken_act"), core.event("taken_dve")
    n = len(turns)
    with nc.Block() as block:
        @block.tensor
        def _(pe):
            for i, (dst, srcs, m) in enumerate(turns):
                if i >= 8:
                    j = i - 8
                    pe.wait_ge(*(taken_d if j % 2 else taken_a)(j // 2 + 1))
                for c, src in enumerate(srcs):
                    bank = core.psum[0:src.shape[1], i % 8, c * P:(c + 1) * P]
                    if m is core.ident:
                        last = nc.tensor.transpose(bank, src, m[:])
                    else:
                        last = nc.tensor.matmul(bank, src, m[:], start=True, stop=True)
                last.then_inc(turned.sem, 1)

        @block.scalar
        def _(act):
            for i in range(0, n, 2):
                act.wait_ge(*turned(i + 1))
                dst, srcs, _ = turns[i]
                nc.scalar.activation(dst, core.psum[0:srcs[0].shape[1], i % 8, 0:P * len(srcs)], ACT.Copy).then_inc(taken_a.sem, 1)

        @block.vector
        def _(dve):
            for i in range(1, n, 2):
                dve.wait_ge(*turned(i + 1))
                dst, srcs, _ = turns[i]
                nc.vector.tensor_copy(dst, core.psum[0:srcs[0].shape[1], i % 8, 0:P * len(srcs)]).then_inc(taken_d.sem, 1)
    turned.passed(n)
    taken_a.passed((n + 1) // 2)
    taken_d.passed(n // 2)


def modulation_stage(core, panels, mod, silu_c, bias):
    nc = core.nc
    raw, wide, product, taken = core.event("silu_c"), core.event("c_wide"), core.event("product"), core.event("product_taken")
    count = len(panels.sources[:12])
    first = panels.used
    panels.used_at += [product(n + 1) for n in range(count)]
    with ExitStack() as ctx:
        c_wide = core.sb("c_wide", [P, KD, P], ctx=ctx)
        with nc.Block() as block:
            @block.sync
            def _(sp):
                panels.load_ahead(sp, count)

            @block.scalar
            def _(act):
                nc.scalar.activation(silu_c[:, 1, :], silu_c[:, 0, :], ACT.Exp, scale=-1.0).then_inc(raw.sem, 1)

            @block.vector
            def _(dve):
                dve.wait_ge(*raw(1))
                nc.vector.tensor_scalar(silu_c[:, 1, :], silu_c[:, 1, :], 1.0, None, ALU.add).then_inc(raw.sem, 1)
                dve.wait_ge(*raw(2))
                nc.vector.reciprocal(silu_c[:, 1, :], silu_c[:, 1, :]).then_inc(raw.sem, 1)
                dve.wait_ge(*raw(3))
                nc.vector.tensor_tensor(silu_c[:, 0, :], silu_c[:, 0, :], silu_c[:, 1, :], ALU.mult).then_inc(raw.sem, 1)
                dve.wait_ge(*raw(4))
                nc.vector.tensor_copy(c_wide[:], silu_c[:, 0, :].unsqueeze(2).broadcast_to([P, KD, P])).then_inc(wide.sem, 1)
                for n in range(count):
                    dve.wait_ge(*product(n + 1))
                    cols = slice(n * BANK, (n + 1) * BANK)
                    nc.vector.tensor_tensor(mod[:, cols], core.psum[:, n % 8, :], bias[:, cols], ALU.add).then_inc(taken.sem, 1)

            @block.tensor
            def _(pe):
                pe.wait_ge(*wide(1))
                for n in range(count):
                    panels.arrived(pe, first + n)
                    if n >= 8:
                        pe.wait_ge(*taken(n - 7))
                    w = panels.place(first + n)
                    for k in range(KD):
                        last = nc.tensor.matmul(core.psum[:, n % 8, :], c_wide[:, k, :], w[:, k, :], start=(k == 0), stop=(k == KD - 1))
                    last.then_inc(product.sem, 1)
    panels.used += count
    raw.passed(4); wide.passed(1); product.passed(count); taken.passed(count)


def gains_stage(core, mod, gains):
    nc = core.nc
    chains = []
    part = [mod[:, n * D:(n + 1) * D] for n in range(6)]
    with nc.Block() as block:
        @block.vector
        def _(dve):
            for n, g, one in ((1, 0, 1.0), (2, 1, 0.0), (4, 2, 1.0), (5, 3, 0.0)):
                nc.vector.scalar_tensor_tensor(out=part[n], in0=part[n], scalar=one, in1=gains[:, g, :], op0=ALU.add, op1=ALU.mult)


def mla_stages(core, proj, y, hT, cos, sin, W):
    nc, stats = core.nc, core.stats
    cq, ckv = proj[:, :, 0:Q_RANK], proj[:, :, OFF1[1]:OFF1[2]]
    squares, spread, root = core.event("squares"), core.event("mean_square"), core.event("root")
    chains = []
    ms, rt, rstd = stats[:, 0:2 * T], stats[:, 2 * T:4 * T], stats[:, 4 * T:6 * T]
    with ExitStack() as ctx:
        qT = hT[0:QK1]
        kT = core.sb("mla_kT", [QK1, H1, S], ctx=ctx)
        v = core.sb("mla_v", [P, T, H1 * VDIM], ctx=ctx)
        with ExitStack() as inner:
            gq = core.sb("gain_q", [P, Q_RANK], ctx=inner)
            gkv = core.sb("gain_kv", [P, KV_RANK], ctx=inner)
            wq = core.sb("w_q_b", [P, 2, H1 * QK1], ctx=inner)
            wkv = core.sb("w_kv_b", [P, H1 * (NOPE + VDIM)], ctx=inner)
            latT = core.sb("latentsT", [P, 3, S], ctx=inner)
            qk = core.sb("mla_q_and_k", [P, H1, QK1], ctx=inner)
            kk = core.sb("mla_k_full", [P, H1, QK1], ctx=inner)
            tmp = core.sb("rotate_tmp", [P, 4, H1, ROPE // 2], ctx=inner)
            krot = core.sb("k_rotated", [P, T, 1, ROPE], ctx=inner)
            load_stage(core, [(gq[:], W["g_q_a"][0].partition_broadcast(P)), (gkv[:], W["g_kv_a"][0].partition_broadcast(P)),
                              (wq[:], W["w_q_b"][0].rearrange("(k p) n -> p k n", p=P)), (wkv[:], W["w_kv_b"][0])], "latent_weights")
            with nc.Block() as block:
                @block.scalar
                def _(act):
                    for i in range(2 * T):
                        src = (cq if i < T else ckv)[:, i % T, :]
                        if i:
                            act.wait_ge(*squares(i))
                        nc.scalar.activation(core.junk[:, 0, 0:src.shape[1]], src, ACT.Square, accum_out=stats[:, 6 * T + i:6 * T + i + 1]).then_inc(squares.sem, 1)
                    act.wait_ge(*spread(1))
                    nc.scalar.activation(rt, ms, ACT.Sqrt).then_inc(root.sem, 1)

                @block.vector
                def _(dve):
                    step = core.step("dve_step", dve, chains)
                    dve.wait_ge(*squares(2 * T))
                    nc.vector.tensor_scalar(ms[:, 0:T], stats[:, 6 * T:7 * T], 1.0 / Q_RANK, EPS, ALU.mult, ALU.add)
                    step(nc.vector.tensor_scalar(ms[:, T:2 * T], stats[:, 7 * T:8 * T], 1.0 / KV_RANK, EPS, ALU.mult, ALU.add))
                    dve.sem_inc(spread.sem, 1)
                    dve.wait_ge(*root(1))
                    step(nc.vector.reciprocal(rstd, rt))
                    for t in range(T):
                        nc.vector.scalar_tensor_tensor(out=cq[:, t, :], in0=cq[:, t, :], scalar=rstd[:, t:t + 1], in1=gq[:], op0=ALU.mult, op1=ALU.mult)
                        nc.vector.scalar_tensor_tensor(out=ckv[:, t, :], in0=ckv[:, t, :], scalar=rstd[:, T + t:T + t + 1], in1=gkv[:], op0=ALU.mult, op1=ALU.mult)
            squares.passed(2 * T); spread.passed(1); root.passed(1)
            close(chains)
            chains = []
            turn_stage(core, [(latT[:, c, :], [proj[:, t, c * P:(c + 1) * P] for t in range(T)], core.ident) for c in range(3)])
            made, rotated, k_full, turned, taken = (core.event(s) for s in ("qkv_made", "q_rotated", "k_full", "turned", "product_taken"))
            with nc.Block() as block:
                @block.tensor
                def _(pe):
                    for t in range(T):
                        tile = slice(t * P, (t + 1) * P)
                        if t:
                            pe.wait_ge(*rotated(t))
                            pe.wait_ge(*k_full(t))
                        for n, w in ((0, 4 * QK1), (1, 4 * QK1)):
                            for c in range(2):
                                nc.tensor.matmul(core.psum[:, n, 0:w], latT[:, c, tile], wq[:, c, n * w:(n + 1) * w], start=(c == 0), stop=(c == 1))
                        for n in range(2):
                            last = nc.tensor.matmul(core.psum[:, 2 + n, :], latT[:, 2, tile], wkv[:, n * BANK:(n + 1) * BANK], start=True, stop=True)
                        last.then_inc(made.sem, 1)
                        for i, src in enumerate((qk, kk)):
                            pe.wait_ge(*(rotated, k_full)[i](t + 1))
                            if t:
                                pe.wait_ge(*taken(4 * (t - 1) + 2 * i + 2))
                            for h in range(H1):
                                last = nc.tensor.transpose(core.psum[0:QK1, 4 + 2 * i + h // 4, (h % 4) * P:(h % 4 + 1) * P], src[:, h, :], core.ident[:])
                            last.then_inc(turned.sem, 1)

                @block.vector
                def _(dve):
                    step = core.step("dve_step", dve, chains)
                    for t in range(T):
                        rotate(nc, step, krot[:, t], proj[:, t, OFF1[2]:OFF1[3]].unsqueeze(1), cos[:, t, :], sin[:, t, :], tmp, 1, ROPE // 2)
                    for t in range(T):
                        dve.wait_ge(*made(t + 1))
                        if t:
                            dve.wait_ge(*turned(2 * t))
                        for n in range(2):
                            half = core.psum[:, n, 0:4 * QK1].rearrange("p (h d) -> p h d", h=4)
                            nc.vector.tensor_copy(qk[:, 4 * n:4 * n + 4, 0:NOPE], half[:, :, 0:NOPE])
                            rotate(nc, step, qk[:, 4 * n:4 * n + 4, NOPE:QK1], half[:, :, NOPE:QK1], cos[:, t, :], sin[:, t, :], tmp, 4, ROPE // 2)
                        dve.sem_inc(rotated.sem, 1)
                        for n in range(2):
                            half = core.psum[:, 2 + n, :].rearrange("p (h d) -> p h d", h=4)
                            nc.vector.tensor_copy(kk[:, 4 * n:4 * n + 4, 0:NOPE], half[:, :, 0:NOPE])
                            nc.vector.tensor_copy(v[:, t, n * 4 * VDIM:(n + 1) * 4 * VDIM].rearrange("p (h d) -> p h d", h=4), half[:, :, NOPE:])
                        step(nc.vector.tensor_copy(kk[:, :, NOPE:QK1], krot[:, t].broadcast_to([P, H1, ROPE])))
                        dve.sem_inc(k_full.sem, 1)

                @block.scalar
                def _(act):
                    for t in range(T):
                        for i, dst in enumerate((qT, kT)):
                            act.wait_ge(*turned(2 * t + i + 1))
                            for n in range(2):
                                nc.scalar.activation(dst[:, 4 * n:4 * n + 4, t * P:(t + 1) * P], core.psum[0:QK1, 4 + 2 * i + n, :].rearrange("p (h m) -> p h m", h=4), ACT.Copy).then_inc(taken.sem, 1)
            made.passed(T); rotated.passed(T); k_full.passed(T); turned.passed(2 * T); taken.passed(4 * T)
            close(chains)
        units = []
        for t in range(T):
            keys = (t + 1) * P
            for h in range(H1):
                units.append((qT[:, h, t * P:(t + 1) * P], kT[:, h, 0:keys], core.mask[:, (T - 1 - t) * P:(T - 1 - t) * P + keys],
                              lambda j, h=h: v[:, j, h * VDIM:(h + 1) * VDIM], y[:, t, h * VDIM:(h + 1) * VDIM], keys))
        attention_stage(core, units, QK1 ** -0.5)


def dsa_stages(core, proj, y, hT, posf, W):
    nc = core.nc
    qo, ko, vo, qio, kio, wio = OFF1[3:9]
    with ExitStack() as ctx:
        qT = hT[:, 0:H1 // 2, :]
        kT = hT[:, H1 // 2:H1 // 2 + KV2, :]
        dist = core.sb("dsa_dist", [P, T, S], ctx=ctx)
        sel = core.sb("dsa_sel", [P, T, S], ctx=ctx)
        twice = core.sb("dsa_twice", [P, T, 3, P], ctx=ctx)
        posk_i = core.sb("key_pos_i", [P, S], I32, ctx=ctx)
        biasb = core.sb("dsa_bias", [P, 2, S], ctx=ctx)
        with ExitStack() as inner:
            qiT = core.sb("idx_qT", [P, 2, S], ctx=inner)
            kiT = core.sb("idx_kT", [P, S], ctx=inner)
            rel = core.sb("idx_rel", [P, 2, S], ctx=inner)
            best = core.sb("idx_best", [P, 8], ctx=inner)
            load_stage(core, [(posk_i[:], W["positions"][0].partition_broadcast(P))], "key_positions")
            chains = []
            with nc.Block() as block:
                @block.vector
                def _(dve):
                    step = core.step("dve_step", dve, chains)
                    for g in range(2):
                        nc.vector.tensor_copy(twice[:, :, 0, g * HD:(g + 1) * HD], proj[:, :, ko:ko + HD])
                        nc.vector.tensor_copy(twice[:, :, 1, g * HD:(g + 1) * HD], proj[:, :, ko + HD:ko + 2 * HD])
                    for g in range(4):
                        nc.vector.tensor_copy(twice[:, :, 2, g * IDX_D:(g + 1) * IDX_D], proj[:, :, kio:kio + IDX_D])
                    nc.vector.tensor_scalar(proj[:, :, wio:wio + IDX_H], proj[:, :, wio:wio + IDX_H], IDX_H ** -0.5, None, ALU.mult)
                    step(nc.vector.tensor_copy(biasb[:, 0, :], posk_i[:]))
                    for t in range(T):
                        step(nc.vector.tensor_scalar(dist[:, t, :], biasb[:, 0, :], posf[:, t:t + 1], None, ALU.subtract))
                        nc.vector.scalar_tensor_tensor(out=dist[:, t, :], in0=dist[:, t, :], scalar=-1.0, in1=dist[:, t, :], op0=ALU.mult, op1=ALU.max)
            close(chains)
            turns = [(kT[:, g, :], [twice[:, t, g, :] for t in range(T)], core.ident) for g in range(KV2)]
            turns += [(kiT[:], [twice[:, t, 2, :] for t in range(T)], core.ident)]
            turns += [(qiT[:, c, :], [proj[:, t, qio + c * P:qio + (c + 1) * P] for t in range(T)], core.ident) for c in range(2)]
            turns += [(qT[:, c, :], [proj[:, t, qo + c * P:qo + (c + 1) * P] for t in range(T)], core.ident) for c in range(4)]
            turn_stage(core, turns)
            score, relu, added = core.event("idx_scores"), core.event("idx_relu"), core.event("idx_added")
            chains = []
            tiles = range(1, T)
            with nc.Block() as block:
                @block.tensor
                def _(pe):
                    i = 0
                    for t in tiles:
                        for h in range(IDX_H):
                            if i >= 8:
                                pe.wait_ge(*relu(i - 7))
                            g = (h % 4) * IDX_D
                            nc.tensor.matmul(core.psum[:, i % 8, 0:(t + 1) * P], qiT[g:g + IDX_D, h // 4, t * P:(t + 1) * P], kiT[g:g + IDX_D, 0:(t + 1) * P], start=True, stop=True).then_inc(score.sem, 1)
                            i += 1

                @block.scalar
                def _(act):
                    i = 0
                    for t in tiles:
                        for h in range(IDX_H):
                            act.wait_ge(*score(i + 1))
                            if i >= 2:
                                act.wait_ge(*added(i - 1))
                            nc.scalar.activation(rel[:, i % 2, 0:(t + 1) * P], core.psum[:, i % 8, 0:(t + 1) * P], ACT.Relu, scale=IDX_D ** -0.5).then_inc(relu.sem, 1)
                            i += 1

                @block.vector
                def _(dve):
                    step = core.step("dve_step", dve, chains)
                    i = 0
                    nc.vector.tensor_copy(sel[:, 0, 0:P], core.mask[:, (T - 1) * P:T * P])
                    for t in tiles:
                        keys = (t + 1) * P
                        acc = sel[:, t, 0:keys]
                        for h in range(IDX_H):
                            dve.wait_ge(*relu(i + 1))
                            base = core.mask[:, (T - 1 - t) * P:(T - 1 - t) * P + keys] if h == 0 else acc
                            ins = nc.vector.scalar_tensor_tensor(out=acc, in0=rel[:, i % 2, 0:keys], scalar=proj[:, t, wio + h:wio + h + 1], in1=base, op0=ALU.mult, op1=ALU.add)
                            ins.then_inc(added.sem, 1)
                            dve.wait_ge(*added(i + 1))
                            i += 1
                        for r in range(TOPK // 8):
                            step(nc.vector.max(best[:], acc))
                            step(nc.vector.match_replace(acc, best[:], acc, -3e38))
                        step(nc.vector.tensor_scalar(acc, acc, -2e38, 8 * NEG, ALU.is_gt, ALU.mult))
                        nc.vector.tensor_tensor(acc[:, t * P:keys], acc[:, t * P:keys], core.mask[:, (T - 1) * P:T * P], ALU.add)
            n = IDX_H * len(tiles)
            score.passed(n); relu.passed(n); added.passed(n)
            close(chains)
        units = []
        for t in range(T):
            keys = (t + 1) * P
            for h in range(H1):
                g, half = h // (H1 // KV2), (h % 2) * HD
                u = len(units)
                units.append((qT[half:half + HD, h // 2, t * P:(t + 1) * P], kT[half:half + HD, g, 0:keys], biasb[:, u % 2, 0:keys],
                              lambda j, g=g: proj[:, j, vo + g * HD:vo + (g + 1) * HD], y[:, t, H1 * VDIM + h * HD:H1 * VDIM + (h + 1) * HD], keys))

        def alibi(step, u):
            t, h = u // H1, u % H1
            keys = (t + 1) * P
            slope = 2.0 ** (-8.0 * (h + 1) / H1) * HD ** 0.5
            step(nc.vector.scalar_tensor_tensor(out=biasb[:, u % 2, 0:keys], in0=dist[:, t, 0:keys], scalar=-slope, in1=sel[:, t, 0:keys], op0=ALU.mult, op1=ALU.add))

        attention_stage(core, units, HD ** -0.5, alibi)


def first_mixer(core, W, x, mod, ring):
    nc = core.nc
    sources = [panel_of(W["w_ada"][0], 0, n * BANK) for n in range(12)]
    widths1 = [min(BANK, IN1 - n * BANK) for n in range(3)]
    sources += [panel_of(W["w_in"][0], 0, n * BANK, widths1[n]) for n in range(3)]
    sources += [panel_of(W["w_o"][0], 0, n * BANK) for n in range(2)]
    panels = Panels(core, ring, sources)
    with ExitStack() as ctx:
        with ExitStack() as inner:
            silu_c = core.sb("silu_c", [P, 2, KD], ctx=inner)
            b_row = core.sb("b_ada_row", [P, 6 * D], ctx=inner)
            gains = core.sb("gains", [P, 4, D], ctx=inner)
            g = [(gains[:, i, :], W[n][0].partition_broadcast(P)) for i, n in enumerate(("g_pre_mix", "g_post_mix", "g_pre_ffn", "g_post_ffn"))]
            load_stage(core, [(silu_c[:, 0, :], W["c_cols"]), (b_row[:], W["b_ada"][0].partition_broadcast(P)),
                              *[(x[:, t, :], W["x"][0, t * P:(t + 1) * P, :]) for t in range(T)], *g], "first_loads")
            modulation_stage(core, panels, mod, silu_c, b_row)
            gains_stage(core, mod, gains)
        part = [mod[:, n * D:(n + 1) * D] for n in range(6)]
        y = core.sb("mix1", [P, T, D], ctx=ctx)
        hT = core.sb("hT1", [P, KD, S], ctx=ctx)
        norm_stage(core, x, part[1], part[0], y, hT)
        with ExitStack() as inner:
            proj = core.sb("proj1", [P, T, IN1], ctx=inner)
            posi = core.sb("pos_i1", [P, T], I32, ctx=inner)
            posf = core.sb("pos_f1", [P, T], ctx=inner)
            cos = core.sb("cos1", [P, T, ROPE // 2], ctx=inner)
            sin = core.sb("sin1", [P, T, ROPE // 2], ctx=inner)
            tmp = core.sb("angle_tmp1", [P, 3, T, ROPE // 2], ctx=inner)
            load_stage(core, [(posi[:], W["pos_cols"])], "positions1")
            angle_stage(core, posi, posf, core.freq1[:], ROPE // 2, cos, sin, [tmp[:, i] for i in range(3)])
            product_stage(core, panels, hT, widths1, lambda n, t, bank: nc.vector.tensor_copy(proj[:, t, n * BANK:n * BANK + bank.shape[1]], bank))
            mla_stages(core, proj, y, hT, cos, sin, W)
            dsa_stages(core, proj, y, hT, posf, W)
        transpose_stage(core, y, hT)
        product_stage(core, panels, hT, [BANK] * 2, lambda n, t, bank: nc.vector.tensor_copy(y[:, t, n * BANK:(n + 1) * BANK], bank))
        panels.close()
        residual_stage(core, x, y, part[2])


def store_stage(core, x, out):
    nc, stored = core.nc, core.event("stored")
    with nc.Block() as block:
        @block.sync
        def _(sp):
            for t in range(T):
                sp.dma_start(out[t * P:(t + 1) * P, :], x[:, t, :]).then_inc(stored.sem, 16)
            sp.wait_ge(*stored(16 * T))
    stored.passed(16 * T)


def setup(nc, W, out, ctx):
    core = Core(nc, ctx, W, out)
    core.psum = ctx.enter_context(nc.psum_tensor("banks", [P, 8, BANK], F32))
    core.ident = core.sb("ident", [P, P])
    core.mask = core.sb("mask", [P, S])
    core.freq1 = core.sb("freq1", [P, ROPE // 2])
    core.stats = core.sb("stats", [P, 8 * T])
    core.junk = core.sb("junk", [P, 1, D])
    x = core.sb("x", [P, T, D])
    with nc.Block() as block:
        @block.vector
        def _(dve):
            nc.vector.memset(core.mask[:, 0:S - P], 0.0)
    load_stage(core, [(core.ident[:], W["ident"]), (core.mask[:, S - P:S], W["causal"]), (core.freq1[:], W["freq1"])], "constants")
    return core, x


CAP = P
BLOCKS = S // CAP
ROWS = S


class Moe:

    def __init__(self, core, ctx):
        sb = lambda name, shape, dtype=F32: core.sb(name, shape, dtype, ctx=ctx)
        self.w1 = sb("w1", [P, KD, 2 * F])
        self.w2 = sb("w2", [P, F // P, D])
        self.b1 = sb("b1", [P, 2 * F])
        self.index = sb("token_of_slot", [P, E * BLOCKS], I32)
        self.slot = sb("slot_of_token", [P, T, TOP_E], U32)
        self.rank = sb("rank_in_expert", [P, T, E])
        self.gate = sb("gate", [P, T, TOP_E])
        self.spread = sb("gate_by_expert", [P, T, E])
        self.flag = sb("more_blocks", [1, 2], I32)
        nc = core.nc
        self.h2 = nc.dram_tensor("h2_rows", [S, D], F32).ap()
        self.slots = nc.dram_tensor("expert_out", [E * CAP, D], F32).ap()
        self.table = nc.dram_tensor("token_table", [E * ROWS, 1], F32).ap()

    def w1_src(self, W, e, j):
        return W["w_mlp1"][0, e].rearrange("(k p) n -> p k n", p=P)[:, 2 * j:2 * j + 2, :]

    def w2_src(self, W, e, j):
        return W["w_mlp2"][0, e].rearrange("(k p) n -> p k n", p=P)[:, 4 * j:4 * j + 4, :]

    def b1_src(self, W, e):
        return W["b_mlp1"][0, e].partition_broadcast(P)


def expert_loads(core, moe):
    return [core.event(f"w1_full{j}") for j in range(4)], [core.event(f"w2_full{j}") for j in range(2)], core.event("b1_full")


def routing_stages(core, W, moe, hT, ctx):
    nc = core.nc
    w1_full, w2_full, b1_full = expert_loads(core, moe)
    sb = lambda name, shape, dtype=F32: core.sb(name, shape, dtype, ctx=ctx)
    wr, br = sb("w_router", [P, KD, E]), sb("b_router", [P, E])
    before, iota, tok = sb("before", [P, P]), sb("iota", [P, ROWS]), sb("tok", [P, T])
    ones, zeros = sb("ones", [P, P]), sb("zeros", [P, P])
    lg, top, topi, topf = sb("logits", [P, T, E]), sb("top", [P, T, 8]), sb("top_i", [P, T, 8], U32), sb("top_f", [P, T, 8])
    low, den, eg = sb("neg_top", [P, T]), sb("gate_sum", [P, T]), sb("gate_exp", [P, T, TOP_E])
    hot, mask = sb("one_hot", [P, T, TOP_E, E]), sb("chosen", [P, T, E])
    place, count = sb("place", [P, T, TOP_E], U32), sb("count", [P, E])
    placef, slotf, rankf, scratch = sb("place_f", [P, T, TOP_E]), sb("slot_f", [P, T, TOP_E]), sb("rank_f", [P, T, TOP_E]), sb("route_tmp", [P, E])
    tokens = sb("table_rows", [P, CAP])
    load_stage(core, [(wr[:], W["w_router"][0].rearrange("(k p) n -> p k n", p=P)), (br[:], W["b_router"][0].partition_broadcast(P)),
                      (before[:], W["before"]), (iota[:], W["iota"]), (tok[:], W["tok"])], "router_loads")
    logits, best, exps, chosen, ranks, slots_ready = (core.event(s) for s in ("logits", "best", "gate_exps", "chosen", "ranks", "slots_ready"))
    cleared, scattered, table_in = core.event("table_cleared"), core.event("table_scattered"), core.event("table_in")
    table_turned, spread_ready = core.event("table_turned"), core.event("zeros_ready")
    chains = []
    with nc.Block() as block:
        @block.sync
        def _(sp):
            for j in range(4):
                sp.dma_start(moe.w1[:, 2 * j:2 * j + 2, :], moe.w1_src(W, 0, j)).then_inc(w1_full[j].sem, 16)
            sp.dma_start(moe.b1[:], moe.b1_src(W, 0)).then_inc(b1_full.sem, 16)
            for j in range(2):
                sp.dma_start(moe.w2[:, 4 * j:4 * j + 4, :], moe.w2_src(W, 0, j)).then_inc(w2_full[j].sem, 16)

        @block.tensor
        def _(pe):
            for t in range(T):
                for k in range(KD):
                    last = nc.tensor.matmul(core.psum[:, t, 0:E], hT[:, k, t * P:(t + 1) * P], wr[:, k, :], start=(k == 0), stop=(k == KD - 1))
                last.then_inc(logits.sem, 1)
            pe.wait_ge(*chosen(1))
            for t in range(T):
                for s in range(t):
                    nc.tensor.matmul(core.psum[:, 4 + t, 0:E], ones[:], mask[:, s, :], start=(s == 0), stop=False)
                nc.tensor.matmul(core.psum[:, 4 + t, 0:E], before[:], mask[:, t, :], start=(t == 0), stop=True)
            for t in range(T):
                last = nc.tensor.matmul(core.psum[:, 0, 0:E], ones[:], mask[:, t, :], start=(t == 0), stop=(t == T - 1))
            last.then_inc(ranks.sem, 1)
            pe.wait_ge(*table_in(16))
            nc.tensor.transpose(core.psum[:, 1, 0:P], tokens[:], core.ident[:]).then_inc(table_turned.sem, 1)

        @block.scalar
        def _(act):
            act.wait_ge(*spread_ready(1))
            act.dma_start(moe.table.rearrange("(p n) o -> p (n o)", p=P), zeros[:]).then_inc(cleared.sem, 16)
            for t in range(T):
                act.wait_ge(*best(t + 1))
                nc.scalar.activation(eg[:, t, :], top[:, t, 0:TOP_E], ACT.Exp, bias=low[:, t:t + 1], accum_out=den[:, t:t + 1]).then_inc(exps.sem, 1)

        @block.vector
        def _(dve):
            step = core.step("dve_step", dve, chains)
            nc.vector.memset(ones[:], 1.0)
            nc.vector.memset(zeros[:], 0.0).then_inc(spread_ready.sem, 1)
            for t in range(T):
                dve.wait_ge(*logits(t + 1))
                step(nc.vector.tensor_tensor(lg[:, t, :], core.psum[:, t, 0:E], br[:], ALU.add))
                step(nc.vector.max(top[:, t, :], lg[:, t, :]))
                step(nc.vector.max_index(topi[:, t, :], top[:, t, :], lg[:, t, :]))
                nc.vector.tensor_scalar(low[:, t:t + 1], top[:, t, 0:1], -1.0, None, ALU.mult).then_inc(best.sem, 1)
                step(nc.vector.tensor_copy(topf[:, t, :], topi[:, t, :]))
                for j in range(TOP_E):
                    step(nc.vector.tensor_scalar(hot[:, t, j, :], iota[:, 0:E], topf[:, t, j:j + 1], None, ALU.is_equal))
                step(nc.vector.tensor_tensor(mask[:, t, :], hot[:, t, 0, :], hot[:, t, 1, :], ALU.add))
                for j in range(2, TOP_E):
                    step(nc.vector.tensor_tensor(mask[:, t, :], mask[:, t, :], hot[:, t, j, :], ALU.add))
            dve.sem_inc(chosen.sem, 1)
            dve.wait_ge(*exps(T))
            step(nc.vector.reciprocal(den[:], den[:]))
            for t in range(T):
                step(nc.vector.tensor_scalar(moe.gate[:, t, :], eg[:, t, :], den[:, t:t + 1], None, ALU.mult))
                step(nc.vector.tensor_scalar(moe.spread[:, t, :], hot[:, t, 0, :], moe.gate[:, t, 0:1], None, ALU.mult))
                for j in range(1, TOP_E):
                    step(nc.vector.scalar_tensor_tensor(out=moe.spread[:, t, :], in0=hot[:, t, j, :], scalar=moe.gate[:, t, j:j + 1], in1=moe.spread[:, t, :], op0=ALU.mult, op1=ALU.add))
            dve.wait_ge(*ranks(1))
            step(nc.vector.tensor_reduce(count[:, 0:1], core.psum[:, 0, 0:E], AX.X, ALU.max))
            step(nc.vector.tensor_scalar(count[:, 1:2], count[:, 0:1], float(CAP), None, ALU.is_gt))
            nc.vector.tensor_copy(moe.flag[0:1, 0:1], count[0:1, 1:2])
            for t in range(T):
                step(nc.vector.tensor_copy(moe.rank[:, t, :], core.psum[:, 4 + t, 0:E]))
                for j in range(TOP_E):
                    step(nc.vector.tensor_tensor(scratch[:], moe.rank[:, t, :], hot[:, t, j, :], ALU.mult))
                    step(nc.vector.tensor_reduce(rankf[:, t, j:j + 1], scratch[:], AX.X, ALU.add))
            step(nc.vector.tensor_copy(slotf[:], topf[:, :, 0:TOP_E]))
            step(nc.vector.scalar_tensor_tensor(out=placef[:], in0=slotf[:], scalar=float(ROWS), in1=rankf[:], op0=ALU.mult, op1=ALU.add))
            step(nc.vector.tensor_copy(place[:], placef[:]))
            dve.sem_inc(slots_ready.sem, 1)
            step(nc.vector.tensor_scalar(placef[:], rankf[:], float(CAP), None, ALU.is_lt))
            step(nc.vector.tensor_tensor(moe.gate[:], moe.gate[:], placef[:], ALU.mult))
            step(nc.vector.tensor_tensor(rankf[:], rankf[:], placef[:], ALU.mult))
            step(nc.vector.scalar_tensor_tensor(out=slotf[:], in0=slotf[:], scalar=float(CAP), in1=rankf[:], op0=ALU.mult, op1=ALU.add))
            step(nc.vector.tensor_copy(moe.slot[:], slotf[:]))
            dve.wait_ge(*table_turned(1))
            nc.vector.tensor_copy(moe.index[:], core.psum[:, 1, 0:P])

        @block.gpsimd
        def _(pool):
            pool.wait_ge(*slots_ready(1))
            pool.wait_ge(*cleared(16))
            for t in range(T):
                for j in range(TOP_E):
                    pool.indirect_dma_start(moe.table, bass.IndirectOffsetOnAxis(place[:, t, j:j + 1], 0), tok[:, t:t + 1], None).then_inc(scattered.sem, 16)
            pool.wait_ge(*scattered(16 * T * TOP_E))
            pool.dma_start(tokens[:], moe.table.rearrange("(r n) o -> r (n o)", n=CAP)).then_inc(table_in.sem, 16)
    for s, n in ((logits, T), (best, T), (exps, T), (chosen, 1), (ranks, 1), (slots_ready, 1), (cleared, 16), (scattered, 16 * T * TOP_E), (table_in, 16), (table_turned, 1), (spread_ready, 1)):
        s.passed(n)
    close(chains)


def experts_stage(core, W, moe):
    nc = core.nc
    w1_full, w2_full, b1_full = expert_loads(core, moe)
    names = ("index_ready", "x_turned", "xT_ready", "w1_used", "hidden_taken", "glu_ready", "sigmoid_ready", "lin_ready", "pre_act", "act_ready",
             "act_turned", "actT_ready", "w2_used", "y_taken")
    index_ready, x_turned, xT_ready, w1_used, hidden_taken, glu_ready, sigmoid_ready, lin_ready, pre_act, act_ready, act_turned, actT_ready, w2_used, y_taken = (core.event(n) for n in names)
    gathered = [core.event(f"x_gathered{q}") for q in range(2)]
    stored = [core.event(f"y_stored{q}") for q in range(2)]
    begun = core.event("gather_begun")
    with ExitStack() as ctx:
        sb = lambda name, shape, dtype=F32: core.sb(name, shape, dtype, ctx=ctx)
        xg, xT = sb("x_rows", [P, 2, D]), sb("xT", [P, 2, KD, P])
        hid, sg, act_sb, actT = sb("hidden", [P, 2 * F]), sb("sigmoid", [P, F]), sb("act", [P, F]), sb("actT", [P, F // P, P])
        y, idx = sb("y", [P, 2, D]), [sb(f"index_now{q}", [P, 1], I32) for q in range(2)]
        glu = hid[:].rearrange("p (n two) -> p two n", two=2)[:, 0, :]
        lin = hid[:].rearrange("p (n two) -> p two n", two=2)[:, 1, :]
        banks = core.psum

        with nc.Block() as block:
            @block.sync
            def _(sp):
                def next_w1(e):
                    for j in range(4):
                        sp.wait_ge(*w1_used(4 * e + j + 1))
                        sp.dma_start(moe.w1[:, 2 * j:2 * j + 2, :], moe.w1_src(W, e + 1, j)).then_inc(w1_full[j].sem, 16)
                    sp.wait_ge(*hidden_taken(e + 1))
                    sp.dma_start(moe.b1[:], moe.b1_src(W, e + 1)).then_inc(b1_full.sem, 16)

                def own_w2(e):
                    for j in range(2):
                        sp.wait_ge(*w2_used(2 * (e - 1) + j + 1))
                        sp.dma_start(moe.w2[:, 4 * j:4 * j + 4, :], moe.w2_src(W, e, j)).then_inc(w2_full[j].sem, 16)

                next_w1(0)
                with sp.Fori(1, E - 1) as e:
                    next_w1(e)
                    own_w2(e)
                own_w2(E - 1)

            @block.gpsimd
            def _(pool):
                def gather(e, q, h, reused):
                    pool.wait_ge(*index_ready(e + 1))
                    if reused:
                        pool.wait_ge(*x_turned(e - 1))
                    pool.sem_inc(begun.sem, 1)
                    pool.indirect_dma_start(xg[:, q, :], None, moe.h2, bass.IndirectOffsetOnAxis(idx[q][:].bitcast(U32), 0)).then_inc(gathered[q].sem, 16)

                gather(0, 0, 0, False)
                gather(1, 1, 0, False)
                with pool.Fori(1, E // 2) as i:
                    gather(2 * i, 0, i, True)
                    gather(2 * i + 1, 1, i, True)

            @block.tensor
            def _(pe):
                def turn_x(e, q, h, banks_used):
                    pe.wait_ge(*gathered[q](16 * (h + 1)))
                    if banks_used is not None:
                        pe.wait_ge(*actT_ready(banks_used))
                    for k in range(KD):
                        last = nc.tensor.transpose(banks[:, 4 + k // 4, (k % 4) * P:(k % 4 + 1) * P], xg[:, q, k * P:(k + 1) * P], core.ident[:])
                    last.then_inc(x_turned.sem, 1)

                def hidden(e, q, first):
                    pe.wait_ge(*xT_ready(e + 1))
                    if not first:
                        pe.wait_ge(*hidden_taken(e))
                    for k in range(KD):
                        if k % 2 == 0:
                            pe.wait_ge(*w1_full[k // 2](16 * (e + 1)))
                        for n in range(4):
                            last = nc.tensor.matmul(banks[:, n, :], xT[:, q, k, :], moe.w1[:, k, n * BANK:(n + 1) * BANK], start=(k == 0), stop=(k == KD - 1))
                        if k % 2:
                            last.then_inc(w1_used.sem, 1)

                def output(e, first):
                    pe.wait_ge(*actT_ready(e + 1))
                    if not first:
                        pe.wait_ge(*y_taken(e))
                    for k in range(F // P):
                        if k % 4 == 0:
                            pe.wait_ge(*w2_full[k // 4](16 * (e + 1)))
                        for n in range(2):
                            last = nc.tensor.matmul(banks[:, 6 + n, :], actT[:, k, :], moe.w2[:, k, n * BANK:(n + 1) * BANK], start=(k == 0), stop=(k == F // P - 1))
                        if k % 4 == 3:
                            last.then_inc(w2_used.sem, 1)

                def turn_act(e, xT_done):
                    pe.wait_ge(*act_ready(e + 1))
                    pe.wait_ge(*xT_ready(xT_done))
                    for k in range(F // P):
                        last = nc.tensor.transpose(banks[:, 4 + k // 4, (k % 4) * P:(k % 4 + 1) * P], act_sb[:, k * P:(k + 1) * P], core.ident[:])
                    last.then_inc(act_turned.sem, 1)

                def body(e, q, h, first=False):
                    hidden(e, q, False)
                    turn_x(e + 1, 1 - q, h + (1 if q else 0), e)
                    output(e - 1, first)
                    turn_act(e, e + 2)

                turn_x(0, 0, 0, None)
                hidden(0, 0, True)
                turn_x(1, 1, 0, None)
                turn_act(0, 2)
                body(1, 1, 0, True)
                body(2, 0, 1)
                with pe.Fori(1, (E - 2) // 2) as i:
                    body(2 * i + 1, 1, i)
                    body(2 * i + 2, 0, i + 1)
                hidden(E - 1, 1, False)
                output(E - 2, False)
                turn_act(E - 1, E)
                output(E - 1, False)

            @block.scalar
            def _(act):
                def copy_x(e, q, w1_done):
                    act.wait_ge(*x_turned(e + 1))
                    if w1_done is not None:
                        act.wait_ge(*w1_used(w1_done))
                    for n in range(2):
                        last = nc.scalar.activation(xT[:, q, 4 * n:4 * n + 4, :], banks[:, 4 + n, :].rearrange("p (k n) -> p k n", k=4), ACT.Copy)
                    last.then_inc(xT_ready.sem, 1)

                def sigmoid(e):
                    act.wait_ge(*glu_ready(e + 1))
                    nc.scalar.activation(sg[:], glu, ACT.Sigmoid, scale=1.702).then_inc(sigmoid_ready.sem, 1)

                def copy_y(e, q, h, reused):
                    act.wait_ge(*w2_used(2 * (e + 1)))
                    if reused:
                        act.wait_ge(*stored[q](16 * h))
                    for n in range(2):
                        last = nc.scalar.activation(y[:, q, n * BANK:(n + 1) * BANK], banks[:, 6 + n, :], ACT.Copy)
                    last.then_inc(y_taken.sem, 1)
                    act.wait_ge(*y_taken(e + 1))
                    act.dma_start(moe.slots[bass.ds(e * CAP, CAP), :], y[:, q, :]).then_inc(stored[q].sem, 16)

                def copy_act(e, reused):
                    act.wait_ge(*act_turned(e + 1))
                    if reused:
                        act.wait_ge(*w2_used(2 * e))
                    for n in range(2):
                        last = nc.scalar.activation(actT[:, 4 * n:4 * n + 4, :], banks[:, 4 + n, :].rearrange("p (k n) -> p k n", k=4), ACT.Copy)
                    last.then_inc(actT_ready.sem, 1)

                copy_x(0, 0, None)
                copy_x(1, 1, None)
                sigmoid(0)
                copy_act(0, False)
                copy_x(2, 0, 4)
                sigmoid(1)
                copy_y(0, 0, 0, False)
                copy_act(1, True)
                copy_x(3, 1, 8)
                sigmoid(2)
                copy_y(1, 1, 0, False)
                copy_act(2, True)

                def body(e, q, h):
                    copy_x(e + 1, 1 - q, 4 * e)
                    sigmoid(e)
                    copy_y(e - 1, 1 - q, h if q else h - 1, True)
                    copy_act(e, True)

                with act.Fori(1, (E - 2) // 2) as i:
                    body(2 * i + 1, 1, i)
                    body(2 * i + 2, 0, i + 1)
                sigmoid(E - 1)
                copy_y(E - 2, 0, (E - 2) // 2, True)
                copy_act(E - 1, True)
                copy_y(E - 1, 1, (E - 1) // 2, True)
                for q in range(2):
                    act.wait_ge(*stored[q](16 * (E // 2)))

            @block.vector
            def _(dve):
                def index(e, q, h, reused):
                    if reused:
                        dve.wait_ge(*gathered[q](16 * h))
                    nc.vector.tensor_scalar(idx[q][:], moe.index[:, bass.ds(e * BLOCKS, 1)], 0, None, ALU.add).then_inc(index_ready.sem, 1)

                def activate(e, reused):
                    dve.wait_ge(*w1_used(4 * (e + 1)))
                    dve.wait_ge(*b1_full(16 * (e + 1)))
                    nc.vector.tensor_tensor(hid[:], banks[:, 0:4, :].rearrange("p b n -> p (b n)"), moe.b1[:], ALU.add).then_inc(hidden_taken.sem, 1)
                    dve.wait_ge(*hidden_taken(e + 1))
                    nc.vector.tensor_scalar(glu, glu, 7.0, None, ALU.min).then_inc(glu_ready.sem, 1)
                    nc.vector.tensor_scalar(lin, lin, 7.0, -7.0, ALU.min, ALU.max).then_inc(lin_ready.sem, 1)
                    dve.wait_ge(*lin_ready(e + 1))
                    dve.wait_ge(*glu_ready(e + 1))
                    if reused:
                        dve.wait_ge(*act_turned(e))
                    nc.vector.scalar_tensor_tensor(out=act_sb[:], in0=lin, scalar=1.0, in1=glu, op0=ALU.add, op1=ALU.mult).then_inc(pre_act.sem, 1)
                    dve.wait_ge(*pre_act(e + 1))
                    dve.wait_ge(*sigmoid_ready(e + 1))
                    nc.vector.tensor_tensor(act_sb[:], act_sb[:], sg[:], ALU.mult).then_inc(act_ready.sem, 1)

                index(0, 0, 0, False)
                index(1, 1, 0, False)
                activate(0, False)
                index(2, 0, 1, True)
                activate(1, True)
                index(3, 1, 1, True)
                activate(2, True)
                with dve.Fori(1, (E - 2) // 2) as i:
                    index(2 * i + 2, 0, i + 1, True)
                    activate(2 * i + 1, True)
                    index(2 * i + 3, 1, i + 1, True)
                    activate(2 * i + 2, True)
                activate(E - 1, True)
    for s in (index_ready, x_turned, xT_ready, hidden_taken, glu_ready, sigmoid_ready, lin_ready, pre_act, act_ready, act_turned, actT_ready, y_taken):
        s.passed(E)
    w1_used.passed(4 * E)
    w2_used.passed(2 * E)
    for s in (*gathered, *stored):
        s.passed(16 * E // 2)
    for s in (*w1_full, *w2_full, b1_full):
        s.passed(16 * E)


def more_blocks_stage(core, W, moe, more):
    nc = core.nc
    names = ("more_weights", "more_index", "more_rows", "more_turned", "more_copied", "more_hidden", "more_act", "more_out", "more_y", "more_sigmoid", "more_gates_made", "more_gates_turned", "more_spread")
    signals = [core.event(n) for n in names]
    signals.remove(core.event("more_rows"))
    rows = core.event("more_rows")
    weights, index, turned, copied, hidden, acted, product, y_ready, sigmoid, gates_made, gates_turned, spread = signals
    banks = core.psum
    with ExitStack() as ctx:
        sb = lambda name, shape, dtype=F32: core.sb(name, shape, dtype, ctx=ctx)
        xg, xT, hid, sg, act_sb = sb("more_x", [P, D]), sb("more_xT", [P, KD, P]), sb("more_hid", [P, 2 * F]), sb("more_sg", [P, F]), sb("more_act", [P, F])
        idx = sb("more_idx", [P, 1], I32)
        iota, gates, gT = sb("more_iota", [P, S]), sb("more_gates", [P, T, P]), sb("more_gatesT", [P, T, P])
        with nc.Block() as block:
            @block.vector
            def _(dve):
                nc.vector.memset(more[:], 0.0)
        load_stage(core, [(iota[:], W["iota"])], "more_loads")
        glu = hid[:].rearrange("p (n two) -> p two n", two=2)[:, 0, :]
        lin = hid[:].rearrange("p (n two) -> p two n", two=2)[:, 1, :]
        flag = nc.values_load(moe.flag[0:1, 0:1], min_val=0, max_val=1)
        with nc.If(flag > 0):
            with nc.Fori(0, E) as e:
                with nc.Block() as block:
                    @block.sync
                    def _(sp):
                        sp.dma_start(moe.w1[:], W["w_mlp1"][0, e].rearrange("(k p) n -> p k n", p=P)).then_inc(weights.sem, 16)
                        sp.dma_start(moe.w2[:], W["w_mlp2"][0, e].rearrange("(k p) n -> p k n", p=P)).then_inc(weights.sem, 16)
                        sp.dma_start(moe.b1[:], moe.b1_src(W, e)).then_inc(weights.sem, 16)
                        sp.wait_ge(*weights(48))
                for b in range(1, BLOCKS):
                    with nc.Block() as block:
                        @block.gpsimd
                        def _(pool):
                            pool.wait_ge(*index(1))
                            pool.indirect_dma_start(xg[:], None, moe.h2, bass.IndirectOffsetOnAxis(idx[:].bitcast(U32), 0)).then_inc(rows.sem, 16)

                        @block.tensor
                        def _(pe):
                            pe.wait_ge(*rows(e * (16 * (BLOCKS - 1)) + 16 * b))
                            for k in range(KD):
                                last = nc.tensor.transpose(banks[:, 4 + k // 4, (k % 4) * P:(k % 4 + 1) * P], xg[:, k * P:(k + 1) * P], core.ident[:])
                            last.then_inc(turned.sem, 1)
                            pe.wait_ge(*copied(1))
                            for k in range(KD):
                                for n in range(4):
                                    last = nc.tensor.matmul(banks[:, n, :], xT[:, k, :], moe.w1[:, k, n * BANK:(n + 1) * BANK], start=(k == 0), stop=(k == KD - 1))
                            last.then_inc(product.sem, 1)
                            pe.wait_ge(*acted(2))
                            for k in range(KD):
                                last = nc.tensor.transpose(banks[:, 4 + k // 4, (k % 4) * P:(k % 4 + 1) * P], act_sb[:, k * P:(k + 1) * P], core.ident[:])
                            last.then_inc(turned.sem, 1)
                            pe.wait_ge(*copied(2))
                            for k in range(KD):
                                for n in range(2):
                                    last = nc.tensor.matmul(banks[:, 6 + n, :], xT[:, k, :], moe.w2[:, k, n * BANK:(n + 1) * BANK], start=(k == 0), stop=(k == KD - 1))
                            last.then_inc(product.sem, 1)
                            pe.wait_ge(*gates_made(1))
                            for t in range(T):
                                last = nc.tensor.transpose(banks[:, 0, t * P:(t + 1) * P], gates[:, t, :], core.ident[:])
                            last.then_inc(turned.sem, 1)
                            pe.wait_ge(*gates_turned(1))
                            pe.wait_ge(*y_ready(1))
                            for t in range(T):
                                if t == 2:
                                    pe.wait_ge(*spread(2))
                                for n in range(2):
                                    last = nc.tensor.matmul(banks[:, 2 + 2 * (t % 2) + n, :], gT[:, t, :], xg[:, n * BANK:(n + 1) * BANK], start=True, stop=True)
                                last.then_inc(product.sem, 1)

                        @block.scalar
                        def _(act):
                            def copy(n, to):
                                act.wait_ge(*turned(n))
                                for j in range(2):
                                    last = nc.scalar.activation(to[:, 4 * j:4 * j + 4, :], banks[:, 4 + j, :].rearrange("p (k n) -> p k n", k=4), ACT.Copy)
                                last.then_inc(copied.sem, 1)

                            copy(1, xT)
                            act.wait_ge(*hidden(2))
                            nc.scalar.activation(sg[:], glu, ACT.Sigmoid, scale=1.702).then_inc(sigmoid.sem, 1)
                            copy(2, xT)
                            act.wait_ge(*product(2))
                            for j in range(2):
                                last = nc.scalar.activation(xg[:, j * BANK:(j + 1) * BANK], banks[:, 6 + j, :], ACT.Copy)
                            last.then_inc(y_ready.sem, 1)
                            act.wait_ge(*turned(3))
                            nc.scalar.activation(gT[:].rearrange("p t n -> p (t n)"), banks[:, 0, :], ACT.Copy).then_inc(gates_turned.sem, 1)

                        @block.vector
                        def _(dve):
                            nc.vector.tensor_scalar(idx[:], moe.index[:, bass.ds(e * BLOCKS + b, 1)], 0, None, ALU.add).then_inc(index.sem, 1)
                            dve.wait_ge(*product(1))
                            nc.vector.tensor_tensor(hid[:], banks[:, 0:4, :].rearrange("p b n -> p (b n)"), moe.b1[:], ALU.add).then_inc(hidden.sem, 1)
                            dve.wait_ge(*hidden(1))
                            nc.vector.tensor_scalar(glu, glu, 7.0, None, ALU.min).then_inc(hidden.sem, 1)
                            nc.vector.tensor_scalar(lin, lin, 7.0, -7.0, ALU.min, ALU.max).then_inc(hidden.sem, 1)
                            dve.wait_ge(*hidden(3))
                            nc.vector.scalar_tensor_tensor(out=act_sb[:], in0=lin, scalar=1.0, in1=glu, op0=ALU.add, op1=ALU.mult).then_inc(acted.sem, 1)
                            dve.wait_ge(*acted(1))
                            dve.wait_ge(*sigmoid(1))
                            nc.vector.tensor_tensor(act_sb[:], act_sb[:], sg[:], ALU.mult).then_inc(acted.sem, 1)
                            for t in range(T):
                                last = nc.vector.tensor_scalar(gates[:, t, :], iota[:, b * CAP:(b + 1) * CAP], moe.rank[:, t, bass.ds(e, 1)], moe.spread[:, t, bass.ds(e, 1)], ALU.is_equal, ALU.mult)
                            last.then_inc(gates_made.sem, 1)
                            for t in range(T):
                                dve.wait_ge(*product(3 + t))
                                bank = 2 + 2 * (t % 2)
                                nc.vector.tensor_tensor(more[:, t, :], more[:, t, :], banks[:, bank:bank + 2, :].rearrange("p b n -> p (b n)"), ALU.add).then_inc(spread.sem, 1)
                    gates_made.passed(1); gates_turned.passed(1); spread.passed(T)
                    index.passed(1); turned.passed(3); copied.passed(2); product.passed(2 + T); acted.passed(2)
                    hidden.passed(3); sigmoid.passed(1); y_ready.passed(1)
                with nc.Block() as block:
                    @block.gpsimd
                    def _(pool):
                        for s in signals:
                            pool.sem_clear(s.sem)
                for s in signals:
                    s.base = 0


def combine_stage(core, W, moe, ffn):
    nc = core.nc
    turned, taken, bias, bias_taken = core.event("turned"), core.event("gates_turned"), core.event("bias_product"), core.event("bias_taken")
    fetched = [core.event(f"row_fetched{i}") for i in range(4)]
    added = core.event("rows_added")
    with ExitStack() as ctx:
        rows = core.sb("slot_rows", [P, 4, D], ctx=ctx)
        b2 = core.sb("b_mlp2", [E, D], ctx=ctx)
        gT = core.sb("gatesT", [E, T, P], ctx=ctx)
        load_stage(core, [(b2[:], W["b_mlp2"][0])], "b_mlp2_load")
        with nc.Block() as block:
            @block.gpsimd
            def _(pool):
                for i in range(T * TOP_E):
                    t, j = i // TOP_E, i % TOP_E
                    if i >= 4:
                        pool.wait_ge(*added(i - 3))
                    pool.indirect_dma_start(rows[:, i % 4, :], None, moe.slots, bass.IndirectOffsetOnAxis(moe.slot[:, t, j:j + 1], 0)).then_inc(fetched[i % 4].sem, 16)

            @block.tensor
            def _(pe):
                for t in range(T):
                    last = nc.tensor.transpose(core.psum[0:E, 0, t * P:(t + 1) * P], moe.spread[:, t, :], core.ident[:])
                last.then_inc(turned.sem, 1)
                pe.wait_ge(*taken(1))
                for t in range(T):
                    if t == 3:
                        pe.wait_ge(*bias_taken(1))
                    for n in range(2):
                        last = nc.tensor.matmul(core.psum[:, 2 + 2 * (t % 3) + n, :], gT[:, t, :], b2[:, n * BANK:(n + 1) * BANK], start=True, stop=True)
                    last.then_inc(bias.sem, 1)

            @block.scalar
            def _(act):
                act.wait_ge(*turned(1))
                nc.scalar.activation(gT[:].rearrange("e t p -> e (t p)"), core.psum[0:E, 0, :], ACT.Copy).then_inc(taken.sem, 1)

            @block.vector
            def _(dve):
                for i in range(T * TOP_E):
                    t, j = i // TOP_E, i % TOP_E
                    dve.wait_ge(*fetched[i % 4](16 * (i // 4 + 1)))
                    if j == 0:
                        dve.wait_ge(*bias(t + 1))
                        b = 2 + 2 * (t % 3)
                        nc.vector.tensor_tensor(ffn[:, t, :], ffn[:, t, :], core.psum[:, b:b + 2, :].rearrange("p b n -> p (b n)"), ALU.add).then_inc(bias_taken.sem, 1)
                        dve.wait_ge(*bias_taken(t + 1))
                    if j:
                        dve.wait_ge(*added(i))
                    nc.vector.scalar_tensor_tensor(out=ffn[:, t, :], in0=rows[:, i % 4, :], scalar=moe.gate[:, t, j:j + 1], in1=ffn[:, t, :], op0=ALU.mult, op1=ALU.add).then_inc(added.sem, 1)
    turned.passed(1); taken.passed(1); bias.passed(T); bias_taken.passed(T); added.passed(T * TOP_E)
    for s in fetched:
        s.passed(16 * T)


def first_ffn(core, W, x, mod):
    part = [mod[:, n * D:(n + 1) * D] for n in range(6)]
    with ExitStack() as ctx:
        moe = Moe(core, ctx)
        with ExitStack() as inner:
            h2 = core.sb("h2", [P, T, D], ctx=inner)
            hT = core.sb("h2T", [P, KD, S], ctx=inner)
            norm_stage(core, x, part[4], part[3], h2, hT, moe.h2)
            routing_stages(core, W, moe, hT, inner)
        experts_stage(core, W, moe)
        with ExitStack() as inner:
            ffn = core.sb("ffn", [P, T, D], ctx=inner)
            more_blocks_stage(core, W, moe, ffn)
            combine_stage(core, W, moe, ffn)
            residual_stage(core, x, ffn, part[5])


GROUPS = 4
OFF2 = [GW * i for i in range(7)] + [6 * GW + AW, 6 * GW + 2 * AW]
LEVELS = 7


def clear_stage(core, signals):
    nc = core.nc
    with nc.Block() as block:
        @block.gpsimd
        def _(pool):
            for s in signals:
                pool.sem_clear(s.sem)
    for s in signals:
        s.base = 0


def lower_bounds_stage(core, raw, lb):
    nc, largest, exps = core.nc, core.event("lb_max"), core.event("lb_exps")
    chains = []
    with ExitStack() as ctx:
        top = core.sb("lb_top", [P, GROUPS], ctx=ctx)
        total = core.sb("lb_total", [P, GROUPS], ctx=ctx)
        with nc.Block() as block:
            @block.vector
            def _(dve):
                step = core.step("dve_step", dve, chains)
                step(nc.vector.tensor_tensor(top[:], raw[:, 0, :], raw[:, 1, :], ALU.max))
                nc.vector.tensor_tensor(raw[:, 0, :], raw[:, 0, :], top[:], ALU.subtract)
                nc.vector.tensor_tensor(raw[:, 1, :], raw[:, 1, :], top[:], ALU.subtract).then_inc(largest.sem, 1)
                dve.wait_ge(*exps(1))
                step(nc.vector.tensor_tensor(total[:], raw[:, 0, :], raw[:, 1, :], ALU.add))
                step(nc.vector.reciprocal(total[:], total[:]))
                nc.vector.tensor_tensor(raw[:, 0, :], raw[:, 0, :], total[:], ALU.mult)
                step(nc.vector.tensor_tensor(raw[:, 1, :], raw[:, 1, :], total[:], ALU.mult))
                nc.vector.tensor_tensor(lb[:, 0, :], raw[:, 0, :], raw[:, 0, :], ALU.subtract)
                step(nc.vector.tensor_tensor(top[:], raw[:, 0, :], raw[:, 1, :], ALU.add))
                nc.vector.tensor_tensor(lb[:, 1, :], top[:], raw[:, 0, :], ALU.subtract)

            @block.scalar
            def _(act):
                act.wait_ge(*largest(1))
                nc.scalar.activation(raw[:], raw[:], ACT.Exp).then_inc(exps.sem, 1)
    largest.passed(1); exps.passed(1)
    close(chains)


def recurrence_stages(core, W, proj, mixed, hT, lb, layer):
    nc = core.nc
    qT, kT = hT[:, 0:GROUPS, :], hT[:, GROUPS:2 * GROUPS, :]
    with ExitStack() as ctx:
        sb = lambda name, shape, dtype=F32: core.sb(name, shape, dtype, ctx=ctx)
        bT, vrev = sb("log_sum", [P, GROUPS, S]), sb("v_reversed", [P, T, GW])
        split, heads2, flip = sb("split", [P, 8, P], I32), sb("heads2", [P, P]), sb("flip", [P, P])
        lbn, omlb, scan = sb("lb_now", [P, GROUPS]), sb("one_less_lb", [P, GROUPS]), sb("scan_mask", [P, S])
        load_stage(core, [(split[:], W["split"].rearrange("p (n m) -> p n m", n=8)), (heads2[:], W["heads2"]), (flip[:], W["flip"])], "recurrence_loads")
        turns = []
        for src, to in ((0, qT), (None, kT)):
            for d in range(2):
                off = OFF2[0] if src == 0 else OFF2[2 + d]
                for pair in range(2):
                    tiles = range(T) if d == 0 else range(T - 1, -1, -1)
                    turns.append((to[:, 2 * d + pair, :], [proj[:, t, off + pair * P:off + (pair + 1) * P] for t in tiles], flip if d else core.ident))
        turn_stage(core, turns)
        capped, exps, f_ready, logs, reversed_, sig = (core.event(n) for n in ("z_capped", "z_exps", "f_ready", "f_logs", "v_flipped", "q_sigmoid"))
        chains = []
        with ExitStack() as inner:
            tmp = core.sb("gate_tmp", [P, GROUPS, S], ctx=inner)
            with nc.Block() as block:
                @block.tensor
                def _(pe):
                    for t in range(T):
                        last = nc.tensor.matmul(core.psum[:, t, 0:GW], flip[:], proj[:, T - 1 - t, OFF2[1]:OFF2[2]], start=True, stop=True)
                    last.then_inc(reversed_.sem, 1)

                @block.scalar
                def _(act):
                    act.wait_ge(*capped(1))
                    nc.scalar.activation(tmp[:], kT, ACT.Exp, scale=-1.0).then_inc(exps.sem, 1)
                    act.wait_ge(*reversed_(1))
                    for t in range(T):
                        nc.scalar.activation(vrev[:, t, :], core.psum[:, t, 0:GW], ACT.Copy)
                    act.wait_ge(*f_ready(1))
                    nc.scalar.activation(bT[:], tmp[:], ACT.Ln).then_inc(logs.sem, 1)
                    act.wait_ge(*logs(1))
                    nc.scalar.activation(tmp[:], qT, ACT.Sigmoid).then_inc(sig.sem, 1)

                @block.vector
                def _(dve):
                    step = core.step("dve_step", dve, chains)
                    nc.vector.tensor_scalar(kT, kT, -60.0, None, ALU.max).then_inc(capped.sem, 1)
                    nc.vector.tensor_scalar(lbn[:], lb[:, bass.ds(layer, 1), :].rearrange("p l g -> p (l g)"), 0.0, None, ALU.add)
                    step(nc.vector.memset(scan[:], 1.0))
                    nc.vector.memset(scan[:].rearrange("p (t n) -> p t n", t=T)[:, :, 0:1], 0.0)
                    step(nc.vector.tensor_scalar(omlb[:], lbn[:], -1.0, 1.0, ALU.mult, ALU.add))
                    dve.wait_ge(*exps(1))
                    step(nc.vector.tensor_scalar(tmp[:], tmp[:], 1.0, None, ALU.add))
                    step(nc.vector.reciprocal(tmp[:], tmp[:]))
                    for g in range(GROUPS):
                        last = nc.vector.tensor_scalar(tmp[:, g, :], tmp[:, g, :], omlb[:, g:g + 1], lbn[:, g:g + 1], ALU.mult, ALU.add)
                    step(last)
                    step(nc.vector.tensor_scalar(kT, tmp[:], -1.0, 1.0, ALU.mult, ALU.add))
                    nc.vector.tensor_scalar(tmp[:], tmp[:], 1.1e-19, None, ALU.max).then_inc(f_ready.sem, 1)
                    dve.wait_ge(*logs(1))
                    for g in range(GROUPS):
                        nc.vector.tensor_tensor_scan(bT[:, g, :], scan[:], bT[:, g, :], 0.0, ALU.mult, ALU.add)
                    dve.wait_ge(*sig(1))
                    nc.vector.tensor_tensor(qT, qT, tmp[:], ALU.mult)
        for s in (capped, exps, f_ready, logs, reversed_, sig):
            s.passed(1)
        close(chains)
        names = ("split_diff", "split_exp", "split_factor", "split_scores", "split_taken", "cross_exps", "cross_keys", "cross_turned", "cross_rows",
                 "state_parts", "states", "group_out", "group_taken")
        diff, exped, factor, scored, level_taken, cross_exps, cross_keys, cross_turned, cross_rows, parts, states, out_ready, out_taken = (core.event(n) for n in names)
        o = [sb(f"rec_out{d}", [P, T, GW]) for d in range(2)]
        ex, m = sb("split_exps", [P, 2, S]), sb("split_factors", [P, 2, S])
        acc = sb("split_sums", [P, 2 * T * P])
        qx, kx, kxr = sb("cross_q", [P, S]), sb("cross_k", [P, S]), sb("cross_k_rows", [P, S])
        eb, st = sb("tile_decay", [P, T]), sb("state", [P, T, P])
        chains = []
        banks = core.psum
        per = LEVELS + 1

        def halves(ap, n):
            v = ap.rearrange("p (b two h) -> p b two h", two=2, h=1 << n)
            return v[:, :, 0, :], v[:, :, 1, :]

        with nc.Block() as block:
            @block.vector
            def _(dve):
                step = core.step("dve_step", dve, chains)
                for g in range(GROUPS):
                    b, q, k = bT[:, g, :], qT[:, g, :], kT[:, g, :]

                    def exponents(n):
                        i = g * LEVELS + n
                        if i >= 2:
                            dve.wait_ge(*exped(i - 1))
                        b1, b2 = halves(b, n)
                        e1, e2 = halves(ex[:, i % 2, :], n)
                        r = b1[:, :, (1 << n) - 1:1 << n].broadcast_to(b1.shape)
                        if i >= 2:
                            dve.wait_ge(*factor(i - 1))
                        nc.vector.tensor_tensor(e1, r, b1, ALU.subtract)
                        nc.vector.tensor_tensor(e2, b2, r, ALU.subtract).then_inc(diff.sem, 1)

                    def factors(n):
                        i = g * LEVELS + n
                        e1, e2 = halves(ex[:, i % 2, :], n)
                        m1, m2 = halves(m[:, i % 2, :], n)
                        dve.wait_ge(*exped(i + 1))
                        if i >= 2:
                            dve.wait_ge(*scored(g * per + n - 1 if n >= 2 else (g - 1) * per + LEVELS + n - 1))
                        nc.vector.tensor_tensor(m1, e1, halves(k, n)[0], ALU.mult)
                        nc.vector.tensor_tensor(m2, e2, halves(q, n)[1], ALU.mult).then_inc(factor.sem, 1)

                    def take(n):
                        j = g * per + n
                        if j:
                            dve.wait_ge(*level_taken(j))
                        dve.wait_ge(*scored(j + 1))
                        bank = 2 * (j % 2)
                        nc.vector.copy_predicated(acc[:].rearrange("p (a s) -> p a s", s=P), split[:, n, :].unsqueeze(1).broadcast_to([P, 2 * T, P]),
                                                  banks[:, bank:bank + 2, :].rearrange("p b (t s) -> p (b t) s", s=P)).then_inc(level_taken.sem, 1)

                    if g:
                        dve.wait_ge(*out_ready(g))
                    step(nc.vector.memset(acc[:], 0.0))
                    exponents(0)
                    for n in range(LEVELS):
                        if n + 1 < LEVELS:
                            exponents(n + 1)
                        factors(n)
                        if n:
                            take(n - 1)
                    bt = b.rearrange("p (t s) -> p t s", t=T)
                    last_b = bt[:, :, P - 1:P]
                    step(nc.vector.tensor_tensor(kx[:].rearrange("p (t s) -> p t s", t=T), last_b.broadcast_to([P, T, P]), bt, ALU.subtract))
                    dve.sem_inc(cross_exps.sem, 1)
                    take(LEVELS - 1)
                    take(LEVELS)
                    dve.wait_ge(*cross_exps(4 * g + 4))
                    nc.vector.tensor_tensor(qx[:], qx[:], q, ALU.mult).then_inc(cross_keys.sem, 1)
                    nc.vector.tensor_tensor(kx[:], kx[:], k, ALU.mult).then_inc(cross_keys.sem, 1)
                    dve.wait_ge(*parts(g + 1))
                    step(nc.vector.tensor_tensor(st[:, 1:T, :], banks[:, 5, 0:(T - 1) * P].rearrange("p (t n) -> p t n", n=P), heads2[:].unsqueeze(1).broadcast_to([P, T - 1, P]), ALU.mult))
                    for t in range(2, T):
                        step(nc.vector.scalar_tensor_tensor(out=st[:, t, :], in0=st[:, t - 1, :], scalar=eb[:, t - 1:t], in1=st[:, t, :], op0=ALU.mult, op1=ALU.add))
                    dve.sem_inc(states.sem, 1)

            @block.scalar
            def _(act):
                for g in range(GROUPS):
                    for n in range(LEVELS):
                        i = g * LEVELS + n
                        act.wait_ge(*diff(i + 1))
                        nc.scalar.activation(ex[:, i % 2, :], ex[:, i % 2, :], ACT.Exp).then_inc(exped.sem, 1)
                    act.wait_ge(*cross_exps(4 * g + 1))
                    nc.scalar.activation(kx[:], kx[:], ACT.Exp).then_inc(cross_exps.sem, 1)
                    if g:
                        act.wait_ge(*out_ready(g))
                        act.wait_ge(*states(g))
                    nc.scalar.activation(qx[:], bT[:, g, :], ACT.Exp).then_inc(cross_exps.sem, 1)
                    nc.scalar.activation(eb[:], bT[:, g, :].rearrange("p (t s) -> p t s", t=T)[:, :, P - 1], ACT.Exp).then_inc(cross_exps.sem, 1)
                    act.wait_ge(*cross_turned(g + 1))
                    nc.scalar.activation(kxr[:], banks[:, 4, :], ACT.Copy).then_inc(cross_rows.sem, 1)
                    act.wait_ge(*out_ready(g + 1))
                    d, pair = g // 2, g % 2
                    nc.scalar.activation(o[d][:, :, pair * P:(pair + 1) * P], banks[:, 6 + g % 2, :].rearrange("p (t n) -> p t n", t=T), ACT.Copy).then_inc(out_taken.sem, 1)

            @block.tensor
            def _(pe):
                for g in range(GROUPS):
                    d, pair = g // 2, g % 2
                    v = lambda t, a, b: (vrev[:, t, pair * P + a:pair * P + b] if d else proj[:, t, OFF2[1] + pair * P + a:OFF2[1] + pair * P + b])

                    def scores(n):
                        i, j = g * LEVELS + n, g * per + n
                        if n < LEVELS:
                            pe.wait_ge(*factor(i + 1))
                        if j >= 2:
                            pe.wait_ge(*level_taken(j - 1))
                        for h in range(2):
                            for t in range(T):
                                cols, rows = slice(t * P, (t + 1) * P), slice(h * HD, (h + 1) * HD)
                                a, b = (m[rows, i % 2, cols], m[rows, i % 2, cols]) if n < LEVELS else (kT[rows, g, cols], qT[rows, g, cols])
                                last = nc.tensor.matmul(banks[:, 2 * (j % 2) + h, cols], a, b, start=True, stop=True)
                        last.then_inc(scored.sem, 1)

                    for n in range(per):
                        scores(n)
                    pe.wait_ge(*cross_keys(2 * g + 2))
                    for t in range(T):
                        last = nc.tensor.transpose(banks[:, 4, t * P:(t + 1) * P], kx[:, t * P:(t + 1) * P], core.ident[:])
                    last.then_inc(cross_turned.sem, 1)
                    pe.wait_ge(*cross_rows(g + 1))
                    for t in range(T - 1):
                        last = nc.tensor.matmul(banks[:, 5, t * P:(t + 1) * P], kxr[:, t * P:(t + 1) * P], v(t, 0, P), start=True, stop=True)
                    last.then_inc(parts.sem, 1)
                    if g >= 2:
                        pe.wait_ge(*out_taken(g - 1))
                    pe.wait_ge(*states(g + 1))
                    for t in range(T):
                        out = banks[:, 6 + g % 2, t * P:(t + 1) * P]
                        if t:
                            nc.tensor.matmul(out, qx[:, t * P:(t + 1) * P], st[:, t, :], start=True, stop=False, skip_group_check=True)
                        for h in range(2):
                            pe.wait_ge(*level_taken((g + 1) * per))
                            last = nc.tensor.matmul(out[:, h * HD:(h + 1) * HD], acc[:, (h * T + t) * P:(h * T + t + 1) * P], v(t, h * HD, (h + 1) * HD), start=(t == 0), stop=True, skip_group_check=True)
                    last.then_inc(out_ready.sem, 1)
        diff.passed(GROUPS * LEVELS); exped.passed(GROUPS * LEVELS); factor.passed(GROUPS * LEVELS)
        scored.passed(GROUPS * per); level_taken.passed(GROUPS * per)
        cross_exps.passed(4 * GROUPS); cross_keys.passed(2 * GROUPS)
        for s in (cross_turned, cross_rows, parts, states, out_ready, out_taken):
            s.passed(GROUPS)
        close(chains)
        summed, spread, root, gated = (core.event(n) for n in ("directions", "mean_square", "root", "g_sigmoid"))
        chains = []
        with ExitStack() as inner:
            sq = bT[:, 0:2, :].rearrange("p g s -> p (g s)").rearrange("p (a d) -> p a d", d=HD)
            gs = bT[:, 2:4, :].rearrange("p g s -> p (g s)").rearrange("p (t n) -> p t n", t=T)
            ms = core.sb("rec_ms", [P, 3, T * 4], ctx=inner)
            of = o[0][:].rearrange("p t n -> p (t n)")
            with nc.Block() as block:
                @block.tensor
                def _(pe):
                    for t in range(T):
                        last = nc.tensor.matmul(banks[:, t, 0:GW], flip[:], o[1][:, T - 1 - t, :], start=True, stop=True)
                    last.then_inc(summed.sem, 1)

                @block.scalar
                def _(act):
                    nc.scalar.activation(gs, proj[:, :, OFF2[4]:OFF2[5]], ACT.Sigmoid).then_inc(gated.sem, 1)
                    act.wait_ge(*spread(1))
                    nc.scalar.activation(ms[:, 1, :], ms[:, 0, :], ACT.Sqrt).then_inc(root.sem, 1)

                @block.vector
                def _(dve):
                    step = core.step("dve_step", dve, chains)
                    dve.wait_ge(*gated(1))
                    nc.vector.tensor_tensor(gs, gs, proj[:, :, OFF2[4]:OFF2[5]], ALU.mult)
                    dve.wait_ge(*summed(1))
                    step(nc.vector.tensor_tensor(o[0][:], o[0][:], banks[:, 0:T, 0:GW], ALU.add))
                    step(nc.vector.tensor_tensor(sq.rearrange("p a d -> p (a d)"), of, of, ALU.mult))
                    step(nc.vector.tensor_reduce(ms[:, 0, :], sq, AX.X, ALU.add))
                    nc.vector.tensor_scalar(ms[:, 0, :], ms[:, 0, :], 1.0 / HD, EPS, ALU.mult, ALU.add).then_inc(spread.sem, 1)
                    dve.wait_ge(*root(1))
                    step(nc.vector.reciprocal(ms[:, 2, :], ms[:, 1, :]))
                    step(nc.vector.tensor_tensor(sq, of.rearrange("p (a d) -> p a d", d=HD), ms[:, 2, :].unsqueeze(2).broadcast_to([P, T * 4, HD]), ALU.mult))
                    nc.vector.tensor_tensor(mixed[:, :, 0:GW], sq.rearrange("p (t h) d -> p t (h d)", t=T), gs, ALU.mult)
        for s in (summed, spread, root, gated):
            s.passed(1)
        close(chains)


def fourier_stages(core, W, proj, mixed, hT):
    nc = core.nc
    uT = hT[:, 0:2, :]
    channels, taken, out_ready = core.event("dft_channels"), core.event("dft_taken"), core.event("dft_out")
    with ExitStack() as ctx:
        cos, sin = core.sb("dft_cos", [P, T, S], ctx=ctx), core.sb("dft_sin", [P, T, S], ctx=ctx)
        ch, ab = core.sb("dft_ch", [P, 2 * P], ctx=ctx), core.sb("dft_ab", [P, T, 2, 2, P], ctx=ctx)
        load_stage(core, [(cos[:], W["dft_cos"].rearrange("p (t n) -> p t n", t=T)), (sin[:], W["dft_sin"].rearrange("p (t n) -> p t n", t=T)), (ch[:], W["dft_ch"])], "dft_loads")
        turn_stage(core, [(uT[:, c, :], [proj[:, t, OFF2[5] + c * P:OFF2[5] + (c + 1) * P] for t in range(T)], core.ident) for c in range(2)])
        with nc.Block() as block:
            @block.tensor
            def _(pe):
                for t in range(T):
                    for c in range(2):
                        last = nc.tensor.matmul(core.psum[:, t, c * 2 * P:(c + 1) * 2 * P], uT[:, c, t * P:(t + 1) * P], ch[:], start=True, stop=True)
                    last.then_inc(channels.sem, 1)
                pe.wait_ge(*taken(T))
                for t in range(T):
                    for s in range(T):
                        for i, table in enumerate((cos, sin)):
                            last = nc.tensor.matmul(core.psum[:, 4 + t, 0:2 * P], table[:, s, t * P:(t + 1) * P], ab[:, s, :, i, :], start=(s == 0 and i == 0), stop=(s == T - 1 and i == 1))
                    last.then_inc(out_ready.sem, 1)

            @block.scalar
            def _(act):
                for t in range(T):
                    act.wait_ge(*channels(t + 1))
                    nc.scalar.activation(ab[:, t].rearrange("p c i n -> p (c i n)"), core.psum[:, t, :], ACT.Copy).then_inc(taken.sem, 1)

            @block.vector
            def _(dve):
                for t in range(T):
                    dve.wait_ge(*out_ready(t + 1))
                    nc.vector.tensor_copy(mixed[:, t, GW:2 * GW], core.psum[:, 4 + t, 0:2 * P])
    channels.passed(T); taken.passed(T); out_ready.passed(T)


def dilated_stages(core, W, proj, mixed, hT, cos, sin):
    nc = core.nc
    qT, kT = hT[:, 0:4, :], hT[:, 4:8, :]
    qo, ko, vo = OFF2[6], OFF2[7], OFF2[8]
    with ExitStack() as ctx:
        pairs = core.sb("pairs", [P, T, S], ctx=ctx)
        load_stage(core, [(pairs[:], W["pairs"].rearrange("p (t n) -> p t n", t=T))], "pairs_load")
        chains = []
        with ExitStack() as inner:
            tmp = core.sb("rotate_tmp2", [P, 4, 2 * H2, HD // 2], ctx=inner)
            with nc.Block() as block:
                @block.vector
                def _(dve):
                    step = core.step("dve_step", dve, chains)
                    for t in range(T):
                        qk = proj[:, t, qo:vo].rearrange("p (h d) -> p h d", d=HD)
                        rotate(nc, step, qk, qk, cos[:, t, :], sin[:, t, :], tmp, 2 * H2, HD // 2)
            close(chains)
        turn_stage(core, [(to[:, c, :], [proj[:, t, off + c * P:off + (c + 1) * P] for t in range(T)], core.ident) for off, to in ((qo, qT), (ko, kT)) for c in range(4)])
        units = []
        for t in range(T):
            for h in range(H2):
                half = (h % 2) * HD
                units.append((qT[half:half + HD, h // 2, t * P:(t + 1) * P], kT[half:half + HD, h // 2, :], pairs[:, t, :],
                              lambda j, h=h: proj[:, j, vo + h * HD:vo + (h + 1) * HD], mixed[:, t, 2 * GW + h * HD:2 * GW + (h + 1) * HD], S))
        attention_stage(core, units, HD ** -0.5)


def ffn_stages(core, panels, hT, uT, x):
    nc = core.nc
    product, relus, squared, done = core.event("product"), core.event("relus"), core.event("product_taken"), core.event("down_product")
    first = panels.used
    ups = DFF // BANK
    chunks = 4 * ups
    panels.used_at += [product(4 * (n + 1)) for n in range(ups)]
    with ExitStack() as ctx:
        relu = core.sb("relu", [P, 4, S], ctx=ctx)
        with nc.Block() as block:
            @block.sync
            def _(sp):
                panels.load_ahead(sp, ups)

            @block.tensor
            def _(pe):
                for f in range(chunks):
                    if f % 4 == 0:
                        panels.arrived(pe, first + f // 4)
                    w = panels.place(first + f // 4)
                    if f >= 8:
                        pe.wait_ge(*relus(f - 7))
                    for k in range(KD):
                        last = nc.tensor.matmul(core.psum[:, f % 8, :], w[:, k, (f % 4) * P:(f % 4 + 1) * P], hT[:, k, :], start=(k == 0), stop=(k == KD - 1))
                    last.then_inc(product.sem, 1)

            @block.scalar
            def _(act):
                for f in range(chunks):
                    act.wait_ge(*product(f + 1))
                    if f >= 4:
                        act.wait_ge(*squared(f - 3))
                    nc.scalar.activation(relu[:, f % 4, :], core.psum[:, f % 8, :], ACT.Relu).then_inc(relus.sem, 1)

            @block.vector
            def _(dve):
                for f in range(chunks):
                    dve.wait_ge(*relus(f + 1))
                    nc.vector.tensor_tensor(uT[:, f, :], relu[:, f % 4, :], relu[:, f % 4, :], ALU.mult).then_inc(squared.sem, 1)
    panels.used += ups
    product.passed(chunks); relus.passed(chunks); squared.passed(chunks)
    first = panels.used
    groups = DFF // D
    panels.used_at += [product(n + 1) for n in range(2 * groups)]
    with nc.Block() as block:
        @block.sync
        def _(sp):
            panels.load_ahead(sp, 2 * groups)

        @block.tensor
        def _(pe):
            for n in range(2):
                for r in range(groups):
                    p = n * groups + r
                    panels.arrived(pe, first + p)
                    w = panels.place(first + p)
                    for t in range(T):
                        for k in range(KD):
                            last = nc.tensor.matmul(core.psum[:, 4 * n + t, :], uT[:, r * KD + k, t * P:(t + 1) * P], w[:, k, :], start=(r == 0 and k == 0), stop=(r == groups - 1 and k == KD - 1))
                    last.then_inc(product.sem, 1)

        @block.vector
        def _(dve):
            for n in range(2):
                dve.wait_ge(*product((n + 1) * groups))
                for t in range(T):
                    cols = slice(n * BANK, (n + 1) * BANK)
                    nc.vector.tensor_tensor(x[:, t, cols], x[:, t, cols], core.psum[:, 4 * n + t, :], ALU.add)
    panels.used += 2 * groups
    product.passed(2 * groups)


def second_block(core, W, x, ring, out):
    nc = core.nc
    half = HD // 2
    with ExitStack() as ctx:
        sb = lambda name, shape, dtype=F32: core.sb(name, shape, dtype, ctx=ctx)
        hT, mixed, gains = sb("hT2", [P, KD, S]), sb("mixed", [P, T, D]), sb("gains2", [P, 2, D])
        cos, sin, lb = sb("cos2", [P, T, half]), sb("sin2", [P, T, half]), sb("lower_bounds", [P, L2, GROUPS])
        with ExitStack() as inner:
            posi, posf = core.sb("pos_i2", [P, T], I32, ctx=inner), core.sb("pos_f2", [P, T], ctx=inner)
            freq, tmp, raw = core.sb("freq2", [P, half], ctx=inner), core.sb("angle_tmp2", [P, 3, T, half], ctx=inner), core.sb("lb_raw", [P, L2, GROUPS], ctx=inner)
            load_stage(core, [(posi[:], W["pos2_cols"]), (freq[:], W["freq2"]), (raw[:], W["lb_cols"])], "second_loads")
            angle_stage(core, posi, posf, freq[:], half, cos, sin, [tmp[:, i] for i in range(3)])
            lower_bounds_stage(core, raw, lb)
        pooled = ("table_scattered", "table_in", "x_gathered0", "x_gathered1", "more_rows", "row_fetched0", "row_fetched1", "row_fetched2", "row_fetched3")
        clear_stage(core, [s for n, s in core.events.items() if s.base and n not in pooled])
        with nc.Fori(0, L2) as layer:
            w_in, w_out, w_up, w_down = (W[n][layer] for n in ("w_in_2", "w_out_2", "w_up_2", "w_down_2"))
            sources = [panel_of(w_in, 0, n * BANK) for n in range(IN2 // BANK)]
            sources += [panel_of(w_out, 0, n * BANK) for n in range(2)]
            sources += [panel_of(w_up, 0, n * BANK) for n in range(DFF // BANK)]
            sources += [panel_of(w_down, r, n * BANK) for n in range(2) for r in range(DFF // D)]
            panels = Panels(core, ring, sources)
            load_stage(core, [(gains[:, 0, :], W["attn_norm_w_2"][layer].partition_broadcast(P)), (gains[:, 1, :], W["mlp_norm_w_2"][layer].partition_broadcast(P))], "layer_gains")
            norm_stage(core, x, gains[:, 0, :], None, mixed, hT)
            with ExitStack() as inner:
                proj = core.sb("proj2", [P, T, IN2], ctx=inner)
                product_stage(core, panels, hT, [BANK] * (IN2 // BANK), lambda n, t, bank: nc.vector.tensor_copy(proj[:, t, n * BANK:(n + 1) * BANK], bank))
                recurrence_stages(core, W, proj, mixed, hT, lb, layer)
                fourier_stages(core, W, proj, mixed, hT)
                dilated_stages(core, W, proj, mixed, hT, cos, sin)
            transpose_stage(core, mixed, hT)

            def add(n, t, bank):
                cols = slice(n * BANK, (n + 1) * BANK)
                return nc.vector.tensor_tensor(x[:, t, cols], x[:, t, cols], bank, ALU.add)

            product_stage(core, panels, hT, [BANK] * 2, add)
            norm_stage(core, x, gains[:, 1, :], None, mixed, hT)
            with ExitStack() as inner:
                uT = core.sb("uT", [P, DFF // P, S], ctx=inner)
                ffn_stages(core, panels, hT, uT, x)
            panels.close()
            clear_stage(core, [s for s in core.events.values() if s.base])
        load_stage(core, [(gains[:, 0, :], W["final_norm_w_2"].partition_broadcast(P))], "final_gain")
        norm_stage(core, x, gains[:, 0, :], None, mixed, None, out)


def two_blocks_kernel(nc, W, out):
    with ExitStack() as ctx:
        core, x = setup(nc, W, out, ctx)
        with ExitStack() as first:
            mod = core.sb("mod", [P, 6 * D], ctx=first)
            with ExitStack() as inner:
                ring = core.sb("panels1", [P, PANELS, PW], ctx=inner)
                first_mixer(core, W, x, mod, ring)
            first_ffn(core, W, x, mod)
        ring = core.sb("panels2", [P, PANELS, PW])
        second_block(core, W, x, ring, out)


_AS_THEY_ARE = ["x", "positions", "b_ada", "w_ada", "g_pre_mix", "g_post_mix", "g_pre_ffn", "g_post_ffn", "w_in", "g_q_a", "g_kv_a",
                "w_q_b", "w_kv_b", "w_o", "w_router", "b_router", "w_mlp1", "b_mlp1", "w_mlp2", "b_mlp2", "attn_norm_w_2", "w_in_2",
                "w_out_2", "mlp_norm_w_2", "w_up_2", "w_down_2", "final_norm_w_2"]


def kernel(**inputs):
    import concourse.bacc as _bacc
    from concourse.bass_utils import run_bass_kernel_spmd as _run

    def columns(a):
        return np.ascontiguousarray(np.asarray(a).reshape(-1, P).T)

    arrays = {n: np.ascontiguousarray(inputs[n]) for n in _AS_THEY_ARE}
    arrays["c_cols"] = columns(inputs["c"])
    arrays["pos_cols"] = columns(inputs["positions"])
    arrays["pos2_cols"] = columns(inputs["positions_2"])
    arrays["lb_cols"] = columns(inputs["hgrn_lower_bounds_2"]).reshape(P, L2, GROUPS)
    arrays.update(shape_constants())
    nc = _bacc.Bacc("TRN2", target_bir_lowering=False, num_devices=1)
    W = {n: nc.dram_tensor(f"in_{n}", a.shape, mybir.dt.from_np(a.dtype), kind="ExternalInput").ap() for n, a in arrays.items()}
    out = nc.dram_tensor("out", (S, D), F32, kind="ExternalOutput").ap()
    two_blocks_kernel(nc, W, out)
    r = _run(nc, [{f"in_{n}": a for n, a in arrays.items()}], core_ids=[0])
    return r.results[0]["out"].reshape(1, S, D)
```

```python
from contextlib import ExitStack

import numpy as np

import concourse.bass as bass
from concourse import mybir

ALU = mybir.AluOpType
ACT = mybir.ActivationFunctionType
AX = mybir.AxisListType
F32 = mybir.dt.float32
I32 = mybir.dt.int32
U32 = mybir.dt.uint32
F32R = mybir.dt.float32r

P = 128
D = 1024
KD = D // P
S = 512
T = S // P
BANK = 512
NEG = -1e30
EPS = 1e-6

H1 = 8
Q_RANK, KV_RANK, ROPE = 256, 128, 32
NOPE, VDIM = 64, 64
QK1 = NOPE + ROPE
HD = 64
KV2 = 2
IDX_H, IDX_D = 8, 32
TOPK = 128
E = 32
TOP_E = 4
F = 1024
SPLITS1 = (Q_RANK, KV_RANK, ROPE, H1 * HD, KV2 * HD, KV2 * HD, IDX_H * IDX_D, IDX_D, IDX_H)
OFF1 = [sum(SPLITS1[:i]) for i in range(len(SPLITS1) + 1)]
IN1 = OFF1[-1]

L2 = 2
GW = 256
AW = 512
IN2 = 5 * GW + GW + 3 * AW
H2 = AW // HD
DFF = 4 * D
FFN_GROUPS = DFF // 512
PATTERNS = ((128, 1), (512, 4), (2048, 16))


PIECE = 1024
PIECES = KD * BANK // PIECE
RAW = 6
PARTS = 7
ADA_PARTS, MIX_PARTS = 5, 5


def shape_constants():
    f32 = np.float32
    i = np.arange(P)
    c = {}
    c["ident"] = np.eye(P, dtype=f32)
    c["flip"] = np.eye(P, dtype=f32)[::-1].copy()
    c["causal"] = np.where(i[None, :] <= i[:, None], 0.0, NEG).astype(f32)
    c["before"] = (i[:, None] < i[None, :]).astype(f32)
    c["iota"] = np.tile(np.arange(S, dtype=f32)[None, :], (P, 1))
    c["tok"] = (i[:, None] + P * np.arange(T)[None, :]).astype(f32)
    half = ROPE // 2
    c["freq1"] = np.tile((f32(10000.0) ** (-np.arange(half, dtype=f32) / f32(half))).astype(f32)[None, :], (P, 1))
    half = HD // 2
    c["freq2"] = np.tile((f32(10000.0) ** (-np.arange(0, HD, 2, dtype=f32) / f32(HD))).astype(f32)[None, :], (P, 1))
    q = np.arange(S)
    count = np.zeros((S, S))
    for window, dil in PATTERNS:
        r = window // (2 * dil)
        same = (q[:, None] % dil) == (q[None, :] % dil)
        count += same & (np.abs(q[:, None] // dil - q[None, :] // dil) <= r)
    scale = HD ** -0.5
    table = np.where(count > 0, np.log(np.maximum(count, 1)), NEG) / scale
    c["pairs"] = table.astype(f32).reshape(T, P, S).transpose(1, 0, 2).reshape(P, T * S).copy()
    a = 2 * np.pi * ((q[:, None] * q[None, :]) % S) / S
    c["dft_cos"] = (np.cos(a) / np.sqrt(S)).astype(f32).reshape(T, P, S).transpose(1, 0, 2).reshape(P, T * S).copy()
    c["dft_sin"] = (np.sin(a) / np.sqrt(S)).astype(f32).reshape(T, P, S).transpose(1, 0, 2).reshape(P, T * S).copy()
    h = np.arange(HD)
    a = 2 * np.pi * ((h[:, None] * h[None, :]) % HD) / HD
    ch = np.zeros((P, 2, P))
    for g in range(2):
        s = slice(g * HD, (g + 1) * HD)
        ch[s, 0, s] = np.cos(a) / np.sqrt(HD)
        ch[s, 1, s] = -np.sin(a) / np.sqrt(HD)
    c["dft_ch"] = ch.astype(f32).reshape(P, 2 * P)
    lv = np.zeros((P, 8, P), np.int32)
    for n in range(7):
        lv[:, n, :] = ((i[:, None] >> (n + 1)) == (i[None, :] >> (n + 1))) & (((i[:, None] >> n) & 1) == 0) & (((i[None, :] >> n) & 1) == 1)
    lv[:, 7, :] = np.eye(P)
    c["split"] = lv.reshape(P, 8 * P)
    c["heads2"] = np.kron(np.eye(2), np.ones((HD, HD))).astype(f32)
    return c


class Signal:

    def __init__(self, sem):
        self.sem, self.base = sem, 0

    def __call__(self, n):
        return self.sem, self.base + n

    def passed(self, n):
        self.base += n


class Chain:

    def __init__(self, eng, signal):
        self.eng, self.count, self.n = eng, signal, 0

    def __call__(self, ins):
        self.n += 1
        ins.then_inc(self.count.sem, 1)
        self.eng.wait_ge(*self.count(self.n))


POOL_SIGNALS = ("table_scattered", "table_in", "x_gathered0", "x_gathered1", "more_rows", "row_fetched0", "row_fetched1", "row_fetched2", "row_fetched3")


class Core:
    def __init__(self, nc, ctx, ins, out):
        self.nc, self.ctx, self.ins, self.out = nc, ctx, ins, out
        self.events = {}
        self.scope = None
        self.tensors = 0

    def event(self, name):
        if name not in self.events:
            ctx = self.ctx if name in POOL_SIGNALS or self.scope is None else self.scope
            self.events[name] = Signal(ctx.enter_context(self.nc.semaphore(name)))
        return self.events[name]

    def sb(self, name, shape, dtype=F32, ctx=None):
        self.tensors += 1
        return (ctx or self.ctx).enter_context(self.nc.sbuf_tensor(f"{name}_{self.tensors}", shape, dtype))

    def step(self, name, eng, signal_total):
        c = Chain(eng, self.event(name))
        signal_total.append(c)
        return c


def close(chains):
    for c in chains:
        c.count.passed(c.n)


class Pieces:

    def __init__(self, core, raw, sources):
        self.core, self.raw, self.sources, self.places = core, raw, sources, raw.shape[1]
        self.full = [core.event(f"piece_full{i}") for i in range(self.places)]
        self.high, self.low, self.used = core.event("piece_high"), core.event("piece_low"), core.event("piece_used")
        self.issued = 0
        self.begun = 0
        self.hi = self.lo = None

    def stage(self, ctx, count=PARTS):
        self.count = count
        self.hi = self.core.sb("weights_high", [P, count, PIECE], F32R, ctx=ctx)
        self.lo = self.core.sb("weights_low", [P, count, PIECE], F32R, ctx=ctx)

    def columns(self, ring, places, p):
        k, n = self.sources[p].shape[1:]
        return ring[:, p % places, 0:k * n].rearrange("p (k n) -> p k n", k=k)

    def load_ahead(self, sp, count):
        last = min(self.begun + count + self.places, len(self.sources))
        while self.issued < last:
            p = self.issued
            if p >= self.places:
                sp.wait_ge(*self.low(p - self.places + 1))
            sp.dma_start(self.columns(self.raw, self.places, p), self.sources[p]).then_inc(self.full[p % self.places].sem, 16)
            self.issued += 1

    def split_high(self, act, p):
        act.wait_ge(*self.full[p % self.places](16 * (p // self.places + 1)))
        if p - self.begun >= self.count:
            act.wait_ge(*self.used(p - self.count + 1))
        self.core.nc.scalar.activation(self.columns(self.hi, self.count, p), self.columns(self.raw, self.places, p), ACT.Copy).then_inc(self.high.sem, 1)

    def split_low(self, dve, p):
        dve.wait_ge(*self.high(p + 1))
        if p - self.begun >= self.count:
            dve.wait_ge(*self.used(p - self.count + 1))
        self.core.nc.vector.tensor_tensor(self.columns(self.lo, self.count, p), self.columns(self.raw, self.places, p), self.columns(self.hi, self.count, p), ALU.subtract).then_inc(self.low.sem, 1)

    def arrived(self, pe, p):
        pe.wait_ge(*self.low(p + 1))

    def parts(self, p):
        return self.columns(self.hi, self.count, p), self.columns(self.lo, self.count, p)

    def close(self):
        n = len(self.sources)
        for p in range(n):
            self.full[p % self.places].passed(16)
        for s in (self.high, self.low, self.used):
            s.passed(n)


def pieces_of(w, r, n, width=BANK):
    return [w[r + q * 2 * P:r + (q + 1) * 2 * P, n:n + width].rearrange("(k p) n -> p k n", p=P) for q in range(PIECES)]


def load_stage(core, loads, name, ahead=None):
    nc, arrived_a, arrived_b = core.nc, core.event(name + "_a"), core.event(name + "_b")
    halves = loads[0::2], loads[1::2]
    with nc.Block() as block:
        @block.sync
        def _(sp):
            for dst, src in halves[0]:
                sp.dma_start(dst, src).then_inc(arrived_a.sem, 16)
            if ahead is not None:
                ahead(sp)
            if halves[0]:
                sp.wait_ge(*arrived_a(16 * len(halves[0])))

        @block.scalar
        def _(act):
            for dst, src in halves[1]:
                act.dma_start(dst, src).then_inc(arrived_b.sem, 16)
            if halves[1]:
                act.wait_ge(*arrived_b(16 * len(halves[1])))
    arrived_a.passed(16 * len(halves[0]))
    arrived_b.passed(16 * len(halves[1]))


def transposes_pe(core, pe, src_tile, done, bank0):
    for j in range(2):
        for c in range(4):
            k = 4 * j + c
            last = core.nc.tensor.transpose(core.psum[:, bank0 + j, c * P:(c + 1) * P], src_tile[:, k * P:(k + 1) * P], core.ident[:])
        last.then_inc(done.sem, 1)


def norm_stage(core, x, gain, shift, h, hT=None, out=None):
    nc, stats = core.nc, core.stats
    squares, spread, root = core.event("squares"), core.event("mean_square"), core.event("root")
    h_ready, turned = core.event("h_ready"), core.event("turned")
    stored = core.event("stored")
    ms, rt, rstd = stats[:, 0:T], stats[:, T:2 * T], stats[:, 2 * T:3 * T]
    copied = core.event("high_copied")
    high, low = hT if isinstance(hT, tuple) else (hT, None)
    chunks = lambda dst, j: dst[:, 4 * (j % 2):4 * (j % 2) + 4, (j // 2) * P:(j // 2 + 1) * P]
    bank = lambda j: core.psum[:, j, :].rearrange("p (k n) -> p k n", k=4)
    chains = []
    with nc.Block() as block:
        @block.scalar
        def _(act):
            for t in range(T):
                if t:
                    act.wait_ge(*squares(t))
                nc.scalar.activation(core.junk[:, 0, :], x[:, t, :], ACT.Square, accum_out=stats[:, 3 * T + t:3 * T + t + 1]).then_inc(squares.sem, 1)
            act.wait_ge(*spread(1))
            nc.scalar.activation(rt, ms, ACT.Sqrt).then_inc(root.sem, 1)
            for j in range(2 * T if hT is not None else 0):
                act.wait_ge(*turned(j + 1))
                nc.scalar.activation(chunks(high, j), bank(j), ACT.Copy).then_inc(copied.sem, 1)

        @block.vector
        def _(dve):
            step = core.step("dve_step", dve, chains)
            dve.wait_ge(*squares(T))
            nc.vector.tensor_scalar(ms, stats[:, 3 * T:4 * T], 1.0 / D, EPS, ALU.mult, ALU.add).then_inc(spread.sem, 1)
            dve.wait_ge(*root(1))
            step(nc.vector.reciprocal(rstd, rt))
            for t in range(T):
                ins = nc.vector.scalar_tensor_tensor(out=h[:, t, :], in0=x[:, t, :], scalar=rstd[:, t:t + 1], in1=gain, op0=ALU.mult, op1=ALU.mult)
                if shift is not None:
                    step(ins)
                    ins = nc.vector.tensor_tensor(h[:, t, :], h[:, t, :], shift, ALU.add)
                ins.then_inc(h_ready.sem, 1)
            for j in range(2 * T if low is not None else 0):
                dve.wait_ge(*copied(j + 1))
                nc.vector.tensor_tensor(chunks(low, j), bank(j), chunks(high, j), ALU.subtract)

        if hT is not None:
            @block.tensor
            def _(pe):
                for t in range(T):
                    pe.wait_ge(*h_ready(t + 1))
                    transposes_pe(core, pe, h[:, t, :], turned, 2 * t)

        if out is not None:
            @block.sync
            def _(sp):
                for t in range(T):
                    sp.wait_ge(*h_ready(t + 1))
                    sp.dma_start(out[t * P:(t + 1) * P, :], h[:, t, :]).then_inc(stored.sem, 16)
                sp.wait_ge(*stored(16 * T))
    squares.passed(T); spread.passed(1); root.passed(1); h_ready.passed(T)
    if hT is not None:
        turned.passed(2 * T)
        copied.passed(2 * T)
    if out is not None:
        stored.passed(16 * T)
    close(chains)


def transpose_stage(core, src, dstT):
    nc, turned, copied = core.nc, core.event("turned"), core.event("high_copied")
    chunks = lambda dst, j: dst[:, 4 * (j % 2):4 * (j % 2) + 4, (j // 2) * P:(j // 2 + 1) * P]
    bank = lambda j: core.psum[:, j, :].rearrange("p (k n) -> p k n", k=4)
    with nc.Block() as block:
        @block.tensor
        def _(pe):
            for t in range(T):
                transposes_pe(core, pe, src[:, t, :], turned, 2 * t)

        @block.scalar
        def _(act):
            for j in range(2 * T):
                act.wait_ge(*turned(j + 1))
                nc.scalar.activation(chunks(dstT[0], j), bank(j), ACT.Copy).then_inc(copied.sem, 1)

        @block.vector
        def _(dve):
            for j in range(2 * T):
                dve.wait_ge(*copied(j + 1))
                nc.vector.tensor_tensor(chunks(dstT[1], j), bank(j), chunks(dstT[0], j), ALU.subtract)
    turned.passed(2 * T)
    copied.passed(2 * T)


def product_in_parts(nc, out, a, b, start, stop):
    nc.tensor.matmul(out, a[0], b[0], start=start, stop=False)
    nc.tensor.matmul(out, a[0], b[1], start=False, stop=False)
    return nc.tensor.matmul(out, a[1], b[0], start=False, stop=stop)


def product_parts_stage(core, pieces, hT, widths, take, places=PARTS):
    nc = core.nc
    product, taken = core.event("product"), core.event("product_taken")
    first, count = pieces.begun, len(widths)
    with ExitStack() as ctx:
        pieces.stage(ctx, places)
        with nc.Block() as block:
            @block.sync
            def _(sp):
                pieces.load_ahead(sp, count * PIECES)

            @block.scalar
            def _(act):
                for p in range(first, first + count * PIECES):
                    pieces.split_high(act, p)

            @block.tensor
            def _(pe):
                for n, width in enumerate(widths):
                    for t in range(T):
                        i = n * T + t
                        if i >= 8:
                            pe.wait_ge(*taken(i - 7))
                        for k in range(KD):
                            p = first + n * PIECES + k // 2
                            if t == 0 and k % 2 == 0:
                                pieces.arrived(pe, p)
                            w = [part[:, k % 2, :] for part in pieces.parts(p)]
                            tokens = [part[:, k, t * P:(t + 1) * P] for part in hT]
                            last = product_in_parts(nc, core.psum[:, i % 8, 0:width], tokens, w, k == 0, k == KD - 1)
                            if t == T - 1 and k % 2:
                                last.then_inc(pieces.used.sem, 1)
                        if t < T - 1:
                            last.then_inc(product.sem, 1)

            @block.vector
            def _(dve):
                for q in range(PIECES):
                    pieces.split_low(dve, first + q)
                for n in range(count):
                    for t in range(T):
                        i = n * T + t
                        if n + 1 < count:
                            pieces.split_low(dve, first + (n + 1) * PIECES + t)
                        dve.wait_ge(*(product(n * (T - 1) + t + 1) if t < T - 1 else pieces.used(first + (n + 1) * PIECES)))
                        take(n, t, core.psum[:, i % 8, 0:widths[n]]).then_inc(taken.sem, 1)
    pieces.begun += count * PIECES
    product.passed((T - 1) * count)
    taken.passed(T * count)


def residual_stage(core, x, y, gain):
    nc, stats = core.nc, core.stats
    squares, spread, root = core.event("squares"), core.event("mean_square"), core.event("root")
    ms, rt, rstd = stats[:, 0:T], stats[:, T:2 * T], stats[:, 2 * T:3 * T]
    chains = []
    with nc.Block() as block:
        @block.scalar
        def _(act):
            for t in range(T):
                if t:
                    act.wait_ge(*squares(t))
                nc.scalar.activation(core.junk[:, 0, :], y[:, t, :], ACT.Square, accum_out=stats[:, 3 * T + t:3 * T + t + 1]).then_inc(squares.sem, 1)
            act.wait_ge(*spread(1))
            nc.scalar.activation(rt, ms, ACT.Sqrt).then_inc(root.sem, 1)

        @block.vector
        def _(dve):
            step = core.step("dve_step", dve, chains)
            dve.wait_ge(*squares(T))
            nc.vector.tensor_scalar(ms, stats[:, 3 * T:4 * T], 1.0 / D, EPS, ALU.mult, ALU.add).then_inc(spread.sem, 1)
            dve.wait_ge(*root(1))
            step(nc.vector.reciprocal(rstd, rt))
            for t in range(T):
                step(nc.vector.scalar_tensor_tensor(out=y[:, t, :], in0=y[:, t, :], scalar=rstd[:, t:t + 1], in1=gain, op0=ALU.mult, op1=ALU.mult))
                step(nc.vector.tensor_tensor(x[:, t, :], x[:, t, :], y[:, t, :], ALU.add))
    squares.passed(T); spread.passed(1); root.passed(1)
    close(chains)


def angles(core, step, posf, freq, cos, sin, tmp):
    nc = core.nc
    magic = 1.5 * 2.0 ** 23
    c1 = 6.28125
    c2 = float(np.float32(np.round((2 * np.pi - c1) * 2 ** 21) / 2 ** 21))
    c3 = float(np.float32(2 * np.pi - c1 - c2))
    ang, turns, red = tmp
    for t in range(T):
        step(nc.vector.tensor_scalar(ang[:, t, :], freq, posf[:, t:t + 1], None, ALU.mult))
    for out, quarter in ((cos, 0.25), (sin, 0.0)):
        step(nc.vector.tensor_scalar(turns, ang, 1.0 / (2 * np.pi), quarter, ALU.mult, ALU.add))
        step(nc.vector.tensor_scalar(turns, turns, magic, None, ALU.add))
        step(nc.vector.tensor_scalar(turns, turns, magic, None, ALU.subtract))
        step(nc.vector.scalar_tensor_tensor(out=red, in0=turns, scalar=-c1, in1=ang, op0=ALU.mult, op1=ALU.add))
        step(nc.vector.scalar_tensor_tensor(out=red, in0=turns, scalar=-c2, in1=red, op0=ALU.mult, op1=ALU.add))
        step(nc.vector.scalar_tensor_tensor(out=red, in0=turns, scalar=-c3, in1=red, op0=ALU.mult, op1=ALU.add))
        step(nc.vector.tensor_scalar(red, red, quarter * 2 * np.pi, 3.1415925, ALU.add, ALU.min))
        step(nc.vector.tensor_scalar(out, red, -3.1415925, None, ALU.max))


def angle_stage(core, posi, posf, freq, half, cos, sin, tmp):
    nc, reduced = core.nc, core.event("angles_reduced")
    chains = []
    with nc.Block() as block:
        @block.vector
        def _(dve):
            step = core.step("dve_step", dve, chains)
            step(nc.vector.tensor_copy(posf[:], posi[:]))
            angles(core, step, posf, freq, cos[:], sin[:], tmp)
            dve.sem_inc(reduced.sem, 1)

        @block.scalar
        def _(act):
            act.wait_ge(*reduced(1))
            nc.scalar.activation(cos[:], cos[:], ACT.Sin)
            nc.scalar.activation(sin[:], sin[:], ACT.Sin)
    reduced.passed(1)
    close(chains)


def rotate(nc, step, dst, src, cos, sin, tmp, heads, half):
    c = cos.unsqueeze(1).broadcast_to([P, heads, half])
    s = sin.unsqueeze(1).broadcast_to([P, heads, half])
    a, b = src[:, :, 0:half], src[:, :, half:2 * half]
    t1, t2 = tmp[:, 0, 0:heads, 0:half], tmp[:, 1, 0:heads, 0:half]
    nc.vector.tensor_tensor(t1, a, c, ALU.mult)
    step(nc.vector.tensor_tensor(t2, b, s, ALU.mult))
    t3, t4 = tmp[:, 2, 0:heads, 0:half], tmp[:, 3, 0:heads, 0:half]
    nc.vector.tensor_tensor(t3, b, c, ALU.mult)
    step(nc.vector.tensor_tensor(t4, a, s, ALU.mult))
    nc.vector.tensor_tensor(dst[:, :, 0:half], t1, t2, ALU.subtract)
    step(nc.vector.tensor_tensor(dst[:, :, half:2 * half], t3, t4, ALU.add))


def warm_up(core, count=4):
    for _ in range(count):
        core.nc.tensor.matmul(core.psum[:, 7, :], core.ident[:], core.mask[:], start=True, stop=True)


def attention_stage(core, units, scale, prepare=None, warm=False):
    nc = core.nc
    n = len(units)
    scores, biased = core.event("scores"), core.event("scores_biased")
    probs, turned, turned_sb = core.event("probs"), core.event("probs_turned"), core.event("probs_turned_sb")
    summed, done = core.event("values_summed"), core.event("head_out")
    chains = []
    with ExitStack() as ctx:
        s_sb = core.sb("att_scores", [P, 3, S], ctx=ctx)
        p_sb = core.sb("att_probs", [P, 3, S], ctx=ctx)
        pt_sb = core.sb("att_turned", [P, 3, S], ctx=ctx)
        top = core.sb("att_max", [P, 8], ctx=ctx)
        low = core.sb("att_negmax", [P, 8], ctx=ctx)
        den = core.sb("att_den", [P, 8], ctx=ctx)
        inv = core.sb("att_inv", [P, 8], ctx=ctx)
        with nc.Block() as block:
            @block.tensor
            def _(pe):
                def score(u):
                    q, k, _, _, _, keys = units[u]
                    if u >= 3:
                        pe.wait_ge(*biased(u - 2))
                    nc.tensor.matmul(core.psum[:, u % 3, 0:keys], q, k, start=True, stop=True).then_inc(scores.sem, 1)

                def turn(u):
                    keys = units[u][5]
                    pe.wait_ge(*probs(u + 1))
                    if u >= 3:
                        pe.wait_ge(*turned_sb(u - 2))
                    for j in range(keys // P):
                        last = nc.tensor.transpose(core.psum[:, 3 + u % 3, j * P:(j + 1) * P], p_sb[:, u % 3, j * P:(j + 1) * P], core.ident[:])
                    last.then_inc(turned.sem, 1)

                def values(u):
                    _, _, _, v, _, keys = units[u]
                    pe.wait_ge(*turned_sb(u + 1))
                    if u >= 2:
                        pe.wait_ge(*done(u - 1))
                    for j in range(keys // P):
                        last = nc.tensor.matmul(core.psum[:, 6 + u % 2, 0:HD], pt_sb[:, u % 3, j * P:(j + 1) * P], v(j), start=(j == 0), stop=(j == keys // P - 1))
                    last.then_inc(summed.sem, 1)

                if warm:
                    warm_up(core)
                for u in range(n + 4):
                    if u < n:
                        score(u)
                    if 2 <= u < n + 2:
                        turn(u - 2)
                    if u >= 4:
                        values(u - 4)

            @block.vector
            def _(dve):
                step = core.step("dve_step", dve, chains)

                def bias(u):
                    _, _, b, _, _, keys = units[u]
                    if prepare is not None:
                        prepare(step, u)
                    dve.wait_ge(*scores(u + 1))
                    if u >= 3:
                        dve.wait_ge(*probs(u - 2))
                    step(nc.vector.tensor_tensor_reduce(out=s_sb[:, u % 3, 0:keys], in0=core.psum[:, u % 3, 0:keys], in1=b, scale=scale, scalar=-3e38,
                                                        op0=ALU.add, op1=ALU.max, accum_out=top[:, u % 8:u % 8 + 1]))
                    nc.vector.tensor_scalar(low[:, u % 8:u % 8 + 1], top[:, u % 8:u % 8 + 1], -1.0, None, ALU.mult).then_inc(biased.sem, 1)

                def finish(u):
                    dve.wait_ge(*summed(u + 1))
                    step(nc.vector.reciprocal(inv[:, u % 8:u % 8 + 1], den[:, u % 8:u % 8 + 1]))
                    nc.vector.tensor_scalar(units[u][4], core.psum[:, 6 + u % 2, 0:HD], inv[:, u % 8:u % 8 + 1], None, ALU.mult).then_inc(done.sem, 1)

                for u in range(n + 4):
                    if u < n:
                        bias(u)
                    if u >= 4:
                        finish(u - 4)

            @block.scalar
            def _(act):
                def exps(u):
                    keys = units[u][5]
                    act.wait_ge(*biased(u + 1))
                    if u >= 3:
                        act.wait_ge(*turned(u - 2))
                    if u >= 8:
                        act.wait_ge(*done(u - 7))
                    nc.scalar.activation(p_sb[:, u % 3, 0:keys], s_sb[:, u % 3, 0:keys], ACT.Exp, bias=low[:, u % 8:u % 8 + 1], accum_out=den[:, u % 8:u % 8 + 1]).then_inc(probs.sem, 1)

                def copy(u):
                    keys = units[u][5]
                    act.wait_ge(*turned(u + 1))
                    if u >= 3:
                        act.wait_ge(*summed(u - 2))
                    nc.scalar.activation(pt_sb[:, u % 3, 0:keys], core.psum[:, 3 + u % 3, 0:keys], ACT.Copy).then_inc(turned_sb.sem, 1)

                for u in range(n + 2):
                    if u < n:
                        exps(u)
                    if u >= 2:
                        copy(u - 2)
    for s in (scores, biased, probs, turned, turned_sb, summed, done):
        s.passed(n)
    close(chains)


def turn_stage(core, turns):
    nc, turned, taken_a, taken_d = core.nc, core.event("turned"), core.event("taken_act"), core.event("taken_dve")
    n = len(turns)
    with nc.Block() as block:
        @block.tensor
        def _(pe):
            for i, (dst, srcs, m) in enumerate(turns):
                if i >= 8:
                    j = i - 8
                    pe.wait_ge(*(taken_d if j % 2 else taken_a)(j // 2 + 1))
                for c, src in enumerate(srcs):
                    bank = core.psum[0:src.shape[1], i % 8, c * P:(c + 1) * P]
                    if m is core.ident:
                        last = nc.tensor.transpose(bank, src, m[:])
                    else:
                        last = nc.tensor.matmul(bank, src, m[:], start=True, stop=True)
                last.then_inc(turned.sem, 1)

        @block.scalar
        def _(act):
            for i in range(0, n, 2):
                act.wait_ge(*turned(i + 1))
                dst, srcs, _ = turns[i]
                nc.scalar.activation(dst, core.psum[0:srcs[0].shape[1], i % 8, 0:P * len(srcs)], ACT.Copy).then_inc(taken_a.sem, 1)

        @block.vector
        def _(dve):
            for i in range(1, n, 2):
                dve.wait_ge(*turned(i + 1))
                dst, srcs, _ = turns[i]
                nc.vector.tensor_copy(dst, core.psum[0:srcs[0].shape[1], i % 8, 0:P * len(srcs)]).then_inc(taken_d.sem, 1)
    turned.passed(n)
    taken_a.passed((n + 1) // 2)
    taken_d.passed(n // 2)


def modulation_stage(core, pieces, mod, gate, silu_c, b_rows, loads):
    nc = core.nc
    raw, wide, product, taken, loaded = core.event("silu_c"), core.event("c_wide"), core.event("product"), core.event("product_taken"), core.event("later_loads")
    row_high, row_low = core.event("b_row_high"), core.event("b_row_low")
    count, first = 12, pieces.begun
    with ExitStack() as ctx:
        c_wide = [core.sb(n, [P, KD, P], F32R, ctx=ctx) for n in ("c_high", "c_low")]
        wide_f = core.sb("c_wide", [P, KD, P], ctx=ctx)
        pick = core.sb("bias_row_picked", [count, count, P], F32R, ctx=ctx)
        rows = [core.sb(n, [count, BANK], F32R, ctx=ctx) for n in ("b_rows_high", "b_rows_low")]
        pieces.stage(ctx, ADA_PARTS)
        with nc.Block() as block:
            @block.sync
            def _(sp):
                pieces.load_ahead(sp, count * PIECES)

            @block.scalar
            def _(act):
                for dst, src in loads:
                    act.dma_start(dst, src).then_inc(loaded.sem, 16)
                nc.scalar.activation(silu_c[:, 1, :], silu_c[:, 0, :], ACT.Exp, scale=-1.0).then_inc(raw.sem, 1)
                act.wait_ge(*wide(1))
                nc.scalar.activation(c_wide[0][:], wide_f[:], ACT.Copy).then_inc(wide.sem, 1)
                for p in range(count * PIECES):
                    if p == PIECES:
                        nc.scalar.activation(rows[0][:], b_rows[:], ACT.Copy).then_inc(row_high.sem, 1)
                    pieces.split_high(act, first + p)
                act.wait_ge(*loaded(16 * len(loads)))

            @block.vector
            def _(dve):
                nc.vector.tensor_copy(pick[:], core.ident[0:count, 0:count].unsqueeze(2).broadcast_to([count, count, P])).then_inc(raw.sem, 1)
                dve.wait_ge(*raw(2))
                nc.vector.tensor_scalar(silu_c[:, 1, :], silu_c[:, 1, :], 1.0, None, ALU.add).then_inc(raw.sem, 1)
                dve.wait_ge(*raw(3))
                nc.vector.reciprocal(silu_c[:, 1, :], silu_c[:, 1, :]).then_inc(raw.sem, 1)
                dve.wait_ge(*raw(4))
                nc.vector.tensor_tensor(silu_c[:, 0, :], silu_c[:, 0, :], silu_c[:, 1, :], ALU.mult).then_inc(raw.sem, 1)
                dve.wait_ge(*raw(5))
                nc.vector.tensor_copy(wide_f[:], silu_c[:, 0, :].unsqueeze(2).broadcast_to([P, KD, P])).then_inc(wide.sem, 1)
                dve.wait_ge(*wide(2))
                nc.vector.tensor_tensor(c_wide[1][:], wide_f[:], c_wide[0][:], ALU.subtract).then_inc(wide.sem, 1)

                def take(n):
                    dve.wait_ge(*product(n + 1))
                    to = mod[:, n * BANK:(n + 1) * BANK] if n < 10 else gate[:, (n - 10) * BANK:(n - 9) * BANK]
                    nc.vector.tensor_copy(to, core.psum[:, n % 8, :]).then_inc(taken.sem, 1)

                for n in range(count):
                    for q in range(PIECES):
                        pieces.split_low(dve, first + n * PIECES + q)
                        if n == 1 and q == 0:
                            dve.wait_ge(*row_high(1))
                            nc.vector.tensor_tensor(rows[1][:], b_rows[:], rows[0][:], ALU.subtract).then_inc(row_low.sem, 1)
                        if n and q == 1:
                            take(n - 1)
                take(count - 1)

            @block.tensor
            def _(pe):
                pe.wait_ge(*wide(3))
                for n in range(count):
                    bank = core.psum[:, n % 8, :]
                    if n >= 8:
                        pe.wait_ge(*taken(n - 7))
                    for k in range(KD):
                        p = first + n * PIECES + k // 2
                        if k % 2 == 0:
                            pieces.arrived(pe, p)
                        last = product_in_parts(nc, bank, [part[:, k, :] for part in c_wide], [part[:, k % 2, :] for part in pieces.parts(p)], k == 0, False)
                        if k % 2:
                            last.then_inc(pieces.used.sem, 1)
                    if n == 0:
                        pe.wait_ge(*row_low(1))
                    nc.tensor.matmul(bank, pick[:, n, :], rows[0][:], start=False, stop=False)
                    nc.tensor.matmul(bank, pick[:, n, :], rows[1][:], start=False, stop=True).then_inc(product.sem, 1)
    pieces.begun += count * PIECES
    raw.passed(5); wide.passed(3); product.passed(count); taken.passed(count); loaded.passed(16 * len(loads)); row_high.passed(1); row_low.passed(1)


def gains_stage(core, mod, gate, gains):
    nc = core.nc
    chains = []
    part = [mod[:, n * D:(n + 1) * D] for n in range(5)] + [gate[:]]
    with nc.Block() as block:
        @block.vector
        def _(dve):
            for n, g, one in ((1, 0, 1.0), (2, 1, 0.0), (4, 2, 1.0), (5, 3, 0.0)):
                nc.vector.scalar_tensor_tensor(out=part[n], in0=part[n], scalar=one, in1=gains[:, g, :], op0=ALU.add, op1=ALU.mult)


def mla_stages(core, proj, y, hT, cos, sin, W, prepare):
    nc, stats = core.nc, core.stats
    cq, ckv = proj[:, :, 0:Q_RANK], proj[:, :, OFF1[1]:OFF1[2]]
    squares, spread, root = core.event("squares"), core.event("mean_square"), core.event("root")
    chains = []
    ms, rt, rstd = stats[:, 0:2 * T], stats[:, 2 * T:4 * T], stats[:, 4 * T:6 * T]
    with ExitStack() as ctx:
        qT = hT[0:QK1]
        kT = core.sb("mla_kT", [QK1, H1, S], ctx=ctx)
        v = core.sb("mla_v", [P, T, H1 * VDIM], ctx=ctx)
        with ExitStack() as inner:
            gq = core.sb("gain_q", [P, Q_RANK], ctx=inner)
            gkv = core.sb("gain_kv", [P, KV_RANK], ctx=inner)
            wq = core.sb("w_q_b", [P, 2, H1 * QK1], ctx=inner)
            wkv = core.sb("w_kv_b", [P, H1 * (NOPE + VDIM)], ctx=inner)
            latT = core.sb("latentsT", [P, 3, S], ctx=inner)
            qk = core.sb("mla_q_and_k", [P, H1, QK1], ctx=inner)
            kk = core.sb("mla_k_full", [P, H1, QK1], ctx=inner)
            tmp = core.sb("rotate_tmp", [P, 4, H1, ROPE // 2], ctx=inner)
            krot = core.sb("k_rotated", [P, T, 1, ROPE], ctx=inner)
            load_stage(core, [(gq[:], W["g_q_a"][0].partition_broadcast(P)), (gkv[:], W["g_kv_a"][0].partition_broadcast(P)),
                              (wq[:], W["w_q_b"][0].rearrange("(k p) n -> p k n", p=P)), (wkv[:], W["w_kv_b"][0])], "latent_weights")
            with nc.Block() as block:
                @block.scalar
                def _(act):
                    for i in range(2 * T):
                        src = (cq if i < T else ckv)[:, i % T, :]
                        if i:
                            act.wait_ge(*squares(i))
                        nc.scalar.activation(core.junk[:, 0, 0:src.shape[1]], src, ACT.Square, accum_out=stats[:, 6 * T + i:6 * T + i + 1]).then_inc(squares.sem, 1)
                    act.wait_ge(*spread(1))
                    nc.scalar.activation(rt, ms, ACT.Sqrt).then_inc(root.sem, 1)

                @block.vector
                def _(dve):
                    step = core.step("dve_step", dve, chains)
                    dve.wait_ge(*squares(2 * T))
                    nc.vector.tensor_scalar(ms[:, 0:T], stats[:, 6 * T:7 * T], 1.0 / Q_RANK, EPS, ALU.mult, ALU.add)
                    step(nc.vector.tensor_scalar(ms[:, T:2 * T], stats[:, 7 * T:8 * T], 1.0 / KV_RANK, EPS, ALU.mult, ALU.add))
                    dve.sem_inc(spread.sem, 1)
                    dve.wait_ge(*root(1))
                    step(nc.vector.reciprocal(rstd, rt))
                    for t in range(T):
                        nc.vector.scalar_tensor_tensor(out=cq[:, t, :], in0=cq[:, t, :], scalar=rstd[:, t:t + 1], in1=gq[:], op0=ALU.mult, op1=ALU.mult)
                        nc.vector.scalar_tensor_tensor(out=ckv[:, t, :], in0=ckv[:, t, :], scalar=rstd[:, T + t:T + t + 1], in1=gkv[:], op0=ALU.mult, op1=ALU.mult)
            squares.passed(2 * T); spread.passed(1); root.passed(1)
            close(chains)
            chains = []
            turn_stage(core, [(latT[:, c, :], [proj[:, t, c * P:(c + 1) * P] for t in range(T)], core.ident) for c in range(3)])
            made, rotated, k_full, turned, taken = (core.event(s) for s in ("qkv_made", "q_rotated", "k_full", "turned", "product_taken"))
            with nc.Block() as block:
                @block.tensor
                def _(pe):
                    for t in range(T):
                        tile = slice(t * P, (t + 1) * P)
                        if t:
                            pe.wait_ge(*rotated(t))
                            pe.wait_ge(*k_full(t))
                        for n, w in ((0, 4 * QK1), (1, 4 * QK1)):
                            for c in range(2):
                                nc.tensor.matmul(core.psum[:, n, 0:w], latT[:, c, tile], wq[:, c, n * w:(n + 1) * w], start=(c == 0), stop=(c == 1))
                        for n in range(2):
                            last = nc.tensor.matmul(core.psum[:, 2 + n, :], latT[:, 2, tile], wkv[:, n * BANK:(n + 1) * BANK], start=True, stop=True)
                        last.then_inc(made.sem, 1)
                        for i, src in enumerate((qk, kk)):
                            pe.wait_ge(*(rotated, k_full)[i](t + 1))
                            if t:
                                pe.wait_ge(*taken(4 * (t - 1) + 2 * i + 2))
                            for h in range(H1):
                                last = nc.tensor.transpose(core.psum[0:QK1, 4 + 2 * i + h // 4, (h % 4) * P:(h % 4 + 1) * P], src[:, h, :], core.ident[:])
                            last.then_inc(turned.sem, 1)

                @block.vector
                def _(dve):
                    step = core.step("dve_step", dve, chains)
                    for t in range(T):
                        rotate(nc, step, krot[:, t], proj[:, t, OFF1[2]:OFF1[3]].unsqueeze(1), cos[:, t, :], sin[:, t, :], tmp, 1, ROPE // 2)
                    for t in range(T):
                        dve.wait_ge(*made(t + 1))
                        if t:
                            dve.wait_ge(*turned(2 * t))
                        for n in range(2):
                            half = core.psum[:, n, 0:4 * QK1].rearrange("p (h d) -> p h d", h=4)
                            nc.vector.tensor_copy(qk[:, 4 * n:4 * n + 4, 0:NOPE], half[:, :, 0:NOPE])
                            rotate(nc, step, qk[:, 4 * n:4 * n + 4, NOPE:QK1], half[:, :, NOPE:QK1], cos[:, t, :], sin[:, t, :], tmp, 4, ROPE // 2)
                        dve.sem_inc(rotated.sem, 1)
                        for n in range(2):
                            half = core.psum[:, 2 + n, :].rearrange("p (h d) -> p h d", h=4)
                            nc.vector.tensor_copy(kk[:, 4 * n:4 * n + 4, 0:NOPE], half[:, :, 0:NOPE])
                            nc.vector.tensor_copy(v[:, t, n * 4 * VDIM:(n + 1) * 4 * VDIM].rearrange("p (h d) -> p h d", h=4), half[:, :, NOPE:])
                        step(nc.vector.tensor_copy(kk[:, :, NOPE:QK1], krot[:, t].broadcast_to([P, H1, ROPE])))
                        dve.sem_inc(k_full.sem, 1)

                @block.scalar
                def _(act):
                    for t in range(T):
                        for i, dst in enumerate((qT, kT)):
                            act.wait_ge(*turned(2 * t + i + 1))
                            for n in range(2):
                                nc.scalar.activation(dst[:, 4 * n:4 * n + 4, t * P:(t + 1) * P], core.psum[0:QK1, 4 + 2 * i + n, :].rearrange("p (h m) -> p h m", h=4), ACT.Copy).then_inc(taken.sem, 1)
            made.passed(T); rotated.passed(T); k_full.passed(T); turned.passed(2 * T); taken.passed(4 * T)
            close(chains)
        units = []
        for t in range(T):
            keys = (t + 1) * P
            for h in range(H1):
                units.append((qT[:, h, t * P:(t + 1) * P], kT[:, h, 0:keys], core.mask[:, (T - 1 - t) * P:(T - 1 - t) * P + keys],
                              lambda j, h=h: v[:, j, h * VDIM:(h + 1) * VDIM], y[:, t, h * VDIM:(h + 1) * VDIM], keys))
        attention_stage(core, units, QK1 ** -0.5, prepare)


def index_stages(core, proj, sel):
    nc = core.nc
    qio, kio, wio = OFF1[6:9]
    with ExitStack() as inner:
        twice = core.sb("idx_k4", [P, T, P], ctx=inner)
        qiT = core.sb("idx_qT", [P, 2, S], ctx=inner)
        kiT = core.sb("idx_kT", [P, S], ctx=inner)
        rel = core.sb("idx_rel", [P, 2, S], ctx=inner)
        with nc.Block() as block:
            @block.vector
            def _(dve):
                for g in range(4):
                    nc.vector.tensor_copy(twice[:, :, g * IDX_D:(g + 1) * IDX_D], proj[:, :, kio:kio + IDX_D])
                nc.vector.tensor_scalar(proj[:, :, wio:wio + IDX_H], proj[:, :, wio:wio + IDX_H], IDX_H ** -0.5, None, ALU.mult)
        turns = [(kiT[:], [twice[:, t, :] for t in range(T)], core.ident)]
        turns += [(qiT[:, c, :], [proj[:, t, qio + c * P:qio + (c + 1) * P] for t in range(T)], core.ident) for c in range(2)]
        turn_stage(core, turns)
        score, relu, added = core.event("idx_scores"), core.event("idx_relu"), core.event("idx_added")
        chains = []
        tiles = range(1, T)
        with nc.Block() as block:
            @block.tensor
            def _(pe):
                i = 0
                for t in tiles:
                    for h in range(IDX_H):
                        if i >= 8:
                            pe.wait_ge(*relu(i - 7))
                        g = (h % 4) * IDX_D
                        nc.tensor.matmul(core.psum[:, i % 8, 0:(t + 1) * P], qiT[g:g + IDX_D, h // 4, t * P:(t + 1) * P], kiT[g:g + IDX_D, 0:(t + 1) * P], start=True, stop=True).then_inc(score.sem, 1)
                        i += 1

            @block.scalar
            def _(act):
                i = 0
                for t in tiles:
                    for h in range(IDX_H):
                        act.wait_ge(*score(i + 1))
                        if i >= 2:
                            act.wait_ge(*added(i - 1))
                        nc.scalar.activation(rel[:, i % 2, 0:(t + 1) * P], core.psum[:, i % 8, 0:(t + 1) * P], ACT.Relu, scale=IDX_D ** -0.5).then_inc(relu.sem, 1)
                        i += 1

            @block.vector
            def _(dve):
                step = core.step("dve_step", dve, chains)
                i = 0
                nc.vector.tensor_copy(sel[:, 0, 0:P], core.mask[:, (T - 1) * P:T * P])
                for t in tiles:
                    keys = (t + 1) * P
                    acc = sel[:, t, 0:keys]
                    for h in range(IDX_H):
                        dve.wait_ge(*relu(i + 1))
                        base = core.mask[:, (T - 1 - t) * P:(T - 1 - t) * P + keys] if h == 0 else acc
                        ins = nc.vector.scalar_tensor_tensor(out=acc, in0=rel[:, i % 2, 0:keys], scalar=proj[:, t, wio + h:wio + h + 1], in1=base, op0=ALU.mult, op1=ALU.add)
                        ins.then_inc(added.sem, 1)
                        dve.wait_ge(*added(i + 1))
                        i += 1
        n = IDX_H * len(tiles)
        score.passed(n); relu.passed(n); added.passed(n)
        close(chains)


def selection(core, sel, best):
    nc = core.nc
    rounds = TOPK // 8
    total = rounds * (T - 1)

    def some(step, u):
        for i in range(u * total // (T * H1), (u + 1) * total // (T * H1)):
            t = 1 + i // rounds
            keys = (t + 1) * P
            scores = sel[:, t, 0:keys]
            step(nc.vector.max(best[:], scores))
            step(nc.vector.match_replace(scores, best[:], scores, -3e38))
            if i % rounds == rounds - 1:
                step(nc.vector.tensor_scalar(scores, scores, -2e38, 8 * NEG, ALU.is_gt, ALU.mult))
                step(nc.vector.tensor_tensor(scores[:, t * P:keys], scores[:, t * P:keys], core.mask[:, (T - 1) * P:T * P], ALU.add))

    return some


def dsa_stages(core, proj, y, hT, posf, W, sel):
    nc = core.nc
    qo, ko, vo = OFF1[3:6]
    with ExitStack() as ctx:
        qT = hT[:, 0:H1 // 2, :]
        kT = hT[:, H1 // 2:H1 // 2 + KV2, :]
        dist = core.sb("dsa_dist", [P, T, S], ctx=ctx)
        twice = core.sb("dsa_twice", [P, T, 2, P], ctx=ctx)
        posk_i = core.sb("key_pos_i", [P, S], I32, ctx=ctx)
        biasb = core.sb("dsa_bias", [P, 2, S], ctx=ctx)
        load_stage(core, [(posk_i[:], W["positions"][0].partition_broadcast(P))], "key_positions")
        chains = []
        with nc.Block() as block:
            @block.vector
            def _(dve):
                step = core.step("dve_step", dve, chains)
                for g in range(2):
                    nc.vector.tensor_copy(twice[:, :, 0, g * HD:(g + 1) * HD], proj[:, :, ko:ko + HD])
                    nc.vector.tensor_copy(twice[:, :, 1, g * HD:(g + 1) * HD], proj[:, :, ko + HD:ko + 2 * HD])
                step(nc.vector.tensor_copy(biasb[:, 0, :], posk_i[:]))
                for t in range(T):
                    step(nc.vector.tensor_scalar(dist[:, t, :], biasb[:, 0, :], posf[:, t:t + 1], None, ALU.subtract))
                    nc.vector.scalar_tensor_tensor(out=dist[:, t, :], in0=dist[:, t, :], scalar=-1.0, in1=dist[:, t, :], op0=ALU.mult, op1=ALU.max)
        close(chains)
        turns = [(kT[:, g, :], [twice[:, t, g, :] for t in range(T)], core.ident) for g in range(KV2)]
        turns += [(qT[:, c, :], [proj[:, t, qo + c * P:qo + (c + 1) * P] for t in range(T)], core.ident) for c in range(4)]
        turn_stage(core, turns)
        units = []
        for t in range(T):
            keys = (t + 1) * P
            for h in range(H1):
                g, half = h // (H1 // KV2), (h % 2) * HD
                u = len(units)
                units.append((qT[half:half + HD, h // 2, t * P:(t + 1) * P], kT[half:half + HD, g, 0:keys], biasb[:, u % 2, 0:keys],
                              lambda j, g=g: proj[:, j, vo + g * HD:vo + (g + 1) * HD], y[:, t, H1 * VDIM + h * HD:H1 * VDIM + (h + 1) * HD], keys))

        def alibi(step, u):
            t, h = u // H1, u % H1
            keys = (t + 1) * P
            slope = 2.0 ** (-8.0 * (h + 1) / H1) * HD ** 0.5
            step(nc.vector.scalar_tensor_tensor(out=biasb[:, u % 2, 0:keys], in0=dist[:, t, 0:keys], scalar=-slope, in1=sel[:, t, 0:keys], op0=ALU.mult, op1=ALU.add))

        attention_stage(core, units, HD ** -0.5, alibi)


def first_mixer(core, W, x, mod, gate, ring):
    nc = core.nc
    sources = []
    for n in range(12):
        sources += pieces_of(W["w_ada"][0], 0, n * BANK)
    widths1 = [min(BANK, IN1 - n * BANK) for n in range(3)]
    for n in range(3):
        sources += pieces_of(W["w_in"][0], 0, n * BANK, widths1[n])
    for n in range(2):
        sources += pieces_of(W["w_o"][0], 0, n * BANK)
    pieces = Pieces(core, ring, sources)
    with ExitStack() as ctx:
        posi = core.sb("pos_i1", [P, T], I32, ctx=ctx)
        with ExitStack() as inner:
            silu_c = core.sb("silu_c", [P, 2, KD], ctx=inner)
            b_rows = core.sb("b_ada_rows", [12, BANK], ctx=inner)
            gains = core.sb("gains", [P, 4, D], ctx=inner)
            load_stage(core, [(silu_c[:, 0, :], W["c_cols"]), (b_rows[:], W["b_ada"][0].rearrange("(n m) -> n m", m=BANK)), (posi[:], W["pos_cols"])], "first_loads", lambda sp: pieces.load_ahead(sp, 0))
            later = [(x[:, t, :], W["x"][0, t * P:(t + 1) * P, :]) for t in range(T)]
            later += [(gains[:, i, :], W[n][0].partition_broadcast(P)) for i, n in enumerate(("g_pre_mix", "g_post_mix", "g_pre_ffn", "g_post_ffn"))]
            modulation_stage(core, pieces, mod, gate, silu_c, b_rows, later)
            gains_stage(core, mod, gate, gains)
        part = [mod[:, n * D:(n + 1) * D] for n in range(5)]
        proj = core.sb("proj1", [P, T, IN1], ctx=ctx)
        posf = core.sb("pos_f1", [P, T], ctx=ctx)

        def in_parts(inner):
            return tuple(core.sb(n, [P, KD, S], F32R, ctx=inner) for n in ("hT_high", "hT_low"))

        with ExitStack() as inner:
            hT = in_parts(inner)
            with ExitStack() as own:
                norm_stage(core, x, part[1], part[0], core.sb("h1", [P, T, D], ctx=own), hT)
            product_parts_stage(core, pieces, hT, widths1, lambda n, t, bank: nc.vector.tensor_copy(proj[:, t, n * BANK:n * BANK + bank.shape[1]], bank), MIX_PARTS)
        y = core.sb("mix1", [P, T, D], ctx=ctx)
        with ExitStack() as inner:
            hT = core.sb("hT1", [P, KD, S], ctx=inner)
            cos, sin = (core.sb(n, [P, T, ROPE // 2], ctx=inner) for n in ("cos1", "sin1"))
            with ExitStack() as own:
                tmp = core.sb("angle_tmp1", [P, 3, T, ROPE // 2], ctx=own)
                angle_stage(core, posi, posf, core.freq1[:], ROPE // 2, cos, sin, [tmp[:, i] for i in range(3)])
            assert len(sources) % pieces.places + 2 <= pieces.places and 2 * PIECES <= len(sources) % pieces.places
            sel = ring[:, pieces.places - 2:pieces.places, :].rearrange("p a (b n) -> p (a b) n", n=S)
            best = core.sb("idx_best", [P, 8], ctx=inner)
            index_stages(core, proj, sel)
            mla_stages(core, proj, y, hT, cos, sin, W, selection(core, sel, best))
            dsa_stages(core, proj, y, hT, posf, W, sel)
        with ExitStack() as inner:
            hT = in_parts(inner)
            transpose_stage(core, y, hT)
            product_parts_stage(core, pieces, hT, [BANK] * 2, lambda n, t, bank: nc.vector.tensor_copy(y[:, t, n * BANK:(n + 1) * BANK], bank), MIX_PARTS)
        pieces.close()
        residual_stage(core, x, y, part[2])


def store_stage(core, x, out):
    nc, stored = core.nc, core.event("stored")
    with nc.Block() as block:
        @block.sync
        def _(sp):
            for t in range(T):
                sp.dma_start(out[t * P:(t + 1) * P, :], x[:, t, :]).then_inc(stored.sem, 16)
            sp.wait_ge(*stored(16 * T))
    stored.passed(16 * T)


def setup(nc, W, out, ctx):
    core = Core(nc, ctx, W, out)
    core.psum = ctx.enter_context(nc.psum_tensor("banks", [P, 8, BANK], F32))
    core.ident = core.sb("ident", [P, P])
    core.mask = core.sb("mask", [P, S])
    core.freq1 = core.sb("freq1", [P, ROPE // 2])
    core.stats = core.sb("stats", [P, 8 * T])
    core.junk = core.sb("junk", [P, 1, D])
    x = core.sb("x", [P, T, D])
    with nc.Block() as block:
        @block.vector
        def _(dve):
            nc.vector.memset(core.mask[:, 0:S - P], 0.0)
    load_stage(core, [(core.ident[:], W["ident"]), (core.mask[:, S - P:S], W["causal"]), (core.freq1[:], W["freq1"])], "constants")
    return core, x


CAP = P
BLOCKS = S // CAP
ROWS = S


W1_PIECES, W2_PIECES = KD * 2, F // P
PER_EXPERT = W1_PIECES + W2_PIECES
E_RAW = 12
E_PARTS = 8


class Moe:

    def __init__(self, core, ctx, ring):
        sb = lambda name, shape, dtype=F32: core.sb(name, shape, dtype, ctx=ctx)
        self.core, self.raw = core, ring
        self.index = sb("token_of_slot", [P, E * BLOCKS], I32)
        self.slot = sb("slot_of_token", [P, T, TOP_E], U32)
        self.rank = sb("rank_in_expert", [P, T, E])
        self.gate = sb("gate", [P, T, TOP_E])
        self.spread = sb("gate_by_expert", [P, T, E])
        self.flag = sb("more_blocks", [1, 2], I32)
        nc = core.nc
        self.h2 = nc.dram_tensor("h2_rows", [S, D], F32).ap()
        self.slots = nc.dram_tensor("expert_out", [E * CAP, D], F32).ap()
        self.table = nc.dram_tensor("token_table", [E * ROWS, 1], F32).ap()
        self.full = [core.event(f"weight_full{i}") for i in range(E_RAW)]
        self.high, self.low, self.used = core.event("weight_high"), core.event("weight_low"), core.event("weight_used")

    def first_piece(self, e, k):
        return (0, k) if isinstance(e, int) and e == 0 else (e, k - W2_PIECES)

    def second_piece(self, e, k):
        return (E, k - W2_PIECES) if isinstance(e, int) and e == E - 1 else (e, PER_EXPERT + W2_PIECES + k)

    def first_src(self, W, e, k):
        return W["w_mlp1"][0, e][(k // 2) * P:(k // 2 + 1) * P, (k % 2) * PIECE:(k % 2 + 1) * PIECE]

    def second_src(self, W, e, k):
        return W["w_mlp2"][0, e][k * P:(k + 1) * P, :]

    def load(self, sp, piece, src):
        e, c = piece
        if not isinstance(e, int) or PER_EXPERT * e + c >= E_RAW:
            sp.wait_ge(*self.low(e * PER_EXPERT + (c - E_RAW + 1)))
        sp.dma_start(self.raw[:, c % E_RAW, :], src).then_inc(self.full[c % E_RAW].sem, 16)

    def split_high(self, act, piece):
        e, c = piece
        act.wait_ge(*self.full[c % E_RAW](e * (16 * (PER_EXPERT // E_RAW)) + 16 * (c // E_RAW + 1)))
        if not isinstance(e, int) or PER_EXPERT * e + c >= E_PARTS:
            act.wait_ge(*self.used(e * PER_EXPERT + (c - E_PARTS + 1)))
        self.core.nc.scalar.activation(self.hi[:, c % E_PARTS, :], self.raw[:, c % E_RAW, :], ACT.Copy).then_inc(self.high.sem, 1)

    def split_low(self, dve, piece):
        e, c = piece
        dve.wait_ge(*self.high(e * PER_EXPERT + (c + 1)))
        if not isinstance(e, int) or PER_EXPERT * e + c >= E_PARTS:
            dve.wait_ge(*self.used(e * PER_EXPERT + (c - E_PARTS + 1)))
        self.core.nc.vector.tensor_tensor(self.lo[:, c % E_PARTS, :], self.raw[:, c % E_RAW, :], self.hi[:, c % E_PARTS, :], ALU.subtract).then_inc(self.low.sem, 1)

    def through(self, piece, k=0):
        e, c = piece
        return e * PER_EXPERT + (c + k + 1)

    def parts(self, piece, half):
        c = piece[1]
        return [part[:, c % E_PARTS, half * BANK:(half + 1) * BANK] for part in (self.hi, self.lo)]


def routing_stages(core, W, moe, hT, ctx):
    nc = core.nc
    sb = lambda name, shape, dtype=F32: core.sb(name, shape, dtype, ctx=ctx)
    wr, br = sb("w_router", [P, KD, E]), sb("b_router", [P, E])
    before, iota, tok = sb("before", [P, P]), sb("iota", [P, ROWS]), sb("tok", [P, T])
    ones, zeros = sb("ones", [P, P]), sb("zeros", [P, P])
    lg, top, topi, topf = sb("logits", [P, T, E]), sb("top", [P, T, 8]), sb("top_i", [P, T, 8], U32), sb("top_f", [P, T, 8])
    low, den, eg = sb("neg_top", [P, T]), sb("gate_sum", [P, T]), sb("gate_exp", [P, T, TOP_E])
    hot, mask = sb("one_hot", [P, T, TOP_E, E]), sb("chosen", [P, T, E])
    place, count = sb("place", [P, T, TOP_E], U32), sb("count", [P, E])
    placef, slotf, rankf, scratch = sb("place_f", [P, T, TOP_E]), sb("slot_f", [P, T, TOP_E]), sb("rank_f", [P, T, TOP_E]), sb("route_tmp", [P, E])
    tokens = sb("table_rows", [P, CAP])
    load_stage(core, [(wr[:], W["w_router"][0].rearrange("(k p) n -> p k n", p=P)), (br[:], W["b_router"][0].partition_broadcast(P)),
                      (before[:], W["before"]), (iota[:], W["iota"]), (tok[:], W["tok"])], "router_loads")
    logits, best, exps, chosen, ranks, slots_ready = (core.event(s) for s in ("logits", "best", "gate_exps", "chosen", "ranks", "slots_ready"))
    cleared, scattered, table_in = core.event("table_cleared"), core.event("table_scattered"), core.event("table_in")
    table_turned, spread_ready = core.event("table_turned"), core.event("zeros_ready")
    chains = []
    with nc.Block() as block:
        @block.sync
        def _(sp):
            for k in range(E_RAW):
                moe.load(sp, moe.first_piece(0, k), moe.first_src(W, 0, k))

        @block.tensor
        def _(pe):
            for t in range(T):
                for k in range(KD):
                    last = nc.tensor.matmul(core.psum[:, t, 0:E], hT[:, k, t * P:(t + 1) * P], wr[:, k, :], start=(k == 0), stop=(k == KD - 1))
                last.then_inc(logits.sem, 1)
            pe.wait_ge(*chosen(1))
            for t in range(T):
                for s in range(t):
                    nc.tensor.matmul(core.psum[:, 4 + t, 0:E], ones[:], mask[:, s, :], start=(s == 0), stop=False)
                nc.tensor.matmul(core.psum[:, 4 + t, 0:E], before[:], mask[:, t, :], start=(t == 0), stop=True)
            for t in range(T):
                last = nc.tensor.matmul(core.psum[:, 0, 0:E], ones[:], mask[:, t, :], start=(t == 0), stop=(t == T - 1))
            last.then_inc(ranks.sem, 1)
            pe.wait_ge(*table_in(16))
            nc.tensor.transpose(core.psum[:, 1, 0:P], tokens[:], core.ident[:]).then_inc(table_turned.sem, 1)

        @block.scalar
        def _(act):
            act.wait_ge(*spread_ready(1))
            act.dma_start(moe.table.rearrange("(p n) o -> p (n o)", p=P), zeros[:]).then_inc(cleared.sem, 16)
            for t in range(T):
                act.wait_ge(*best(t + 1))
                nc.scalar.activation(eg[:, t, :], top[:, t, 0:TOP_E], ACT.Exp, bias=low[:, t:t + 1], accum_out=den[:, t:t + 1]).then_inc(exps.sem, 1)

        @block.vector
        def _(dve):
            step = core.step("dve_step", dve, chains)
            nc.vector.memset(ones[:], 1.0)
            nc.vector.memset(zeros[:], 0.0).then_inc(spread_ready.sem, 1)
            for t in range(T):
                dve.wait_ge(*logits(t + 1))
                step(nc.vector.tensor_tensor(lg[:, t, :], core.psum[:, t, 0:E], br[:], ALU.add))
                step(nc.vector.max(top[:, t, :], lg[:, t, :]))
                step(nc.vector.max_index(topi[:, t, :], top[:, t, :], lg[:, t, :]))
                nc.vector.tensor_scalar(low[:, t:t + 1], top[:, t, 0:1], -1.0, None, ALU.mult).then_inc(best.sem, 1)
                step(nc.vector.tensor_copy(topf[:, t, :], topi[:, t, :]))
                for j in range(TOP_E):
                    step(nc.vector.tensor_scalar(hot[:, t, j, :], iota[:, 0:E], topf[:, t, j:j + 1], None, ALU.is_equal))
                step(nc.vector.tensor_tensor(mask[:, t, :], hot[:, t, 0, :], hot[:, t, 1, :], ALU.add))
                for j in range(2, TOP_E):
                    step(nc.vector.tensor_tensor(mask[:, t, :], mask[:, t, :], hot[:, t, j, :], ALU.add))
            dve.sem_inc(chosen.sem, 1)
            dve.wait_ge(*exps(T))
            step(nc.vector.reciprocal(den[:], den[:]))
            for t in range(T):
                step(nc.vector.tensor_scalar(moe.gate[:, t, :], eg[:, t, :], den[:, t:t + 1], None, ALU.mult))
                step(nc.vector.tensor_scalar(moe.spread[:, t, :], hot[:, t, 0, :], moe.gate[:, t, 0:1], None, ALU.mult))
                for j in range(1, TOP_E):
                    step(nc.vector.scalar_tensor_tensor(out=moe.spread[:, t, :], in0=hot[:, t, j, :], scalar=moe.gate[:, t, j:j + 1], in1=moe.spread[:, t, :], op0=ALU.mult, op1=ALU.add))
            dve.wait_ge(*ranks(1))
            step(nc.vector.tensor_reduce(count[:, 0:1], core.psum[:, 0, 0:E], AX.X, ALU.max))
            step(nc.vector.tensor_scalar(count[:, 1:2], count[:, 0:1], float(CAP), None, ALU.is_gt))
            nc.vector.tensor_copy(moe.flag[0:1, 0:1], count[0:1, 1:2])
            for t in range(T):
                step(nc.vector.tensor_copy(moe.rank[:, t, :], core.psum[:, 4 + t, 0:E]))
                for j in range(TOP_E):
                    step(nc.vector.tensor_tensor(scratch[:], moe.rank[:, t, :], hot[:, t, j, :], ALU.mult))
                    step(nc.vector.tensor_reduce(rankf[:, t, j:j + 1], scratch[:], AX.X, ALU.add))
            step(nc.vector.tensor_copy(slotf[:], topf[:, :, 0:TOP_E]))
            step(nc.vector.scalar_tensor_tensor(out=placef[:], in0=slotf[:], scalar=float(ROWS), in1=rankf[:], op0=ALU.mult, op1=ALU.add))
            step(nc.vector.tensor_copy(place[:], placef[:]))
            dve.sem_inc(slots_ready.sem, 1)
            step(nc.vector.tensor_scalar(placef[:], rankf[:], float(CAP), None, ALU.is_lt))
            step(nc.vector.tensor_tensor(moe.gate[:], moe.gate[:], placef[:], ALU.mult))
            step(nc.vector.tensor_tensor(rankf[:], rankf[:], placef[:], ALU.mult))
            step(nc.vector.scalar_tensor_tensor(out=slotf[:], in0=slotf[:], scalar=float(CAP), in1=rankf[:], op0=ALU.mult, op1=ALU.add))
            step(nc.vector.tensor_copy(moe.slot[:], slotf[:]))
            dve.wait_ge(*table_turned(1))
            nc.vector.tensor_copy(moe.index[:], core.psum[:, 1, 0:P])

        @block.gpsimd
        def _(pool):
            pool.wait_ge(*slots_ready(1))
            pool.wait_ge(*cleared(16))
            for t in range(T):
                for j in range(TOP_E):
                    pool.indirect_dma_start(moe.table, bass.IndirectOffsetOnAxis(place[:, t, j:j + 1], 0), tok[:, t:t + 1], None).then_inc(scattered.sem, 16)
            pool.wait_ge(*scattered(16 * T * TOP_E))
            pool.dma_start(tokens[:], moe.table.rearrange("(r n) o -> r (n o)", n=CAP)).then_inc(table_in.sem, 16)
    for s, n in ((logits, T), (best, T), (exps, T), (chosen, 1), (ranks, 1), (slots_ready, 1), (cleared, 16), (scattered, 16 * T * TOP_E), (table_in, 16), (table_turned, 1), (spread_ready, 1)):
        s.passed(n)
    close(chains)


def experts_stage(core, W, moe):
    nc = core.nc
    names = ("index_ready", "x_turned", "xT_high", "xT_low", "hidden_taken", "glu_ready", "sigmoid_ready", "pre_act", "act_ready",
             "act_turned", "actT_high", "actT_low", "y_taken", "expert_chosen", "y_stored")
    index_ready, x_turned, xT_high, xT_low, hidden_taken, glu_ready, sigmoid_ready, pre_act, act_ready, act_turned, actT_high, actT_low, y_taken, expert_chosen, stored = (core.event(n) for n in names)
    gathered = [core.event(f"x_gathered{q}") for q in range(2)]
    begun, b1_full, b1_high, b1_low = core.event("gather_begun"), core.event("b1_full"), core.event("b1_high"), core.event("b1_low")
    last_first, last_second = W1_PIECES - 1, W2_PIECES - 1
    with ExitStack() as ctx:
        sb = lambda name, shape, dtype=F32: core.sb(name, shape, dtype, ctx=ctx)
        moe.hi, moe.lo = (sb(n, [P, E_PARTS, PIECE], F32R) for n in ("weights_high", "weights_low"))
        xg = sb("x_rows", [P, 2, D])
        xT = [sb(n, [P, KD, P], F32R) for n in ("xT_high", "xT_low")]
        actT = [sb(n, [P, F // P, P], F32R) for n in ("actT_high", "actT_low")]
        b1 = [sb(n, [E, 2 * F], F32R) for n in ("b1_high", "b1_low")]
        hid, sg, act_sb, y = sb("hidden", [P, 2, F]), sb("sigmoid", [P, F]), sb("act", [P, F]), sb("y", [P, D])
        idx, chosen = [sb(f"index_now{q}", [P, 1], I32) for q in range(2)], sb("expert_row", [E, P], F32R)
        glu, lin = hid[:, 0, :], hid[:, 1, :]
        b1_raw = hid[0:E].rearrange("e two n -> e (two n)")
        banks = core.psum
        pair = banks[:, 0:4, :].rearrange("p b n -> p (b n)").rearrange("p (n two) -> p two n", two=2)
        turned_banks = banks[:, 4:6, :].rearrange("p b (k n) -> p (b k) n", n=P)

        with nc.Block() as block:
            @block.sync
            def _(sp):
                sp.dma_start(b1_raw, W["b_mlp1"][0]).then_inc(b1_full.sem, 16)
                for k in range(E_RAW, W1_PIECES):
                    moe.load(sp, moe.first_piece(0, k), moe.first_src(W, 0, k))
                with sp.Fori(1, E) as e:
                    for k in range(W1_PIECES):
                        moe.load(sp, moe.first_piece(e, k), moe.first_src(W, e, k))
                    for k in range(W2_PIECES):
                        moe.load(sp, moe.second_piece(e - 1, k), moe.second_src(W, e - 1, k))
                for k in range(W2_PIECES):
                    moe.load(sp, moe.second_piece(E - 1, k), moe.second_src(W, E - 1, k))

            @block.gpsimd
            def _(pool):
                def gather(e, q, reused):
                    pool.wait_ge(*index_ready(e + 1))
                    if reused:
                        pool.wait_ge(*x_turned(e - 1))
                    pool.sem_inc(begun.sem, 1)
                    pool.indirect_dma_start(xg[:, q, :], None, moe.h2, bass.IndirectOffsetOnAxis(idx[q][:].bitcast(U32), 0)).then_inc(gathered[q].sem, 16)

                gather(0, 0, False)
                gather(1, 1, False)
                with pool.Fori(1, E // 2) as i:
                    gather(2 * i, 0, True)
                    gather(2 * i + 1, 1, True)

            @block.tensor
            def _(pe):
                def turn_x(e, q, h, act_done):
                    pe.wait_ge(*gathered[q](16 * (h + 1)))
                    if act_done is not None:
                        pe.wait_ge(*actT_low(act_done))
                    for k in range(KD):
                        last = nc.tensor.transpose(banks[:, 4 + k // 4, (k % 4) * P:(k % 4 + 1) * P], xg[:, q, k * P:(k + 1) * P], core.ident[:])
                    last.then_inc(x_turned.sem, 1)

                def hidden(e, first):
                    pe.wait_ge(*expert_chosen(e + 1))
                    if not first:
                        pe.wait_ge(*hidden_taken(e))
                    for n in range(4):
                        cols = slice(n * BANK, (n + 1) * BANK)
                        nc.tensor.matmul(banks[:, n, :], chosen[:], b1[0][:, cols], start=True, stop=False)
                        nc.tensor.matmul(banks[:, n, :], chosen[:], b1[1][:, cols], start=False, stop=False)
                    pe.wait_ge(*xT_low(e + 1))
                    for k in range(W1_PIECES):
                        piece = moe.first_piece(e, k)
                        pe.wait_ge(*moe.low(moe.through(piece)))
                        for n in range(2):
                            last = product_in_parts(nc, banks[:, 2 * (k % 2) + n, :], [part[:, k // 2, :] for part in xT], moe.parts(piece, n), False, k >= W1_PIECES - 2)
                        last.then_inc(moe.used.sem, 1)

                def output(e, first):
                    pe.wait_ge(*actT_low(e + 1))
                    if not first:
                        pe.wait_ge(*y_taken(e))
                    for k in range(W2_PIECES):
                        piece = moe.second_piece(e, k)
                        pe.wait_ge(*moe.low(moe.through(piece)))
                        for n in range(2):
                            last = product_in_parts(nc, banks[:, 6 + n, :], [part[:, k, :] for part in actT], moe.parts(piece, n), k == 0, k == W2_PIECES - 1)
                        last.then_inc(moe.used.sem, 1)

                def turn_act(e, x_done):
                    pe.wait_ge(*act_ready(e + 1))
                    pe.wait_ge(*xT_low(x_done))
                    for k in range(F // P):
                        last = nc.tensor.transpose(banks[:, 4 + k // 4, (k % 4) * P:(k % 4 + 1) * P], act_sb[:, k * P:(k + 1) * P], core.ident[:])
                    last.then_inc(act_turned.sem, 1)

                def body(e, q, h, first=False):
                    hidden(e, False)
                    turn_x(e + 1, 1 - q, h + (1 if q else 0), e)
                    output(e - 1, first)
                    turn_act(e, e + 2)

                turn_x(0, 0, 0, None)
                pe.wait_ge(*b1_low(1))
                hidden(0, True)
                turn_x(1, 1, 0, None)
                turn_act(0, 2)
                body(1, 1, 0, True)
                body(2, 0, 1)
                with pe.Fori(1, (E - 2) // 2) as i:
                    body(2 * i + 1, 1, i)
                    body(2 * i + 2, 0, i + 1)
                hidden(E - 1, False)
                output(E - 2, False)
                turn_act(E - 1, E)
                output(E - 1, False)

            @block.scalar
            def _(act):
                def copy_x(e, hidden_done):
                    act.wait_ge(*x_turned(e + 1))
                    if hidden_done is not None:
                        act.wait_ge(*moe.used(hidden_done))
                    nc.scalar.activation(xT[0][:], turned_banks, ACT.Copy).then_inc(xT_high.sem, 1)

                def copy_y(e, reused):
                    act.wait_ge(*moe.used(moe.through(moe.second_piece(e, last_second))))
                    if reused:
                        act.wait_ge(*stored(16 * e))
                    nc.scalar.activation(y[:], banks[:, 6:8, :].rearrange("p b n -> p (b n)"), ACT.Copy).then_inc(y_taken.sem, 1)
                    act.wait_ge(*y_taken(e + 1))
                    act.dma_start(moe.slots[bass.ds(e * CAP, CAP), :], y[:]).then_inc(stored.sem, 16)

                def body(e, last=False, reused=True, output=True):
                    for k in range(W1_PIECES - E_PARTS, W1_PIECES):
                        moe.split_high(act, moe.first_piece(e, k))
                    for k in range(W2_PIECES if output else 0):
                        moe.split_high(act, moe.second_piece(e - 1, k))
                    hidden_done = moe.through(moe.first_piece(e, last_first))
                    if not last:
                        copy_x(e + 1, hidden_done)
                    act.wait_ge(*glu_ready(e + 1))
                    nc.scalar.activation(sg[:], glu, ACT.Sigmoid, scale=1.702).then_inc(sigmoid_ready.sem, 1)
                    for k in range(E_PARTS):
                        moe.split_high(act, (e + 1, k - W2_PIECES))
                    act.wait_ge(*act_turned(e + 1))
                    if output:
                        act.wait_ge(*moe.used(moe.through(moe.second_piece(e - 1, last_second))))
                    nc.scalar.activation(actT[0][:], turned_banks, ACT.Copy).then_inc(actT_high.sem, 1)
                    if output:
                        copy_y(e - 1, reused)

                act.wait_ge(*b1_full(16))
                nc.scalar.activation(b1[0][:], b1_raw, ACT.Copy).then_inc(b1_high.sem, 1)
                copy_x(0, None)
                for k in range(E_PARTS):
                    moe.split_high(act, moe.first_piece(0, k))
                body(0, output=False)
                body(1, reused=False)
                body(2)
                with act.Fori(3, E - 1) as e:
                    body(e)
                body(E - 1, last=True)
                copy_y(E - 1, True)
                act.wait_ge(*stored(16 * E))

            @block.vector
            def _(dve):
                def index(e, q, h, reused):
                    if reused:
                        dve.wait_ge(*gathered[q](16 * h))
                    nc.vector.tensor_scalar(idx[q][:], moe.index[:, bass.ds(e * BLOCKS, 1)], 0, None, ALU.add).then_inc(index_ready.sem, 1)

                def choose(e):
                    nc.vector.tensor_scalar(chosen[:], core.ident[0:E, bass.ds(e, 1)].broadcast_to([E, P]), 0.0, None, ALU.add).then_inc(expert_chosen.sem, 1)

                def low_x(e):
                    dve.wait_ge(*xT_high(e + 1))
                    nc.vector.tensor_tensor(xT[1][:], turned_banks, xT[0][:], ALU.subtract).then_inc(xT_low.sem, 1)

                def body(e, q, h, last=False, output=True):
                    if not last and output:
                        index(e + 1, 1 - q, h + (1 if q else 0), True)
                    for k in range(W1_PIECES - E_PARTS, W1_PIECES):
                        moe.split_low(dve, moe.first_piece(e, k))
                    for k in range(W2_PIECES if output else 0):
                        moe.split_low(dve, moe.second_piece(e - 1, k))
                    dve.wait_ge(*moe.used(moe.through(moe.first_piece(e, last_first))))
                    nc.vector.tensor_scalar(glu, pair[:, 0, :], 7.0, None, ALU.min).then_inc(glu_ready.sem, 1)
                    nc.vector.tensor_scalar(lin, pair[:, 1, :], 7.0, -7.0, ALU.min, ALU.max).then_inc(hidden_taken.sem, 1)
                    if not last:
                        low_x(e + 1)
                        choose(e + 1)
                    for k in range(2):
                        moe.split_low(dve, (e + 1, k - W2_PIECES))
                    dve.wait_ge(*hidden_taken(e + 1))
                    dve.wait_ge(*glu_ready(e + 1))
                    if output:
                        dve.wait_ge(*act_turned(e))
                    nc.vector.scalar_tensor_tensor(out=act_sb[:], in0=lin, scalar=1.0, in1=glu, op0=ALU.add, op1=ALU.mult).then_inc(pre_act.sem, 1)
                    moe.split_low(dve, (e + 1, 2 - W2_PIECES))
                    dve.wait_ge(*pre_act(e + 1))
                    dve.wait_ge(*sigmoid_ready(e + 1))
                    nc.vector.tensor_tensor(act_sb[:], act_sb[:], sg[:], ALU.mult).then_inc(act_ready.sem, 1)
                    for k in range(3, E_PARTS):
                        moe.split_low(dve, (e + 1, k - W2_PIECES))
                    dve.wait_ge(*actT_high(e + 1))
                    nc.vector.tensor_tensor(actT[1][:], turned_banks, actT[0][:], ALU.subtract).then_inc(actT_low.sem, 1)

                index(0, 0, 0, False)
                index(1, 1, 0, False)
                choose(0)
                dve.wait_ge(*b1_high(1))
                nc.vector.tensor_tensor(b1[1][:], b1_raw, b1[0][:], ALU.subtract).then_inc(b1_low.sem, 1)
                dve.wait_ge(*b1_low(1))
                low_x(0)
                for k in range(E_PARTS):
                    moe.split_low(dve, moe.first_piece(0, k))
                body(0, 0, 0, output=False)
                body(1, 1, 0)
                body(2, 0, 1)
                with dve.Fori(1, (E - 2) // 2) as i:
                    body(2 * i + 1, 1, i)
                    body(2 * i + 2, 0, i + 1)
                body(E - 1, 1, (E - 1) // 2, last=True)
    for s in (index_ready, x_turned, xT_high, xT_low, hidden_taken, glu_ready, sigmoid_ready, pre_act, act_ready, act_turned, actT_high, actT_low, y_taken, expert_chosen):
        s.passed(E)
    for s in (moe.high, moe.low, moe.used):
        s.passed(PER_EXPERT * E)
    for s in moe.full:
        s.passed(16 * PER_EXPERT * E // E_RAW)
    for s in gathered:
        s.passed(16 * E // 2)
    stored.passed(16 * E); b1_full.passed(16); b1_high.passed(1); b1_low.passed(1); begun.passed(E)


def more_blocks_stage(core, W, moe, more):
    nc = core.nc
    names = ("more_weights", "more_index", "more_rows", "more_turned", "more_copied", "more_hidden", "more_act", "more_out", "more_y", "more_sigmoid", "more_gates_made", "more_gates_turned", "more_spread")
    signals = [core.event(n) for n in names]
    signals.remove(core.event("more_rows"))
    rows = core.event("more_rows")
    weights, index, turned, copied, hidden, acted, product, y_ready, sigmoid, gates_made, gates_turned, spread = signals
    banks = core.psum
    with ExitStack() as ctx:
        sb = lambda name, shape, dtype=F32: core.sb(name, shape, dtype, ctx=ctx)
        xg, xT, hid, sg, act_sb = sb("more_x", [P, D]), sb("more_xT", [P, KD, P]), sb("more_hid", [P, 2 * F]), sb("more_sg", [P, F]), sb("more_act", [P, F])
        w1, idx = sb("more_w1", [P, KD, 2 * F]), sb("more_idx", [P, 1], I32)
        w2, b1 = moe.raw[:, 0:W2_PIECES, :], moe.raw[:, W2_PIECES:W2_PIECES + 2, :].rearrange("p r n -> p (r n)")
        iota, gates, gT = sb("more_iota", [P, S]), sb("more_gates", [P, T, P]), sb("more_gatesT", [P, T, P])
        with nc.Block() as block:
            @block.vector
            def _(dve):
                nc.vector.memset(more[:], 0.0)
        load_stage(core, [(iota[:], W["iota"])], "more_loads")
        glu = hid[:].rearrange("p (n two) -> p two n", two=2)[:, 0, :]
        lin = hid[:].rearrange("p (n two) -> p two n", two=2)[:, 1, :]
        flag = nc.values_load(moe.flag[0:1, 0:1], min_val=0, max_val=1)
        with nc.If(flag > 0):
            with nc.Fori(0, E) as e:
                with nc.Block() as block:
                    @block.sync
                    def _(sp):
                        sp.dma_start(w1[:], W["w_mlp1"][0, e].rearrange("(k p) n -> p k n", p=P)).then_inc(weights.sem, 16)
                        sp.dma_start(w2, W["w_mlp2"][0, e].rearrange("(k p) n -> p k n", p=P)).then_inc(weights.sem, 16)
                        sp.dma_start(b1, W["b_mlp1"][0, e].partition_broadcast(P)).then_inc(weights.sem, 16)
                        sp.wait_ge(*weights(48))
                for b in range(1, BLOCKS):
                    with nc.Block() as block:
                        @block.gpsimd
                        def _(pool):
                            pool.wait_ge(*index(1))
                            pool.indirect_dma_start(xg[:], None, moe.h2, bass.IndirectOffsetOnAxis(idx[:].bitcast(U32), 0)).then_inc(rows.sem, 16)

                        @block.tensor
                        def _(pe):
                            pe.wait_ge(*rows(e * (16 * (BLOCKS - 1)) + 16 * b))
                            for k in range(KD):
                                last = nc.tensor.transpose(banks[:, 4 + k // 4, (k % 4) * P:(k % 4 + 1) * P], xg[:, k * P:(k + 1) * P], core.ident[:])
                            last.then_inc(turned.sem, 1)
                            pe.wait_ge(*copied(1))
                            for k in range(KD):
                                for n in range(4):
                                    last = nc.tensor.matmul(banks[:, n, :], xT[:, k, :], w1[:, k, n * BANK:(n + 1) * BANK], start=(k == 0), stop=(k == KD - 1))
                            last.then_inc(product.sem, 1)
                            pe.wait_ge(*acted(2))
                            for k in range(KD):
                                last = nc.tensor.transpose(banks[:, 4 + k // 4, (k % 4) * P:(k % 4 + 1) * P], act_sb[:, k * P:(k + 1) * P], core.ident[:])
                            last.then_inc(turned.sem, 1)
                            pe.wait_ge(*copied(2))
                            for k in range(KD):
                                for n in range(2):
                                    last = nc.tensor.matmul(banks[:, 6 + n, :], xT[:, k, :], w2[:, k, n * BANK:(n + 1) * BANK], start=(k == 0), stop=(k == KD - 1))
                            last.then_inc(product.sem, 1)
                            pe.wait_ge(*gates_made(1))
                            for t in range(T):
                                last = nc.tensor.transpose(banks[:, 0, t * P:(t + 1) * P], gates[:, t, :], core.ident[:])
                            last.then_inc(turned.sem, 1)
                            pe.wait_ge(*gates_turned(1))
                            pe.wait_ge(*y_ready(1))
                            for t in range(T):
                                if t == 2:
                                    pe.wait_ge(*spread(2))
                                for n in range(2):
                                    last = nc.tensor.matmul(banks[:, 2 + 2 * (t % 2) + n, :], gT[:, t, :], xg[:, n * BANK:(n + 1) * BANK], start=True, stop=True)
                                last.then_inc(product.sem, 1)

                        @block.scalar
                        def _(act):
                            def copy(n, to):
                                act.wait_ge(*turned(n))
                                for j in range(2):
                                    last = nc.scalar.activation(to[:, 4 * j:4 * j + 4, :], banks[:, 4 + j, :].rearrange("p (k n) -> p k n", k=4), ACT.Copy)
                                last.then_inc(copied.sem, 1)

                            copy(1, xT)
                            act.wait_ge(*hidden(2))
                            nc.scalar.activation(sg[:], glu, ACT.Sigmoid, scale=1.702).then_inc(sigmoid.sem, 1)
                            copy(2, xT)
                            act.wait_ge(*product(2))
                            for j in range(2):
                                last = nc.scalar.activation(xg[:, j * BANK:(j + 1) * BANK], banks[:, 6 + j, :], ACT.Copy)
                            last.then_inc(y_ready.sem, 1)
                            act.wait_ge(*turned(3))
                            nc.scalar.activation(gT[:].rearrange("p t n -> p (t n)"), banks[:, 0, :], ACT.Copy).then_inc(gates_turned.sem, 1)

                        @block.vector
                        def _(dve):
                            nc.vector.tensor_scalar(idx[:], moe.index[:, bass.ds(e * BLOCKS + b, 1)], 0, None, ALU.add).then_inc(index.sem, 1)
                            dve.wait_ge(*product(1))
                            nc.vector.tensor_tensor(hid[:], banks[:, 0:4, :].rearrange("p b n -> p (b n)"), b1, ALU.add).then_inc(hidden.sem, 1)
                            dve.wait_ge(*hidden(1))
                            nc.vector.tensor_scalar(glu, glu, 7.0, None, ALU.min).then_inc(hidden.sem, 1)
                            nc.vector.tensor_scalar(lin, lin, 7.0, -7.0, ALU.min, ALU.max).then_inc(hidden.sem, 1)
                            dve.wait_ge(*hidden(3))
                            nc.vector.scalar_tensor_tensor(out=act_sb[:], in0=lin, scalar=1.0, in1=glu, op0=ALU.add, op1=ALU.mult).then_inc(acted.sem, 1)
                            dve.wait_ge(*acted(1))
                            dve.wait_ge(*sigmoid(1))
                            nc.vector.tensor_tensor(act_sb[:], act_sb[:], sg[:], ALU.mult).then_inc(acted.sem, 1)
                            for t in range(T):
                                last = nc.vector.tensor_scalar(gates[:, t, :], iota[:, b * CAP:(b + 1) * CAP], moe.rank[:, t, bass.ds(e, 1)], moe.spread[:, t, bass.ds(e, 1)], ALU.is_equal, ALU.mult)
                            last.then_inc(gates_made.sem, 1)
                            for t in range(T):
                                dve.wait_ge(*product(3 + t))
                                bank = 2 + 2 * (t % 2)
                                nc.vector.tensor_tensor(more[:, t, :], more[:, t, :], banks[:, bank:bank + 2, :].rearrange("p b n -> p (b n)"), ALU.add).then_inc(spread.sem, 1)
                    gates_made.passed(1); gates_turned.passed(1); spread.passed(T)
                    index.passed(1); turned.passed(3); copied.passed(2); product.passed(2 + T); acted.passed(2)
                    hidden.passed(3); sigmoid.passed(1); y_ready.passed(1)
                with nc.Block() as block:
                    @block.gpsimd
                    def _(pool):
                        for s in signals:
                            pool.sem_clear(s.sem)
                for s in signals:
                    s.base = 0


def combine_stage(core, W, moe, ffn):
    nc = core.nc
    turned, taken, bias, bias_taken = core.event("turned"), core.event("gates_turned"), core.event("bias_product"), core.event("bias_taken")
    fetched = [core.event(f"row_fetched{i}") for i in range(4)]
    added = core.event("rows_added")
    with ExitStack() as ctx:
        rows = core.sb("slot_rows", [P, 4, D], ctx=ctx)
        b2 = core.sb("b_mlp2", [E, D], ctx=ctx)
        gT = core.sb("gatesT", [E, T, P], ctx=ctx)
        load_stage(core, [(b2[:], W["b_mlp2"][0])], "b_mlp2_load")
        with nc.Block() as block:
            @block.gpsimd
            def _(pool):
                for i in range(T * TOP_E):
                    t, j = i // TOP_E, i % TOP_E
                    if i >= 4:
                        pool.wait_ge(*added(i - 3))
                    pool.indirect_dma_start(rows[:, i % 4, :], None, moe.slots, bass.IndirectOffsetOnAxis(moe.slot[:, t, j:j + 1], 0)).then_inc(fetched[i % 4].sem, 16)

            @block.tensor
            def _(pe):
                for t in range(T):
                    last = nc.tensor.transpose(core.psum[0:E, 0, t * P:(t + 1) * P], moe.spread[:, t, :], core.ident[:])
                last.then_inc(turned.sem, 1)
                pe.wait_ge(*taken(1))
                for t in range(T):
                    if t == 3:
                        pe.wait_ge(*bias_taken(1))
                    for n in range(2):
                        last = nc.tensor.matmul(core.psum[:, 2 + 2 * (t % 3) + n, :], gT[:, t, :], b2[:, n * BANK:(n + 1) * BANK], start=True, stop=True)
                    last.then_inc(bias.sem, 1)

            @block.scalar
            def _(act):
                act.wait_ge(*turned(1))
                nc.scalar.activation(gT[:].rearrange("e t p -> e (t p)"), core.psum[0:E, 0, :], ACT.Copy).then_inc(taken.sem, 1)

            @block.vector
            def _(dve):
                for i in range(T * TOP_E):
                    t, j = i // TOP_E, i % TOP_E
                    dve.wait_ge(*fetched[i % 4](16 * (i // 4 + 1)))
                    if j == 0:
                        dve.wait_ge(*bias(t + 1))
                        b = 2 + 2 * (t % 3)
                        nc.vector.tensor_tensor(ffn[:, t, :], ffn[:, t, :], core.psum[:, b:b + 2, :].rearrange("p b n -> p (b n)"), ALU.add).then_inc(bias_taken.sem, 1)
                        dve.wait_ge(*bias_taken(t + 1))
                    if j:
                        dve.wait_ge(*added(i))
                    nc.vector.scalar_tensor_tensor(out=ffn[:, t, :], in0=rows[:, i % 4, :], scalar=moe.gate[:, t, j:j + 1], in1=ffn[:, t, :], op0=ALU.mult, op1=ALU.add).then_inc(added.sem, 1)
    turned.passed(1); taken.passed(1); bias.passed(T); bias_taken.passed(T); added.passed(T * TOP_E)
    for s in fetched:
        s.passed(16 * T)


def first_ffn(core, W, x, moe, mod, gate):
    part = [mod[:, n * D:(n + 1) * D] for n in range(5)]
    with ExitStack() as inner:
        h2 = core.sb("h2", [P, T, D], ctx=inner)
        hT = core.sb("h2T", [P, KD, S], ctx=inner)
        norm_stage(core, x, part[4], part[3], h2, hT, moe.h2)
        routing_stages(core, W, moe, hT, inner)


def experts_part(core, W, x, moe, gate):
    experts_stage(core, W, moe)
    with ExitStack() as inner:
        ffn = core.sb("ffn", [P, T, D], ctx=inner)
        more_blocks_stage(core, W, moe, ffn)
        combine_stage(core, W, moe, ffn)
        residual_stage(core, x, ffn, gate)


GROUPS = 4
OFF2 = [GW * i for i in range(7)] + [6 * GW + AW, 6 * GW + 2 * AW]
TABLES = 4
LEVELS = 7


def clear_stage(core, signals):
    nc = core.nc
    with nc.Block() as block:
        @block.gpsimd
        def _(pool):
            for s in signals:
                pool.sem_clear(s.sem)
    for s in signals:
        s.base = 0


def lower_bounds_stage(core, raw, lb):
    nc, largest, exps = core.nc, core.event("lb_max"), core.event("lb_exps")
    chains = []
    with ExitStack() as ctx:
        top = core.sb("lb_top", [P, GROUPS], ctx=ctx)
        total = core.sb("lb_total", [P, GROUPS], ctx=ctx)
        with nc.Block() as block:
            @block.vector
            def _(dve):
                step = core.step("dve_step", dve, chains)
                step(nc.vector.tensor_tensor(top[:], raw[:, 0, :], raw[:, 1, :], ALU.max))
                nc.vector.tensor_tensor(raw[:, 0, :], raw[:, 0, :], top[:], ALU.subtract)
                nc.vector.tensor_tensor(raw[:, 1, :], raw[:, 1, :], top[:], ALU.subtract).then_inc(largest.sem, 1)
                dve.wait_ge(*exps(1))
                step(nc.vector.tensor_tensor(total[:], raw[:, 0, :], raw[:, 1, :], ALU.add))
                step(nc.vector.reciprocal(total[:], total[:]))
                nc.vector.tensor_tensor(raw[:, 0, :], raw[:, 0, :], total[:], ALU.mult)
                step(nc.vector.tensor_tensor(raw[:, 1, :], raw[:, 1, :], total[:], ALU.mult))
                nc.vector.tensor_tensor(lb[:, 0, :], raw[:, 0, :], raw[:, 0, :], ALU.subtract)
                step(nc.vector.tensor_tensor(top[:], raw[:, 0, :], raw[:, 1, :], ALU.add))
                nc.vector.tensor_tensor(lb[:, 1, :], top[:], raw[:, 0, :], ALU.subtract)

            @block.scalar
            def _(act):
                act.wait_ge(*largest(1))
                nc.scalar.activation(raw[:], raw[:], ACT.Exp).then_inc(exps.sem, 1)
    largest.passed(1); exps.passed(1)
    close(chains)


def recurrence_stages(core, W, proj, mixed, hT, lb, layer, ahead):
    nc = core.nc
    qT, kT = hT[:, 0:GROUPS, :], hT[:, GROUPS:2 * GROUPS, :]
    with ExitStack() as ctx:
        sb = lambda name, shape, dtype=F32: core.sb(name, shape, dtype, ctx=ctx)
        bT, vrev = sb("log_sum", [P, GROUPS, S]), sb("v_reversed", [P, T, GW])
        split, heads2, flip = sb("split", [P, 8, P], I32), sb("heads2", [P, P]), sb("flip", [P, P])
        lbn, omlb, scan = sb("lb_now", [P, GROUPS]), sb("one_less_lb", [P, GROUPS]), sb("scan_mask", [P, S])
        load_stage(core, [(split[:], W["split"].rearrange("p (n m) -> p n m", n=8)), (heads2[:], W["heads2"]), (flip[:], W["flip"])], "recurrence_loads", ahead)
        turns = []
        for src, to in ((0, qT), (None, kT)):
            for d in range(2):
                off = OFF2[0] if src == 0 else OFF2[2 + d]
                for pair in range(2):
                    tiles = range(T) if d == 0 else range(T - 1, -1, -1)
                    turns.append((to[:, 2 * d + pair, :], [proj[:, t, off + pair * P:off + (pair + 1) * P] for t in tiles], flip if d else core.ident))
        turn_stage(core, turns)
        capped, exps, f_ready, logs, reversed_, sig = (core.event(n) for n in ("z_capped", "z_exps", "f_ready", "f_logs", "v_flipped", "q_sigmoid"))
        chains = []
        tmp = mixed[:, 2:4, :].rearrange("p a (b n) -> p (a b) n", n=S)

        def gate_part(step, g, part):
            f = tmp[:, g, :]
            if part == 0:
                step(nc.vector.tensor_scalar(f, f, 1.0, None, ALU.add))
            if part == 1:
                step(nc.vector.reciprocal(f, f))
            if part == 2:
                step(nc.vector.tensor_scalar(f, f, omlb[:, g:g + 1], lbn[:, g:g + 1], ALU.mult, ALU.add))
                step(nc.vector.tensor_scalar(kT[:, g, :], f, -1.0, 1.0, ALU.mult, ALU.add))
            if part == 3:
                nc.vector.tensor_scalar(f, f, 1.1e-19, None, ALU.max).then_inc(f_ready.sem, 1)

        def summed_logs(dve, g):
            dve.wait_ge(*logs(g + 1))
            return nc.vector.tensor_tensor_scan(bT[:, g, :], scan[:], bT[:, g, :], 0.0, ALU.mult, ALU.add)

        with ExitStack() as inner:
            q_sig = mixed[:, 0:2, :].rearrange("p a (b n) -> p (a b) n", n=S)
            with nc.Block() as block:
                @block.tensor
                def _(pe):
                    for t in range(T):
                        last = nc.tensor.matmul(core.psum[:, t, 0:GW], flip[:], proj[:, T - 1 - t, OFF2[1]:OFF2[2]], start=True, stop=True)
                    last.then_inc(reversed_.sem, 1)

                @block.scalar
                def _(act):
                    for g in range(GROUPS):
                        act.wait_ge(*capped(g + 1))
                        nc.scalar.activation(tmp[:, g, :], kT[:, g, :], ACT.Exp, scale=-1.0).then_inc(exps.sem, 1)
                    nc.scalar.activation(q_sig, qT, ACT.Sigmoid).then_inc(sig.sem, 1)
                    act.wait_ge(*reversed_(1))
                    for t in range(T):
                        nc.scalar.activation(vrev[:, t, :], core.psum[:, t, 0:GW], ACT.Copy)
                    act.wait_ge(*f_ready(1))
                    nc.scalar.activation(bT[:, 0, :], tmp[:, 0, :], ACT.Ln).then_inc(logs.sem, 1)

                @block.vector
                def _(dve):
                    step = core.step("dve_step", dve, chains)
                    for g in range(GROUPS):
                        nc.vector.tensor_scalar(kT[:, g, :], kT[:, g, :], -60.0, None, ALU.max).then_inc(capped.sem, 1)
                    nc.vector.tensor_scalar(lbn[:], lb[:, bass.ds(layer, 1), :].rearrange("p l g -> p (l g)"), 0.0, None, ALU.add)
                    step(nc.vector.memset(scan[:], 1.0))
                    nc.vector.memset(scan[:].rearrange("p (t n) -> p t n", t=T)[:, :, 0:1], 0.0)
                    step(nc.vector.tensor_scalar(omlb[:], lbn[:], -1.0, 1.0, ALU.mult, ALU.add))

                    dve.wait_ge(*exps(1))
                    for part in range(4):
                        gate_part(step, 0, part)
                    dve.wait_ge(*sig(1))
                    nc.vector.tensor_tensor(qT, qT, q_sig, ALU.mult)
                    summed_logs(dve, 0)
                    dve.wait_ge(*exps(GROUPS))
        for s in (capped, exps):
            s.passed(GROUPS)
        reversed_.passed(1); sig.passed(1)
        close(chains)
        names = ("split_diff", "split_exp", "split_factor", "split_scores", "split_taken", "cross_exps", "cross_keys", "cross_turned", "cross_rows",
                 "state_parts", "states", "group_out", "group_taken")
        diff, exped, factor, scored, level_taken, cross_exps, cross_keys, cross_turned, cross_rows, parts, states, out_ready, out_taken = (core.event(n) for n in names)
        o = [sb(f"rec_out{d}", [P, T, GW]) for d in range(2)]
        ex, m = sb("split_exps", [P, 2, S]), sb("split_factors", [P, 2, S])
        acc = [sb(f"split_sums{i}", [P, 2 * T * P]) for i in range(2)]
        qx, kx, kxr = core.junk[:, 0, 0:S], core.junk[:, 0, S:2 * S], sb("cross_k_rows", [P, S])
        eb, st = sb("tile_decay", [P, T]), sb("state", [P, T, P])
        chains = []
        banks = core.psum
        per = LEVELS + 1

        def halves(ap, n):
            v = ap.rearrange("p (b two h) -> p b two h", two=2, h=1 << n)
            return v[:, :, 0, :], v[:, :, 1, :]

        order = [(g, n) for g in range(GROUPS) for n in range(per)]
        step_of = lambda i: (i // LEVELS) * per + i % LEVELS
        with nc.Block() as block:
            @block.vector
            def _(dve):
                step = core.step("dve_step", dve, chains)

                def exponents(i):
                    g, n = i // LEVELS, i % LEVELS
                    if i >= 2:
                        dve.wait_ge(*exped(i - 1))
                        dve.wait_ge(*factor(i - 1))
                    b1, b2 = halves(bT[:, g, :], n)
                    e1, e2 = halves(ex[:, i % 2, :], n)
                    r = b1[:, :, (1 << n) - 1:1 << n].broadcast_to(b1.shape)
                    nc.vector.tensor_tensor(e1, r, b1, ALU.subtract)
                    nc.vector.tensor_tensor(e2, b2, r, ALU.subtract).then_inc(diff.sem, 1)

                def factors(i):
                    g, n = i // LEVELS, i % LEVELS
                    e1, e2 = halves(ex[:, i % 2, :], n)
                    m1, m2 = halves(m[:, i % 2, :], n)
                    dve.wait_ge(*exped(i + 1))
                    if i >= 2:
                        dve.wait_ge(*scored(step_of(i - 2) + 1))
                    nc.vector.tensor_tensor(m1, e1, halves(kT[:, g, :], n)[0], ALU.mult)
                    nc.vector.tensor_tensor(m2, e2, halves(qT[:, g, :], n)[1], ALU.mult).then_inc(factor.sem, 1)

                def take(j):
                    g, n = order[j]
                    if j:
                        dve.wait_ge(*level_taken(j))
                    dve.wait_ge(*scored(j + 1))
                    bank = 2 * (j % 2)
                    nc.vector.copy_predicated(acc[g % 2][:].rearrange("p (a s) -> p a s", s=P), split[:, n, :].unsqueeze(1).broadcast_to([P, 2 * T, P]),
                                              banks[:, bank:bank + 2, :].rearrange("p b (t s) -> p (b t) s", s=P)).then_inc(level_taken.sem, 1)

                def cross_exponents(g):
                    bt = bT[:, g, :].rearrange("p (t s) -> p t s", t=T)
                    if g:
                        dve.wait_ge(*cross_turned(g))
                    step(nc.vector.tensor_tensor(kx[:].rearrange("p (t s) -> p t s", t=T), bt[:, :, P - 1:P].broadcast_to([P, T, P]), bt, ALU.subtract))
                    dve.sem_inc(cross_exps.sem, 1)

                def cross_products(g):
                    dve.wait_ge(*cross_exps(4 * g + 4))
                    nc.vector.tensor_tensor(qx[:], qx[:], qT[:, g, :], ALU.mult).then_inc(cross_keys.sem, 1)
                    nc.vector.tensor_tensor(kx[:], kx[:], kT[:, g, :], ALU.mult).then_inc(cross_keys.sem, 1)

                def carry(g):
                    dve.wait_ge(*parts(g + 1))
                    if g:
                        dve.wait_ge(*out_ready(g))
                    step(nc.vector.tensor_tensor(st[:, 1:T, :], banks[:, 5, 0:(T - 1) * P].rearrange("p (t n) -> p t n", n=P), heads2[:].unsqueeze(1).broadcast_to([P, T - 1, P]), ALU.mult))
                    for t in range(2, T):
                        step(nc.vector.scalar_tensor_tensor(out=st[:, t, :], in0=st[:, t - 1, :], scalar=eb[:, t - 1:t], in1=st[:, t, :], op0=ALU.mult, op1=ALU.add))
                    dve.sem_inc(states.sem, 1)

                exponents(0)
                for j, (g, n) in enumerate(order):
                    i = g * LEVELS + n
                    if n == 6 and g + 1 < GROUPS:
                        step(summed_logs(dve, g + 1))
                    if n < LEVELS and i + 1 < GROUPS * LEVELS:
                        exponents(i + 1)
                    if n == 0:
                        if g >= 2:
                            dve.wait_ge(*out_ready(g - 1))
                        step(nc.vector.memset(acc[g % 2][:], 0.0))
                    if n == 1:
                        cross_exponents(g)
                    if n == 5:
                        cross_products(g)
                    if n < LEVELS:
                        factors(i)
                    if 1 <= n <= 4 and g + 1 < GROUPS:
                        gate_part(step, g + 1, n - 1)
                    if j:
                        take(j - 1)
                    if n == LEVELS:
                        carry(g)
                take(len(order) - 1)

            @block.scalar
            def _(act):
                def out_copy(g):
                    act.wait_ge(*out_ready(g + 1))
                    d, pair = g // 2, g % 2
                    nc.scalar.activation(o[d][:, :, pair * P:(pair + 1) * P], banks[:, 6 + g % 2, :].rearrange("p (t n) -> p t n", t=T), ACT.Copy).then_inc(out_taken.sem, 1)

                for g in range(GROUPS):
                    for n in range(LEVELS):
                        i = g * LEVELS + n
                        act.wait_ge(*diff(i + 1))
                        nc.scalar.activation(ex[:, i % 2, :], ex[:, i % 2, :], ACT.Exp).then_inc(exped.sem, 1)
                        if n == 2:
                            act.wait_ge(*cross_exps(4 * g + 1))
                            nc.scalar.activation(kx[:], kx[:], ACT.Exp).then_inc(cross_exps.sem, 1)
                        if n == 5 and g + 1 < GROUPS:
                            act.wait_ge(*f_ready(g + 2))
                            nc.scalar.activation(bT[:, g + 1, :], tmp[:, g + 1, :], ACT.Ln).then_inc(logs.sem, 1)
                        if n == 3:
                            if g:
                                out_copy(g - 1)
                                act.wait_ge(*states(g))
                            nc.scalar.activation(qx[:], bT[:, g, :], ACT.Exp).then_inc(cross_exps.sem, 1)
                            nc.scalar.activation(eb[:], bT[:, g, :].rearrange("p (t s) -> p t s", t=T)[:, :, P - 1], ACT.Exp).then_inc(cross_exps.sem, 1)
                    act.wait_ge(*cross_turned(g + 1))
                    if g:
                        act.wait_ge(*parts(g))
                    nc.scalar.activation(kxr[:], banks[:, 4, :], ACT.Copy).then_inc(cross_rows.sem, 1)
                out_copy(GROUPS - 1)

            @block.tensor
            def _(pe):
                def v(g, t, a, b):
                    pair = g % 2
                    return vrev[:, t, pair * P + a:pair * P + b] if g // 2 else proj[:, t, OFF2[1] + pair * P + a:OFF2[1] + pair * P + b]

                def scores(j):
                    g, n = order[j]
                    i = g * LEVELS + n
                    if n < LEVELS:
                        pe.wait_ge(*factor(i + 1))
                    if j >= 2:
                        pe.wait_ge(*level_taken(j - 1))
                    for h in range(2):
                        for t in range(T):
                            cols, rows = slice(t * P, (t + 1) * P), slice(h * HD, (h + 1) * HD)
                            a, b = (m[rows, i % 2, cols], m[rows, i % 2, cols]) if n < LEVELS else (kT[rows, g, cols], qT[rows, g, cols])
                            last = nc.tensor.matmul(banks[:, 2 * (j % 2) + h, cols], a, b, start=True, stop=True)
                    last.then_inc(scored.sem, 1)

                def turn_keys(g):
                    pe.wait_ge(*cross_keys(2 * g + 2))
                    if g:
                        pe.wait_ge(*cross_rows(g))
                    for t in range(T):
                        last = nc.tensor.transpose(banks[:, 4, t * P:(t + 1) * P], kx[:, t * P:(t + 1) * P], core.ident[:])
                    last.then_inc(cross_turned.sem, 1)

                def state_parts(g):
                    pe.wait_ge(*cross_rows(g + 1))
                    if g:
                        pe.wait_ge(*states(g))
                    for t in range(T - 1):
                        last = nc.tensor.matmul(banks[:, 5, t * P:(t + 1) * P], kxr[:, t * P:(t + 1) * P], v(g, t, 0, P), start=True, stop=True)
                    last.then_inc(parts.sem, 1)

                def outputs(g):
                    if g >= 2:
                        pe.wait_ge(*out_taken(g - 1))
                    pe.wait_ge(*states(g + 1))
                    pe.wait_ge(*level_taken((g + 1) * per))
                    for t in range(T):
                        out = banks[:, 6 + g % 2, t * P:(t + 1) * P]
                        if t:
                            nc.tensor.matmul(out, qx[:, t * P:(t + 1) * P], st[:, t, :], start=True, stop=False, skip_group_check=True)
                        for h in range(2):
                            last = nc.tensor.matmul(out[:, h * HD:(h + 1) * HD], acc[g % 2][:, (h * T + t) * P:(h * T + t + 1) * P], v(g, t, h * HD, (h + 1) * HD), start=(t == 0), stop=True, skip_group_check=True)
                    last.then_inc(out_ready.sem, 1)

                for j, (g, n) in enumerate(order):
                    scores(j)
                    if n == 1 and g:
                        outputs(g - 1)
                    if n == 5:
                        turn_keys(g)
                    if n == 6:
                        state_parts(g)
                outputs(GROUPS - 1)
        diff.passed(GROUPS * LEVELS); exped.passed(GROUPS * LEVELS); factor.passed(GROUPS * LEVELS)
        scored.passed(GROUPS * per); level_taken.passed(GROUPS * per)
        cross_exps.passed(4 * GROUPS); cross_keys.passed(2 * GROUPS); f_ready.passed(GROUPS); logs.passed(GROUPS)
        for s in (cross_turned, cross_rows, parts, states, out_ready, out_taken):
            s.passed(GROUPS)
        close(chains)
        summed, spread, root, gated = (core.event(n) for n in ("directions", "mean_square", "root", "g_sigmoid"))
        chains = []
        with ExitStack() as inner:
            sq = bT[:, 0:2, :].rearrange("p g s -> p (g s)").rearrange("p (a d) -> p a d", d=HD)
            gs = bT[:, 2:4, :].rearrange("p g s -> p (g s)").rearrange("p (t n) -> p t n", t=T)
            ms = core.junk[:, 0, 0:3 * T * 4].rearrange("p (a n) -> p a n", a=3)
            of = o[0][:].rearrange("p t n -> p (t n)")
            with nc.Block() as block:
                @block.tensor
                def _(pe):
                    for t in range(T):
                        last = nc.tensor.matmul(banks[:, t, 0:GW], flip[:], o[1][:, T - 1 - t, :], start=True, stop=True)
                    last.then_inc(summed.sem, 1)

                @block.scalar
                def _(act):
                    nc.scalar.activation(gs, proj[:, :, OFF2[4]:OFF2[5]], ACT.Sigmoid).then_inc(gated.sem, 1)
                    act.wait_ge(*spread(1))
                    nc.scalar.activation(ms[:, 1, :], ms[:, 0, :], ACT.Sqrt).then_inc(root.sem, 1)

                @block.vector
                def _(dve):
                    step = core.step("dve_step", dve, chains)
                    dve.wait_ge(*gated(1))
                    nc.vector.tensor_tensor(gs, gs, proj[:, :, OFF2[4]:OFF2[5]], ALU.mult)
                    dve.wait_ge(*summed(1))
                    step(nc.vector.tensor_tensor(o[0][:], o[0][:], banks[:, 0:T, 0:GW], ALU.add))
                    step(nc.vector.tensor_tensor(sq.rearrange("p a d -> p (a d)"), of, of, ALU.mult))
                    step(nc.vector.tensor_reduce(ms[:, 0, :], sq, AX.X, ALU.add))
                    nc.vector.tensor_scalar(ms[:, 0, :], ms[:, 0, :], 1.0 / HD, EPS, ALU.mult, ALU.add).then_inc(spread.sem, 1)
                    dve.wait_ge(*root(1))
                    step(nc.vector.reciprocal(ms[:, 2, :], ms[:, 1, :]))
                    step(nc.vector.tensor_tensor(sq, of.rearrange("p (a d) -> p a d", d=HD), ms[:, 2, :].unsqueeze(2).broadcast_to([P, T * 4, HD]), ALU.mult))
                    nc.vector.tensor_tensor(mixed[:, :, 0:GW], sq.rearrange("p (t h) d -> p t (h d)", t=T), gs, ALU.mult)
        for s in (summed, spread, root, gated):
            s.passed(1)
        close(chains)


def fourier_stages(core, proj, mixed, hT, tables, tables_in, cos2, sin2):
    nc = core.nc
    uT = hT[:, 0:2, :]
    channels, taken, out_ready = core.event("dft_channels"), core.event("dft_taken"), core.event("dft_out")
    cos, sin, ch = tables
    chains = []
    with ExitStack() as ctx:
        ab, tmp = core.sb("dft_ab", [P, T, 2, 2, P], ctx=ctx), core.sb("rotate_tmp2", [P, 4, 2 * H2, HD // 2], ctx=ctx)
        turn_stage(core, [(uT[:, c, :], [proj[:, t, OFF2[5] + c * P:OFF2[5] + (c + 1) * P] for t in range(T)], core.ident) for c in range(2)])
        with nc.Block() as block:
            @block.tensor
            def _(pe):
                pe.wait_ge(*tables_in(16 * TABLES))
                for t in range(T):
                    for c in range(2):
                        last = nc.tensor.matmul(core.psum[:, t, c * 2 * P:(c + 1) * 2 * P], uT[:, c, t * P:(t + 1) * P], ch[:], start=True, stop=True)
                    last.then_inc(channels.sem, 1)
                pe.wait_ge(*taken(T))
                for t in range(T):
                    for s in range(T):
                        for i, table in enumerate((cos, sin)):
                            last = nc.tensor.matmul(core.psum[:, 4 + t, 0:2 * P], table[:, s, t * P:(t + 1) * P], ab[:, s, :, i, :], start=(s == 0 and i == 0), stop=(s == T - 1 and i == 1))
                    last.then_inc(out_ready.sem, 1)

            @block.scalar
            def _(act):
                for t in range(T):
                    act.wait_ge(*channels(t + 1))
                    nc.scalar.activation(ab[:, t].rearrange("p c i n -> p (c i n)"), core.psum[:, t, :], ACT.Copy).then_inc(taken.sem, 1)

            @block.vector
            def _(dve):
                step = core.step("dve_step", dve, chains)
                for t in range(T):
                    qk = proj[:, t, OFF2[6]:OFF2[8]].rearrange("p (h d) -> p h d", d=HD)
                    rotate(nc, step, qk, qk, cos2[:, t, :], sin2[:, t, :], tmp, 2 * H2, HD // 2)
                for t in range(T):
                    dve.wait_ge(*out_ready(t + 1))
                    nc.vector.tensor_copy(mixed[:, t, GW:2 * GW], core.psum[:, 4 + t, 0:2 * P])
    close(chains)
    tables_in.passed(16 * TABLES)
    channels.passed(T); taken.passed(T); out_ready.passed(T)


def dilated_stages(core, proj, mixed, hT, pairs):
    qT, kT = hT[:, 0:4, :], hT[:, 4:8, :]
    qo, ko, vo = OFF2[6], OFF2[7], OFF2[8]
    turn_stage(core, [(to[:, c, :], [proj[:, t, off + c * P:off + (c + 1) * P] for t in range(T)], core.ident) for off, to in ((qo, qT), (ko, kT)) for c in range(4)])
    units = []
    for t in range(T):
        for h in range(H2):
            half = (h % 2) * HD
            units.append((qT[half:half + HD, h // 2, t * P:(t + 1) * P], kT[half:half + HD, h // 2, :], pairs[:, t, :],
                          lambda j, h=h: proj[:, j, vo + h * HD:vo + (h + 1) * HD], mixed[:, t, 2 * GW + h * HD:2 * GW + (h + 1) * HD], S))
    attention_stage(core, units, HD ** -0.5, warm=True)


def ffn_sources(w_up, w_down):
    sources = []
    for g in range(FFN_GROUPS + 1):
        if g < FFN_GROUPS:
            sources += pieces_of(w_up, 0, g * BANK)
        if g:
            rows = (g - 1) * BANK
            sources += [w_down[rows + k * P:rows + (k + 1) * P, :].rearrange("(k p) n -> p k n", p=P) for k in range(PIECES)]
    return sources


def ffn_stage(core, pieces, hT, x):
    nc = core.nc
    up, relus, u_ready, u_high, u_low = core.event("up_product"), core.event("relus"), core.event("u_ready"), core.event("u_high"), core.event("u_low")
    down, added = core.event("down_product"), core.event("down_added")
    first = pieces.begun
    steps = []
    for g in range(FFN_GROUPS + 1):
        steps += [("up", g)] * (g < FFN_GROUPS) + [("down", g - 1)] * (g > 0)
    outs = 2 * T
    with ExitStack() as ctx:
        u, relu = core.sb("u", [P, 2, S], ctx=ctx), core.sb("relu", [P, 2, S], ctx=ctx)
        uh, ul = (core.sb(n, [P, 2, 4, S], F32R, ctx=ctx) for n in ("u_high", "u_low"))
        pieces.stage(ctx)
        with nc.Block() as block:
            @block.sync
            def _(sp):
                pieces.load_ahead(sp, len(steps) * PIECES)

            @block.tensor
            def _(pe):
                for s, (kind, g) in enumerate(steps):
                    p0 = first + s * PIECES
                    if kind == "up":
                        for f in range(4):
                            i = 4 * g + f
                            if i >= 4:
                                pe.wait_ge(*relus(i - 3))
                            for k in range(KD):
                                if f == 0 and k % 2 == 0:
                                    pieces.arrived(pe, p0 + k // 2)
                                w = [part[:, k % 2, f * P:(f + 1) * P] for part in pieces.parts(p0 + k // 2)]
                                last = product_in_parts(nc, core.psum[:, f, :], w, [part[:, k, :] for part in hT], k == 0, k == KD - 1)
                                if f == 3 and k % 2:
                                    last.then_inc(pieces.used.sem, 1)
                            if f < 3:
                                last.then_inc(up.sem, 1)
                    else:
                        for o in range(outs):
                            i = outs * g + o
                            t, half = o // 2, slice((o % 2) * BANK, (o % 2 + 1) * BANK)
                            if i >= 4:
                                pe.wait_ge(*added(i - 3))
                            for k in range(4):
                                if o == 0:
                                    pieces.arrived(pe, p0 + k)
                                    pe.wait_ge(*u_low(4 * g + k + 1))
                                w = [part[:, 0, half] for part in pieces.parts(p0 + k)]
                                tokens = [part[:, g % 2, k, t * P:(t + 1) * P] for part in (uh, ul)]
                                last = product_in_parts(nc, core.psum[:, 4 + o % 4, :], tokens, w, k == 0, k == 3)
                                if o == outs - 1:
                                    last.then_inc(pieces.used.sem, 1)
                            if o < outs - 1:
                                last.then_inc(down.sem, 1)

            @block.scalar
            def _(act):
                for q in range(PIECES):
                    pieces.split_high(act, first + q)
                for s, (kind, g) in enumerate(steps):
                    for f in range(4):
                        if s + 1 < len(steps):
                            pieces.split_high(act, first + (s + 1) * PIECES + f)
                        if kind == "up":
                            i = 4 * g + f
                            act.wait_ge(*(up(3 * g + f + 1) if f < 3 else pieces.used(first + (s + 1) * PIECES)))
                            if i >= 2:
                                act.wait_ge(*u_ready(i - 1))
                            nc.scalar.activation(relu[:, i % 2, :], core.psum[:, f, :], ACT.Relu).then_inc(relus.sem, 1)
                            act.wait_ge(*u_ready(i + 1))
                            if g >= 2:
                                act.wait_ge(*pieces.used(first + (steps.index(("down", g - 2)) + 1) * PIECES))
                            nc.scalar.activation(uh[:, g % 2, f, :], u[:, i % 2, :], ACT.Copy).then_inc(u_high.sem, 1)

            @block.vector
            def _(dve):
                for q in range(PIECES):
                    pieces.split_low(dve, first + q)
                for s, (kind, g) in enumerate(steps):
                    for f in range(4):
                        if s + 1 < len(steps):
                            pieces.split_low(dve, first + (s + 1) * PIECES + f)
                        if kind == "up":
                            i = 4 * g + f
                            dve.wait_ge(*relus(i + 1))
                            if i >= 2:
                                dve.wait_ge(*u_low(i - 1))
                            nc.vector.tensor_tensor(u[:, i % 2, :], relu[:, i % 2, :], relu[:, i % 2, :], ALU.mult).then_inc(u_ready.sem, 1)
                            dve.wait_ge(*u_high(i + 1))
                            if g >= 2:
                                dve.wait_ge(*pieces.used(first + (steps.index(("down", g - 2)) + 1) * PIECES))
                            nc.vector.tensor_tensor(ul[:, g % 2, f, :], u[:, i % 2, :], uh[:, g % 2, f, :], ALU.subtract).then_inc(u_low.sem, 1)
                        else:
                            for o in (2 * f, 2 * f + 1):
                                t, half = o // 2, slice((o % 2) * BANK, (o % 2 + 1) * BANK)
                                dve.wait_ge(*(down((outs - 1) * g + o + 1) if o < outs - 1 else pieces.used(first + (s + 1) * PIECES)))
                                if g:
                                    dve.wait_ge(*added(outs * (g - 1) + o + 1))
                                nc.vector.tensor_tensor(x[:, t, half], x[:, t, half], core.psum[:, 4 + o % 4, :], ALU.add).then_inc(added.sem, 1)
    pieces.begun += len(steps) * PIECES
    up.passed(3 * FFN_GROUPS); down.passed((outs - 1) * FFN_GROUPS); added.passed(outs * FFN_GROUPS)
    for e in (relus, u_ready, u_high, u_low):
        e.passed(4 * FFN_GROUPS)


def second_block(core, W, x, raw, out):
    nc = core.nc
    half = HD // 2
    with ExitStack() as ctx:
        sb = lambda name, shape, dtype=F32: core.sb(name, shape, dtype, ctx=ctx)
        gains = sb("gains2", [P, 2, D])
        cos, sin, lb = sb("cos2", [P, T, half]), sb("sin2", [P, T, half]), sb("lower_bounds", [P, L2, GROUPS])
        with ExitStack() as inner:
            posi, posf = core.sb("pos_i2", [P, T], I32, ctx=inner), core.sb("pos_f2", [P, T], ctx=inner)
            freq, tmp, bounds = core.sb("freq2", [P, half], ctx=inner), core.sb("angle_tmp2", [P, 3, T, half], ctx=inner), core.sb("lb_raw", [P, L2, GROUPS], ctx=inner)
            load_stage(core, [(posi[:], W["pos2_cols"]), (freq[:], W["freq2"]), (bounds[:], W["lb_cols"])], "second_loads")
            angle_stage(core, posi, posf, freq[:], half, cos, sin, [tmp[:, i] for i in range(3)])
            lower_bounds_stage(core, bounds, lb)
        clear_stage(core, [s for n, s in core.events.items() if s.base and n not in POOL_SIGNALS])
        with nc.Fori(0, L2) as layer:
            w_in, w_out, w_up, w_down = (W[n][layer] for n in ("w_in_2", "w_out_2", "w_up_2", "w_down_2"))
            sources = []
            for n in range(IN2 // BANK):
                sources += pieces_of(w_in, 0, n * BANK)
            for n in range(2):
                sources += pieces_of(w_out, 0, n * BANK)
            pieces = Pieces(core, raw, sources + ffn_sources(w_up, w_down))
            load_stage(core, [(gains[:, 0, :], W["attn_norm_w_2"][layer].partition_broadcast(P)), (gains[:, 1, :], W["mlp_norm_w_2"][layer].partition_broadcast(P))], "layer_gains")

            def in_parts(inner):
                return tuple(core.sb(n, [P, KD, S], F32R, ctx=inner) for n in ("hT_high", "hT_low"))

            def normed(gain, hT):
                with ExitStack() as inner:
                    norm_stage(core, x, gain, None, core.sb("h2", [P, T, D], ctx=inner), hT)

            def add(n, t, bank):
                cols = slice(n * BANK, (n + 1) * BANK)
                return nc.vector.tensor_tensor(x[:, t, cols], x[:, t, cols], bank, ALU.add)

            with ExitStack() as outer:
                mixed = core.sb("mixed", [P, T, D], ctx=outer)
                with ExitStack() as inner:
                    proj = core.sb("proj2", [P, T, IN2], ctx=inner)
                    with ExitStack() as parts:
                        hT = in_parts(parts)
                        norm_stage(core, x, gains[:, 0, :], None, mixed, hT)
                        product_parts_stage(core, pieces, hT, [BANK] * (IN2 // BANK), lambda n, t, bank: nc.vector.tensor_copy(proj[:, t, n * BANK:(n + 1) * BANK], bank))
                    hT = core.sb("hT2", [P, KD, S], ctx=inner)
                    big = lambda name: core.sb(name, [P, T, S], ctx=inner)
                    dft_cos, dft_sin, pairs, dft_ch = big("dft_cos"), big("dft_sin"), big("pairs"), core.sb("dft_ch", [P, 2 * P], ctx=inner)
                    tables_in = core.event("tables_in")

                    def load_tables(sp):
                        for to, table in ((dft_cos, "dft_cos"), (dft_sin, "dft_sin"), (pairs, "pairs")):
                            sp.dma_start(to[:], W[table].rearrange("p (t n) -> p t n", t=T)).then_inc(tables_in.sem, 16)
                        sp.dma_start(dft_ch[:], W["dft_ch"]).then_inc(tables_in.sem, 16)

                    recurrence_stages(core, W, proj, mixed, hT, lb, layer, load_tables)
                    fourier_stages(core, proj, mixed, hT, (dft_cos, dft_sin, dft_ch), tables_in, cos, sin)
                    dilated_stages(core, proj, mixed, hT, pairs)
                hT = in_parts(outer)
                transpose_stage(core, mixed, hT)
                product_parts_stage(core, pieces, hT, [BANK] * 2, add)
            with ExitStack() as inner:
                hT = in_parts(inner)
                normed(gains[:, 1, :], hT)
                ffn_stage(core, pieces, hT, x)
            pieces.close()
            clear_stage(core, [s for s in core.events.values() if s.base])
        load_stage(core, [(gains[:, 0, :], W["final_norm_w_2"].partition_broadcast(P))], "final_gain")
        norm_stage(core, x, gains[:, 0, :], None, sb("normed", [P, T, D]), None, out)


def two_blocks_kernel(nc, W, out):
    with ExitStack() as ctx:
        core, x = setup(nc, W, out, ctx)
        with ExitStack() as first:
            core.scope = first
            ring, gate = core.sb("pieces1", [P, E_RAW, PIECE], ctx=first), core.sb("ffn_gate", [P, D], ctx=first)
            moe = Moe(core, first, ring)
            with ExitStack() as inner:
                mod = core.sb("mod", [P, 5 * D], ctx=inner)
                first_mixer(core, W, x, mod, gate, ring)
                first_ffn(core, W, x, moe, mod, gate)
            experts_part(core, W, x, moe, gate[:])
            clear_stage(core, [s for n, s in core.events.items() if s.base and n not in POOL_SIGNALS])
        core.events = {n: s for n, s in core.events.items() if n in POOL_SIGNALS}
        core.scope = None
        second_block(core, W, x, core.sb("pieces2", [P, RAW, PIECE]), out)


_AS_THEY_ARE = ["x", "positions", "b_ada", "w_ada", "g_pre_mix", "g_post_mix", "g_pre_ffn", "g_post_ffn", "w_in", "g_q_a", "g_kv_a",
                "w_q_b", "w_kv_b", "w_o", "w_router", "b_router", "w_mlp1", "b_mlp1", "w_mlp2", "b_mlp2", "attn_norm_w_2", "w_in_2",
                "w_out_2", "mlp_norm_w_2", "w_up_2", "w_down_2", "final_norm_w_2"]


def kernel(**inputs):
    import concourse.bacc as _bacc
    from concourse.bass_utils import run_bass_kernel_spmd as _run

    def columns(a):
        return np.ascontiguousarray(np.asarray(a).reshape(-1, P).T)

    arrays = {n: np.ascontiguousarray(inputs[n]) for n in _AS_THEY_ARE}
    arrays["c_cols"] = columns(inputs["c"])
    arrays["pos_cols"] = columns(inputs["positions"])
    arrays["pos2_cols"] = columns(inputs["positions_2"])
    arrays["lb_cols"] = columns(inputs["hgrn_lower_bounds_2"]).reshape(P, L2, GROUPS)
    arrays.update(shape_constants())
    nc = _bacc.Bacc("TRN2", target_bir_lowering=False, num_devices=1)
    W = {n: nc.dram_tensor(f"in_{n}", a.shape, mybir.dt.from_np(a.dtype), kind="ExternalInput").ap() for n, a in arrays.items()}
    out = nc.dram_tensor("out", (S, D), F32, kind="ExternalOutput").ap()
    two_blocks_kernel(nc, W, out)
    r = _run(nc, [{f"in_{n}": a for n, a in arrays.items()}], core_ids=[0])
    return r.results[0]["out"].reshape(1, S, D)
```
